# Optimizing a Trainium2 kernel written in Bass

```python
import jax
import jax.numpy as jnp
from jax import lax
import numpy as np

D_MODEL = 1024
BATCH = 1
SEQ = 256
DEPTH = 2

GRID_W = 64
CTX_LEN = 256
MIX_WIDTH = D_MODEL
MLSTM_WIDTH = MIX_WIDTH // 4
MLSTM_DH = 64
MLSTM_HEADS = MLSTM_WIDTH // MLSTM_DH
MLSTM_GATE_COLS = 2 * 2 * MLSTM_HEADS
HEAD_DIM = 64
ATTN_Q_WIDTH = MIX_WIDTH // 2
ATTN_HEADS = ATTN_Q_WIDTH // HEAD_DIM
ATTN_KV_HEADS = 2
ATTN_GROUP = ATTN_HEADS // ATTN_KV_HEADS
ATTN_KV_WIDTH = ATTN_KV_HEADS * HEAD_DIM
WINDOW = 128
WIN_BLOCK = 128
ROPE_BASE = 10000.0
ROPE_PAIRS = HEAD_DIM // 4
GLA_WIDTH = MIX_WIDTH // 4
GLA_DV = 64
GLA_HEADS = GLA_WIDTH // GLA_DV
GLA_DK = GLA_DV // 2
GLA_KEY_WIDTH = GLA_HEADS * GLA_DK
GLA_RANK = 16
GLA_TAU = 16.0
GLA_GATE_COLS = 2 * GLA_RANK
SCAN_CHUNK = 64
COL_SIZES = (MLSTM_WIDTH, MLSTM_WIDTH, MLSTM_WIDTH, MLSTM_WIDTH, MLSTM_GATE_COLS,
             ATTN_Q_WIDTH, ATTN_KV_WIDTH, ATTN_KV_WIDTH,
             GLA_KEY_WIDTH, GLA_KEY_WIDTH, GLA_WIDTH, GLA_WIDTH, GLA_GATE_COLS)
COL_OFFSETS = tuple(int(o) for o in np.cumsum(COL_SIZES)[:-1])
IN_COLS = sum(COL_SIZES)
D_FF = 2816
N_EXPERTS = 8
TOP_K = 2
D_EXPERT = 3584
MOE_BLOCK = 128
N_DENSE = (DEPTH + 1) // 2
N_MOE = DEPTH // 2
DEEPNORM_ALPHA = (2 * DEPTH) ** 0.25
DEEPNORM_BETA = (8 * DEPTH) ** -0.25
ADA_INIT = 0.5
LN_EPS = 1e-5

kernel_name = 'hymba_mlstm_swa_gla_moe_dit'

def layer_norm(x, w, b):
    xf = x.astype(jnp.float32)
    mu = jnp.mean(xf, -1, keepdims=True)
    var = jnp.mean(jnp.square(xf - mu), -1, keepdims=True)
    return ((xf - mu) * lax.rsqrt(var + LN_EPS) * w + b).astype(x.dtype)

def head_norm(h, w, n_heads):
    hh = h.reshape(h.shape[:-1] + (n_heads, -1))
    mu = jnp.mean(hh, -1, keepdims=True)
    var = jnp.mean(jnp.square(hh - mu), -1, keepdims=True)
    return ((hh - mu) * lax.rsqrt(var + LN_EPS)).reshape(h.shape) * w

def to_heads(a, n):
    b, t, w = a.shape
    return a.reshape(b, t, n, w // n).transpose(0, 2, 1, 3)

def from_heads(a):
    b, n, t, d = a.shape
    return a.transpose(0, 2, 1, 3).reshape(b, t, n * d)

def axial_rope(x, row, col):
    inv = ROPE_BASE ** (-jnp.arange(ROPE_PAIRS, dtype=jnp.float32) / ROPE_PAIRS)

    def rot(xa, pos):
        ang = pos.astype(jnp.float32)[:, None] * inv
        cos, sin = jnp.cos(ang).astype(x.dtype), jnp.sin(ang).astype(x.dtype)
        x1, x2 = xa[..., :ROPE_PAIRS], xa[..., ROPE_PAIRS:]
        return jnp.concatenate([x1 * cos - x2 * sin, x2 * cos + x1 * sin], -1)

    half = HEAD_DIM // 2
    return jnp.concatenate([rot(x[..., :half], row), rot(x[..., half:], col)], -1)

def _chunks(a):
    nc = a.shape[2] // SCAN_CHUNK
    return jnp.moveaxis(a.reshape(a.shape[:2] + (nc, SCAN_CHUNK) + a.shape[3:]), 2, 0)

def _unchunk(hs):
    nc, b, h, l, d = hs.shape
    return jnp.moveaxis(hs, 0, 2).reshape(b, h, nc * l, d)

def mlstm_scan(state, q, k, v, ig, lf):
    tri = jnp.tril(jnp.ones((SCAN_CHUNK, SCAN_CHUNK), bool))

    def step(carry, inp):
        cmat, nvec, m = carry
        qc, kc, vc, ic, fc = inp
        b = jnp.cumsum(fc, axis=-1)
        log_d = jnp.where(tri, b[..., :, None] - b[..., None, :] + ic[..., None, :], -jnp.inf)
        log_inter = b + m[..., None]
        m_t = jnp.maximum(log_inter, jnp.max(log_d, axis=-1))
        d = jnp.exp(log_d - m_t[..., None])
        w_inter = jnp.exp(log_inter - m_t)
        s = jnp.einsum('bhtd,bhsd->bhts', qc, kc) * d
        num = jnp.einsum('bhts,bhsv->bhtv', s, vc) + w_inter[..., None] * jnp.einsum('bhtd,bhdv->bhtv', qc, cmat)
        den = jnp.sum(s, -1) + w_inter * jnp.einsum('bhtd,bhd->bht', qc, nvec)
        h = num / jnp.maximum(jnp.abs(den), jnp.exp(-m_t))[..., None]
        m_new = m_t[..., -1]
        w_state = jnp.exp(b[..., -1:] - b + ic - m_new[..., None])
        decay = jnp.exp(b[..., -1] + m - m_new)
        cmat = decay[..., None, None] * cmat + jnp.einsum('bhs,bhsd,bhsv->bhdv', w_state, kc, vc)
        nvec = decay[..., None] * nvec + jnp.einsum('bhs,bhsd->bhd', w_state, kc)
        return (cmat, nvec, m_new), h

    state, hs = lax.scan(step, state, tuple(_chunks(a) for a in (q, k, v, ig, lf)))
    return _unchunk(hs), state

def gla_scan(state, q, k, v, lg):
    tri = jnp.tril(jnp.ones((SCAN_CHUNK, SCAN_CHUNK), bool))

    def step(smat, inp):
        qc, kc, vc, gc = inp
        b = jnp.cumsum(gc, axis=2)
        q_t = qc * jnp.exp(b)
        k_t = kc * jnp.exp(-b)
        a = jnp.where(tri, jnp.einsum('bhtd,bhsd->bhts', q_t, k_t), 0.0)
        o = jnp.einsum('bhts,bhsv->bhtv', a, vc) + jnp.einsum('bhtd,bhdv->bhtv', q_t, smat)
        b_last = b[:, :, -1:, :]
        smat = jnp.exp(b_last[:, :, 0])[..., None] * smat + jnp.einsum('bhsd,bhsv->bhdv', kc * jnp.exp(b_last - b), vc)
        return smat, o

    state, os_ = lax.scan(step, state, tuple(_chunks(a) for a in (q, k, v, lg)))
    return _unchunk(os_), state

def bidirectional(scan, init, ctx_fwd, ctx_bwd, lat_fwd, lat_bwd):
    flip = lambda ts: tuple(jnp.flip(t, axis=2) for t in ts)
    c_f, s_f = scan(init, *ctx_fwd)
    l_f, _ = scan(s_f, *lat_fwd)
    c_b, s_b = scan(init, *flip(ctx_bwd))
    l_b, _ = scan(s_b, *flip(lat_bwd))
    return c_f + jnp.flip(c_b, 2), l_f + jnp.flip(l_b, 2)

def window_attention(q, k, v, kc, vc, sink):
    b_, _, s_, hd = q.shape
    nb = s_ // WIN_BLOCK
    qg = (q * hd ** -0.5).reshape(b_, ATTN_KV_HEADS, ATTN_GROUP, nb, WIN_BLOCK, hd)

    def band(a):
        ap = jnp.pad(a, ((0, 0), (0, 0), (WIN_BLOCK, WIN_BLOCK), (0, 0))).reshape(b_, ATTN_KV_HEADS, nb + 2, WIN_BLOCK, hd)
        return jnp.concatenate([ap[:, :, :-2], ap[:, :, 1:-1], ap[:, :, 2:]], axis=3)

    kb, vb = band(k), band(v)
    qpos = jnp.arange(nb)[:, None, None] * WIN_BLOCK + jnp.arange(WIN_BLOCK)[None, :, None]
    kpos = jnp.arange(nb)[:, None, None] * WIN_BLOCK - WIN_BLOCK + jnp.arange(3 * WIN_BLOCK)[None, None, :]
    valid = (jnp.abs(kpos - qpos) <= WINDOW) & (kpos >= 0) & (kpos < s_)
    s_loc = jnp.where(valid, jnp.einsum('bkgnqd,bknjd->bkgnqj', qg, kb).astype(jnp.float32), -jnp.inf)
    s_ctx = jnp.einsum('bkgnqd,bkcd->bkgnqc', qg, kc).astype(jnp.float32)
    s_sink = jnp.broadcast_to(sink.astype(jnp.float32).reshape(ATTN_KV_HEADS, ATTN_GROUP, 1, 1, 1), s_ctx.shape[:-1] + (1,))
    p = jax.nn.softmax(jnp.concatenate([s_loc, s_ctx, s_sink], -1), axis=-1).astype(v.dtype)
    n_loc, n_ctx = 3 * WIN_BLOCK, kc.shape[2]
    out = (jnp.einsum('bkgnqj,bknjd->bkgnqd', p[..., :n_loc], vb)
           + jnp.einsum('bkgnqc,bkcd->bkgnqd', p[..., n_loc:n_loc + n_ctx], vc))
    return out.reshape(b_, ATTN_HEADS, s_, hd)

def context_attention(qc, kc, vc, sink):
    b_, _, n_ctx, hd = qc.shape
    qg = (qc * hd ** -0.5).reshape(b_, ATTN_KV_HEADS, ATTN_GROUP, n_ctx, hd)
    s = jnp.einsum('bkgqd,bkcd->bkgqc', qg, kc).astype(jnp.float32)
    s_sink = jnp.broadcast_to(sink.astype(jnp.float32).reshape(ATTN_KV_HEADS, ATTN_GROUP, 1, 1), s.shape[:-1] + (1,))
    p = jax.nn.softmax(jnp.concatenate([s, s_sink], -1), axis=-1).astype(vc.dtype)
    out = jnp.einsum('bkgqc,bkcd->bkgqd', p[..., :n_ctx], vc)
    return out.reshape(b_, ATTN_HEADS, n_ctx, hd)

def mixer(h, hc, w_in, gate_b, mnorm_w, sink, g_up, g_b, gnorm_w, w_out, row, col, with_ctx_out):
    f32 = jnp.float32
    pl = jnp.split(h @ w_in, COL_OFFSETS, axis=-1)
    pc = jnp.split(hc @ w_in, COL_OFFSETS, axis=-1)
    b_ = h.shape[0]

    def mlstm_in(p):
        t_ = p[0].shape[1]
        q = to_heads(p[0], MLSTM_HEADS).astype(f32)
        k = to_heads(p[1], MLSTM_HEADS).astype(f32) * MLSTM_DH ** -0.5
        v = to_heads(p[2], MLSTM_HEADS).astype(f32)
        g = p[4].astype(f32).reshape(b_, t_, 2, 2, MLSTM_HEADS) + gate_b.astype(f32)
        g = jnp.transpose(g, (2, 3, 0, 4, 1))
        ig, lf = g[:, 0], jax.nn.log_sigmoid(g[:, 1])
        return [(q, k, v, ig[d], lf[d]) for d in range(2)]

    mc, ml = mlstm_in(pc), mlstm_in(pl)
    m_init = (jnp.zeros((b_, MLSTM_HEADS, MLSTM_DH, MLSTM_DH), f32),
              jnp.zeros((b_, MLSTM_HEADS, MLSTM_DH), f32),
              jnp.zeros((b_, MLSTM_HEADS), f32))
    m_ctx, m_lat = bidirectional(mlstm_scan, m_init, mc[0], mc[1], ml[0], ml[1])
    mlstm_out = lambda hs, p: (head_norm(from_heads(hs), mnorm_w, MLSTM_HEADS) * jax.nn.sigmoid(p[3].astype(f32))).astype(h.dtype)

    ql = axial_rope(to_heads(pl[5], ATTN_HEADS), row, col)
    kl = axial_rope(to_heads(pl[6], ATTN_KV_HEADS), row, col)
    vl = to_heads(pl[7], ATTN_KV_HEADS)
    kc, vc = to_heads(pc[6], ATTN_KV_HEADS), to_heads(pc[7], ATTN_KV_HEADS)
    a_lat = from_heads(window_attention(ql, kl, vl, kc, vc, sink))

    def gla_in(p):
        t_ = p[8].shape[1]
        q = to_heads(p[8], GLA_HEADS).astype(f32) * GLA_DK ** -0.5
        k = to_heads(p[9], GLA_HEADS).astype(f32)
        v = to_heads(p[10], GLA_HEADS).astype(f32)
        z = jnp.einsum('btzr,zrk->zbtk', p[12].astype(f32).reshape(b_, t_, 2, GLA_RANK), g_up.astype(f32)) + g_b.astype(f32)[:, None, None, :]
        lg = jax.nn.log_sigmoid(z) / GLA_TAU
        lg = jnp.transpose(lg.reshape(2, b_, t_, GLA_HEADS, GLA_DK), (0, 1, 3, 2, 4))
        return [(q, k, v, lg[d]) for d in range(2)]

    gc, gl = gla_in(pc), gla_in(pl)
    g_init = jnp.zeros((b_, GLA_HEADS, GLA_DK, GLA_DV), f32)
    g_ctx, g_lat = bidirectional(gla_scan, g_init, gc[0], gc[1], gl[0], gl[1])
    gla_out = lambda o, p: (head_norm(from_heads(o), gnorm_w, GLA_HEADS) * jax.nn.silu(p[11].astype(f32))).astype(h.dtype)

    lat = jnp.concatenate([mlstm_out(m_lat, pl), a_lat, gla_out(g_lat, pl)], -1) @ w_out
    if not with_ctx_out:
        return lat, None
    a_ctx = from_heads(context_attention(to_heads(pc[5], ATTN_HEADS), kc, vc, sink))
    ctx_o = jnp.concatenate([mlstm_out(m_ctx, pc), a_ctx, gla_out(g_ctx, pc)], -1) @ w_out
    return lat, ctx_o

def swiglu(h, w_gu, w_down):
    g, u = jnp.split(h @ w_gu, 2, axis=-1)
    return (jax.nn.silu(g) * u) @ w_down

def moe_swiglu(h, w_router, b_router, w_gu, w_down):
    n, d = h.shape
    logits = jnp.dot(h, w_router).astype(jnp.float32) + b_router.astype(jnp.float32)
    top_logits, top_e = lax.top_k(logits, TOP_K)
    top_w = jax.nn.softmax(top_logits, axis=-1)
    n_assign = n * TOP_K
    e_flat = top_e.reshape(-1)
    tok_flat = jnp.repeat(jnp.arange(n, dtype=jnp.int32), TOP_K)
    w_flat = top_w.reshape(-1)
    order = jnp.argsort(e_flat)
    e_sorted = e_flat[order]
    counts = jnp.bincount(e_flat, length=N_EXPERTS)
    padded = (counts + MOE_BLOCK - 1) // MOE_BLOCK * MOE_BLOCK
    start = jnp.cumsum(counts) - counts
    pend = jnp.cumsum(padded)
    pstart = pend - padded
    slot = pstart[e_sorted] + jnp.arange(n_assign) - start[e_sorted]
    n_blocks = -(-n_assign // MOE_BLOCK) + N_EXPERTS
    slot_tok = jnp.full((n_blocks * MOE_BLOCK,), n, jnp.int32).at[slot].set(tok_flat[order])
    slot_w = jnp.zeros((n_blocks * MOE_BLOCK,), jnp.float32).at[slot].set(w_flat[order])
    block_e = jnp.minimum(jnp.searchsorted(pend, jnp.arange(n_blocks) * MOE_BLOCK, side='right'), N_EXPERTS - 1)
    h_pad = jnp.concatenate([h, jnp.zeros((1, d), h.dtype)], 0)
    xb = h_pad[slot_tok].reshape(n_blocks, MOE_BLOCK, d)

    def expert_block(args):
        xblk, e = args
        g, u = jnp.split(xblk @ w_gu[e], 2, axis=-1)
        return (jax.nn.silu(g) * u) @ w_down[e]

    yb = lax.map(expert_block, (xb, block_e))
    y = jnp.zeros((n + 1, d), jnp.float32).at[slot_tok].add(yb.reshape(-1, d).astype(jnp.float32) * slot_w[:, None])
    return y[:n].astype(h.dtype)

def setup_inputs(seed: int = 0) -> dict:
    key = jax.random.key(seed)
    ks = jax.random.split(key, 24)
    nrm = lambda k, shape, s=1.0: jax.random.normal(k, shape, jnp.float32) * s
    D = D_MODEL
    gate_base = jnp.stack([jnp.zeros((MLSTM_HEADS,), jnp.float32), jnp.linspace(3.0, 6.0, MLSTM_HEADS)])
    return {
        'x': nrm(ks[0], (BATCH, SEQ, D)),
        'c': nrm(ks[1], (BATCH, D)),
        'ctx': nrm(ks[2], (BATCH, CTX_LEN, D)),
        'c_ctx': nrm(ks[3], (D,)),
        'w_ada': nrm(ks[4], (DEPTH, D, 6 * D), ADA_INIT * D ** -0.5),
        'b_ada': nrm(ks[5], (DEPTH, 6 * D), 0.02),
        'w_in': nrm(ks[6], (DEPTH, D, IN_COLS), D ** -0.5),
        'mlstm_gate_b': gate_base[None, None] + nrm(ks[7], (DEPTH, 2, 2, MLSTM_HEADS), 0.1),
        'mlstm_norm_w': 1.0 + nrm(ks[8], (DEPTH, MLSTM_WIDTH), 0.02),
        'attn_sink': nrm(ks[9], (DEPTH, ATTN_HEADS), 0.5),
        'gla_gate_up': nrm(ks[10], (DEPTH, 2, GLA_RANK, GLA_KEY_WIDTH), GLA_RANK ** -0.5),
        'gla_gate_b': nrm(ks[11], (DEPTH, 2, GLA_KEY_WIDTH), 0.1),
        'gla_norm_w': 1.0 + nrm(ks[12], (DEPTH, GLA_WIDTH), 0.02),
        'w_out': nrm(ks[13], (DEPTH, MIX_WIDTH, D), DEEPNORM_BETA * MIX_WIDTH ** -0.5),
        'ln_w': 1.0 + nrm(ks[14], (DEPTH, 2, D), 0.02),
        'ln_b': nrm(ks[15], (DEPTH, 2, D), 0.02),
        'ffn_w_gu': nrm(ks[16], (N_DENSE, D, 2 * D_FF), D ** -0.5),
        'ffn_w_down': nrm(ks[17], (N_DENSE, D_FF, D), DEEPNORM_BETA * D_FF ** -0.5),
        'router_w': nrm(ks[18], (N_MOE, D, N_EXPERTS), D ** -0.5),
        'router_b': nrm(ks[19], (N_MOE, N_EXPERTS), 0.01),
        'moe_w_gu': nrm(ks[20], (N_MOE, N_EXPERTS, D, 2 * D_EXPERT), D ** -0.5),
        'moe_w_down': nrm(ks[21], (N_MOE, N_EXPERTS, D_EXPERT, D), DEEPNORM_BETA * D_EXPERT ** -0.5),
    }

def reference(x, c, ctx, c_ctx, w_ada, b_ada, w_in, mlstm_gate_b, mlstm_norm_w, attn_sink,
              gla_gate_up, gla_gate_b, gla_norm_w, w_out, ln_w, ln_b, ffn_w_gu, ffn_w_down,
              router_w, router_b, moe_w_gu, moe_w_down):
    b_, seq, d = x.shape
    n_ctx = ctx.shape[1]
    rows = seq // GRID_W
    row = jnp.repeat(jnp.arange(rows), GRID_W)
    col = jnp.tile(jnp.arange(GRID_W), rows)
    sc, scc = jax.nn.silu(c), jax.nn.silu(c_ctx)
    xc = ctx
    for l in range(DEPTH):
        last = l == DEPTH - 1
        mod = (sc @ w_ada[l] + b_ada[l]).reshape(b_, 6, d)[:, :, None, :]
        modc = (scc @ w_ada[l] + b_ada[l]).reshape(6, d)
        h = x * (1.0 + mod[:, 1]) + mod[:, 0]
        hc = xc * (1.0 + modc[1]) + modc[0]
        mix, mix_c = mixer(h, hc, w_in[l], mlstm_gate_b[l], mlstm_norm_w[l], attn_sink[l],
                           gla_gate_up[l], gla_gate_b[l], gla_norm_w[l], w_out[l], row, col, not last)
        x = layer_norm(DEEPNORM_ALPHA * x + mod[:, 2] * mix, ln_w[l, 0], ln_b[l, 0])
        h = x * (1.0 + mod[:, 4]) + mod[:, 3]
        if last:
            tokens = h
        else:
            xc = layer_norm(DEEPNORM_ALPHA * xc + modc[2] * mix_c, ln_w[l, 0], ln_b[l, 0])
            hc = xc * (1.0 + modc[4]) + modc[3]
            tokens = jnp.concatenate([hc, h], axis=1)
        if l % 2 == 0:
            y = swiglu(tokens, ffn_w_gu[l // 2], ffn_w_down[l // 2])
        else:
            y = moe_swiglu(tokens.reshape(-1, d), router_w[l // 2], router_b[l // 2],
                           moe_w_gu[l // 2], moe_w_down[l // 2]).reshape(tokens.shape)
        if not last:
            y_c, y = y[:, :n_ctx], y[:, n_ctx:]
            xc = layer_norm(DEEPNORM_ALPHA * xc + modc[5] * y_c, ln_w[l, 1], ln_b[l, 1])
        x = layer_norm(DEEPNORM_ALPHA * x + mod[:, 5] * y, ln_w[l, 1], ln_b[l, 1])
    return x


_drawn_inputs = setup_inputs


def setup_inputs(seed=0):
    import zlib

    import numpy as np

    out = dict(_drawn_inputs(seed))
    spreads = {}
    factors = {'ctx': 2.805,
     'b_ada': 4.674,
     'mlstm_norm_w': 61.796,
     'attn_sink': 35.726,
     'gla_gate_up': 7.097,
     'gla_gate_b': 8.0,
     'gla_norm_w': 44.804,
     'router_b': 40.428}
    for name, (base, spread) in spreads.items():
        noise = np.random.default_rng([zlib.crc32(name.encode()), seed]).standard_normal(out[name].shape)
        drawn = base * np.exp(spread * noise) if base else spread * noise
        out[name] = jnp.asarray(drawn.astype(out[name].dtype))
    for name, factor in factors.items():
        out[name] = (out[name] * factor).astype(out[name].dtype)
    return out
```

```python
from contextlib import ExitStack

import numpy as np

import concourse.bass as bass
from concourse import mybir
from concourse.alu_op_type import AluOpType as ALU

ACT = mybir.ActivationFunctionType
F32 = mybir.dt.float32
I32 = mybir.dt.int32
U32 = mybir.dt.uint32
AX = mybir.AxisListType.X

P = 128
D = 1024
KT = D // P
NTOK = 512
NT = NTOK // P
DEPTH = 2
HEADS = 4
HD = 64
AH = 8
DK = 32
CH = 64
RANK = 16
NMOD = 6
C_MQ, C_MK, C_MV, C_MO, C_MG = 0, 256, 512, 768, 1024
C_AQ, C_AK, C_AV = 1040, 1552, 1680
C_GQ, C_GK, C_GV, C_GG, C_GR = 1808, 1936, 2064, 2320, 2576
NIN = 2608
WC = 512
N_IN = -(-NIN // WC)
N_ADA = NMOD * D // WC
N_OUT = D // WC
FC = 256
D_FF = 2816
N_FF = D_FF // FC
NE = 8
D_EX = 3584
N_EX = D_EX // FC
ALPHA = float((2 * DEPTH) ** 0.25)
EPS = 1e-5
NEG = -1.0e30

CONSTS = [("ident", 128), ("fwd", 128), ("bwd", 128), ("not_fwd", 128), ("not_bwd", 128),
          ("gnot_fwd", 128), ("gnot_bwd", 128), ("bias_t2", 128), ("bias_t3", 128),
          ("cos", 128), ("sin", 128), ("zeros", 1), ("reset", 512), ("ones", 128), ("blocks", 256),
          ("pick", 2), ("eights", 8), ("slots", 128)]
C_AT = {}
_n = 0
for _name, _w in CONSTS:
    C_AT[_name] = (_n, _w)
    _n += _w
NCONST = _n


def constants():
    c = np.zeros((P, NCONST), np.float32)

    def put(name, a):
        o, w = C_AT[name]
        c[:, o:o + w] = a

    i = np.arange(P)[:, None]
    j = np.arange(P)[None, :]
    put("ident", i == j)
    put("fwd", i <= j)
    put("bwd", i >= j)
    put("not_fwd", i > j)
    put("not_bwd", i < j)
    same = i // CH == j // CH
    put("gnot_fwd", ~(same & (i <= j)))
    put("gnot_bwd", ~(same & (i >= j)))
    put("bias_t2", np.where(j > i, NEG, 0.0))
    put("bias_t3", np.where(j < i, NEG, 0.0))
    inv = np.float32(10000.0) ** (-np.arange(16, dtype=np.float32) / np.float32(16))
    cos, sin = np.zeros((P, 2, 2, 2, 16)), np.zeros((P, 2, 2, 2, 16))
    for t in range(2):
        tok = t * P + np.arange(P)
        for half, pos in enumerate((tok // 64, tok % 64)):
            ang = (pos.astype(np.float32)[:, None] * inv).astype(np.float32)
            cos[:, t, half, :, :] = np.cos(ang)[:, None]
            sin[:, t, half, 0, :] = -np.sin(ang)
            sin[:, t, half, 1, :] = np.sin(ang)
    put("cos", cos.reshape(P, 128))
    put("sin", sin.reshape(P, 128))
    put("reset", np.broadcast_to((np.arange(512) % CH != 0).astype(np.float32), (P, 512)))
    put("ones", 1.0)
    put("blocks", i // DK == np.arange(256)[None, :] // HD)
    put("pick", i % 32 == np.arange(2)[None, :])
    put("eights", np.arange(8)[None, :])
    put("slots", np.arange(128)[None, :])
    return c


def bass_hymba(nc, x, c, ctx_in, c_ctx, w_ada, b_ada, w_in, mlstm_gate_b, mlstm_norm_w, attn_sink,
               gla_gate_up, gla_gate_b, gla_norm_w, w_out, ln_w, ln_b, ffn_w_gu, ffn_w_down,
               router_w, router_b, moe_w_gu, moe_w_down, consts, out):
    es = ExitStack()
    with es:
        def sb(name, shape, dt=F32):
            return es.enter_context(nc.sbuf_tensor(name, shape, dt))

        def sem(name):
            return es.enter_context(nc.semaphore(name))

        def view(t, off, *dims, p0=0, np_=P):
            row = t.shape[1]
            return bass.AP(tensor=t, offset=p0 * row + off, ap=[[row, np_]] + [list(d) for d in dims])

        X = sb("X", [P, NT * D])
        HT = sb("HT", [P, KT * NTOK])
        BIG = sb("BIG", [P, NT * NIN])
        GW = sb("GW", [P, 2 * KT * WC])
        DW = sb("DW", [P, 2 * 2 * D])
        GATE = sb("GATE", [P, 2 * D])
        LNR = sb("LNR", [P, 2 * D])
        CS = sb("CS", [P, NCONST])
        SC = sb("SC", [P, 13072])
        MOD = sb("MOD", [P, DEPTH * 48 * 2])
        PRM = sb("PRM", [P, 844])
        ST = sb("ST", [P, 512])
        RI = sb("RI", [P, 24], I32)
        IDX = sb("IDX", [P, 16], U32)
        bank = [es.enter_context(nc.psum_tensor(f"bank{i}", [P, 512], F32)) for i in range(8)]

        def cst(name, p0=0, np_=P, n=None):
            o, w = C_AT[name]
            return view(CS, o, (1, n or w), p0=p0, np_=np_)

        ident = cst("ident")
        at = 0
        pos = {}
        for name, w in (("sink", 16), ("rw", 64), ("rb", 8), ("gb", 4), ("ib", 4), 
                        ("bada", 192), ("gup", 512), ("ccol", 16), ("ecol", 16)):
            pos[name] = at
            at += w
        assert at <= 844
        NW = sb("NW", [P, 4 * 256])

        def prm(name, *dims, off=0, p0=0, np_=P):
            return view(PRM, pos[name] + off, *dims, p0=p0, np_=np_)

        def xt(t, a=0, n=D):
            return view(X, t * D + a, (1, n))

        def big(t, col, n):
            return view(BIG, t * NIN + col, (1, n))

        def bigs(t0, nt, col, *dims):
            return view(BIG, t0 * NIN + col, (NIN, nt), *dims)

        def ysum(t, a=0, n=D):
            return view(BIG, t * D + a, (1, n))

        def mod(layer, six, kt, s):
            return view(MOD, (layer * 48 + six * 8 + kt) * 2 + s, (1, 1))

        params = sem("params")
        g_loaded = [sem(f"g_loaded{s}{h}") for s in "01" for h in "ab"]
        g_free = [sem(f"g_free{s}") for s in "01"]
        d_loaded = [sem(f"d_loaded{s}") for s in "01"]
        dve_step = sem("dve_step")
        dve_block_step = sem("dve_block_step")
        act_step = sem("act_step")
        pool_step = sem("pool_step")
        S = {}

        def sm(name):
            if name not in S:
                S[name] = sem(name)
            return S[name]

        class Steps:

            def __init__(self, eng, s):
                self.eng, self.s, self.n, self.loop = eng, s, 0, None

            def __call__(self, ins):
                ins.then_inc(self.s, 1)
                self.n += 1
                self.eng.wait_ge(self.s, self.n if self.loop is None else self.n + self.loop)

            def enter(self, moved):
                self.loop = moved

            def leave(self, more):
                self.loop = None
                self.n += more

        base = {}
        n = 0
        for l in range(DEPTH):
            base["ada", l] = n
            n += N_ADA
        for l in range(DEPTH):
            base["in", l] = n
            n += N_IN
            base["out", l] = n
            n += N_OUT
            base["ff", l] = n
            n += N_FF if l == 0 else 0

        def g_slot(n):
            return n % 2

        def gw(n, kt, a=0, w=WC):
            return view(GW, (g_slot(n) * KT + kt) * WC + a, (1, w))

        def dw(m, k, half):
            return view(DW, ((m % 2) * 2 + k) * D + half * WC, (1, WC))

        OUTS = [list(range(NT)), [2, 3]]

        ATT = [[(i, j, half) for i in OUTS[l] for j in range(4) for half in range(2)] for l in range(DEPTH)]
        N_ATT = [len(a) for a in ATT]
        N_TO = [len(o) for o in OUTS]
        X_READY = [0, 4, 8, 10]

        def chunk_of(d, k):
            return k if d == 0 else (3 - k if k < 4 else 11 - k)

        SF = NT * N_FF

        SCT = 2048
        ADAR = 1024
        DIAG = 11264
        V1, ROWI, ROWF, ROWT, ROWB, ROWA, ROWM = 0, 1040, 1552, 2064, 2576, 3088, 3600
        MQT, MKT, ACOL, MD, MT, ROT = 4112, 5136, 6160, 6672, 10768, 11024
        AQT, AP_, APT = 0, 3072, 6672
        GQT, GKF, GRT, GLG, GTMP, GB_, GEB, GNB, GKD, GKT = 0, 512, 1024, 2048, 3072, 4096, 5120, 6144, 7168, 8192
        GKV, GS, GEL, GAT = 9216, 9216, 13056, 2048
        NG, NX, NSQ = 0, 1024, 2048
        FE, FH, FHT, FT = 0, 512, 1024, 1536
        SEL, CWA, YE, XGS, CWS, SELW = 2048, 4096, 6144, 7168, 8192, 10240
        XGA = 2 * D

        def in_pairs(eng, first, second, inner=None):
            first(0, 0)
            for k in range(2 * NT):
                first(k + 1, k + 1)
                second(k, k)
            with eng.Fori(1, N_FF // 2) as it:
                if inner:
                    inner(it)
                for j in range(2 * NT):
                    first(j + 1, it * 2 * NT + j + 1)
                    second(j, it * 2 * NT + j)
            k0 = (N_FF - 1) * NT
            for k in range(k0, k0 + NT):
                if k + 1 < k0 + NT:
                    first(k + 1, k + 1)
                second(k, k)

        def one_expert(eng, k0, e, first, second, inner=None):
            kk = e * N_EX + k0
            first(k0, kk)
            with eng.Fori(0, N_EX // 2 - 1) as it:
                if inner:
                    inner(it)
                for j in range(2):
                    first(k0 + j + 1, kk + it * 2 + (j + 1))
                    second(k0 + j, kk + it * 2 + j)
            if inner:
                inner(None)
            first(k0 + N_EX - 1, kk + (N_EX - 1))
            second(k0 + N_EX - 2, kk + (N_EX - 2))
            second(k0 + N_EX - 1, kk + (N_EX - 1))

        def over_experts(eng, blk, body):
            with eng.Fori(0, NE) as e:
                if not blk:
                    body(e, e)
                    return
                has = eng.value_load(RI[0:1, bass.ds(e + 1, 1)], min_val=0, max_val=1)
                rank = eng.value_load(RI[0:1, bass.ds(e + 9, 1)], min_val=0, max_val=NE - 1)
                with eng.If(has > 0):
                    body(e, rank)

        def exp_gate(act, A, k, kk):
            b = k % 2
            act.wait_ge(sm("f_up"), kk + 1)
            if not (isinstance(kk, int) and kk < 2):
                act.wait_ge(sm("f_h"), kk - 1)
            A(view(SC, FE + b * FC, (1, FC)), bank[4 + b][:, 0:FC], ACT.Exp, scale=-1.0).then_inc(sm("f_exp"), 1)

        def copy_hT(act, A, k, kk):
            b = k % 2
            act.wait_ge(sm("f_tr"), kk + 1)
            A(view(SC, FHT + b * FC, (1, FC)), bank[6 + b][:, 0:FC], ACT.Copy).then_inc(sm("f_hT"), 1)

        block = es.enter_context(nc.Block())

        @block.sync
        def _(sp):
            def weights(n, it, src_a, src_b, dst_a=None, dst_b=None):
                s = g_slot(n)
                if n >= 2 or it is not None:
                    sp.wait_ge(g_free[s], n // 2 + (0 if it is None else it))
                sp.dma_start(dst_a, src_a).then_inc(g_loaded[2 * s], 16)
                sp.dma_start(dst_b, src_b).then_inc(g_loaded[2 * s + 1], 16)

            def by_rows(n, it, w, col, width=WC):
                v = w.rearrange("(k p) n -> p k n", p=P)
                s = g_slot(n)
                dst = [view(GW, (s * KT + 4 * h) * WC, (WC, 4), (1, width)) for h in range(2)]
                src = [v[:, 4 * h:4 * h + 4, bass.ds(col, width)] for h in range(2)]
                weights(n, it, src[0], src[1], dst[0], dst[1])

            def gate_up(n, it, w, hidden, col, k_rows=None):
                v = w.rearrange("(k p) n -> p k n", p=P)
                s = g_slot(n)
                dst = [view(GW, s * KT * WC + FC * h, (WC, KT), (1, FC)) for h in range(2)]
                src = [v[:, :, bass.ds(col + hidden * h, FC)] for h in range(2)]
                weights(n, it, src[0], src[1], dst[0], dst[1])

            def down(m, units, w, row):
                s = m % 2
                if units is not None:
                    sp.wait_ge(sm("f_down"), units)
                src = w[bass.ds(row, FC), :].rearrange("(k p) n -> p k n", p=P)
                sp.dma_start(view(DW, s * 2 * D, (D, 2), (1, D)), src).then_inc(d_loaded[s], 16)

            for l in range(DEPTH):
                if l == 0:
                    for j in range(2):
                        by_rows(j, None, w_ada[0], j * WC)
                with sp.Fori(1 - l, N_ADA // 2) as it:
                    for j in range(2):
                        by_rows(base["ada", l] + j, it, w_ada[l], it * 2 * WC + j * WC)
            for l in range(DEPTH):
                for i in range(N_IN):
                    by_rows(base["in", l] + i, None, w_in[l], i * WC, min(WC, NIN - i * WC))
                for i in range(N_OUT):
                    by_rows(base["out", l] + i, None, w_out[l], i * WC)
                if l == 0:
                    for j in range(2):
                        gate_up(base["ff", 0] + j, None, ffn_w_gu[0], D_FF, j * FC)
                        down(j, None, ffn_w_down[0], j * FC)
                    with sp.Fori(1, N_FF // 2) as it:
                        for j in range(2):
                            gate_up(base["ff", 0] + j, it, ffn_w_gu[0], D_FF, it * 2 * FC + j * FC)
                            down(j, it * 2 * NT + (j - 1) * NT, ffn_w_down[0], it * 2 * FC + j * FC)
                    i = N_FF - 1
                    gate_up(base["ff", 0] + i, None, ffn_w_gu[0], D_FF, i * FC)
                    down(i, (i - 1) * NT, ffn_w_down[0], i * FC)

            def experts(blk):
                n0, m0 = base["ff", 1] + blk * NE * N_EX, N_FF + blk * NE * N_EX
                gu = moe_w_gu[0].rearrange("e d n -> (e d) n")
                dn = moe_w_down[0].rearrange("e f n -> (e f) n")
                def body(e, r):
                    with sp.Fori(0, N_EX // 2) as it:
                        for j in range(2):
                            n, m = n0 + j, m0 + j
                            moved = r * (N_EX // 2) + it
                            s = g_slot(n)
                            sp.wait_ge(g_free[s], n // 2 + moved)
                            for h in range(2):
                                src = gu[bass.ds(e * D, D), bass.ds(it * 2 * FC + (j * FC + D_EX * h), FC)]
                                sp.dma_start(view(GW, s * KT * WC + FC * h, (WC, KT), (1, FC)),
                                             src.rearrange("(k p) n -> p k n", p=P)).then_inc(g_loaded[2 * s + h], 16)
                            down(m, moved * 2 + (SF + blk * NE * N_EX + j - 1), dn, e * D_EX + it * 2 * FC + j * FC)

                over_experts(sp, blk, body)

            experts(0)
            sp.wait_ge(sm("overflow_known"), 1)
            over = sp.value_load(RI[0:1, 0:1], min_val=0, max_val=1)
            with sp.If(over > 0):
                experts(1)
            for t in range(2):
                sp.wait_ge(sm("x_final"), t + 1)
                sp.dma_start(out[0, t * P:(t + 1) * P, :], xt(2 + t)).then_inc(sm("stored"), 16)
            sp.wait_ge(sm("stored"), 32)

        @block.gpsimd
        def _(pool):
            step = Steps(pool, pool_step)
            for l in range(DEPTH):
                if l == 0:
                    step(nc.gpsimd.memset(view(SC, SCT, (1, KT * 32)), 0.0))
                    nc.gpsimd.memset(view(PRM, pos["ib"], (1, 4)), 0.0).then_inc(sm("cleared"), 1)
                pool.wait_ge(sm("p_act"), 12 * (l + 1))
                pool.wait_ge(sm("p_dve"), 12 * (l + 1))
                nc.gpsimd.memset(view(SC, V1 + 64, (65, 16), (1, 1)), 1.0).then_inc(sm("v1"), 1)
                for t in range(NT):
                    ins = nc.gpsimd.tensor_copy(view(SC, V1 + t * 260, (65, 4), (1, 64)),
                                                view(BIG, t * NIN + C_MV, (64, 4), (1, 64)))
                    ins.then_inc(sm("v1"), 1)

        @block.scalar
        def _(act):
            step = Steps(act, act_step)
            A = nc.scalar.activation

            def load(dst, src):
                act.dma_start(dst, src).then_inc(params, 16)

            for t in range(NT):
                src = (ctx_in if t < 2 else x)[0, (t % 2) * P:(t % 2 + 1) * P, :]
                act.dma_start(xt(t), src).then_inc(sm("x_loaded"), 16)
            load(CS[:, :], consts)
            load(view(SC, 0, (1, P), np_=8), c_ctx.rearrange("(k p) -> k p", p=P))
            load(view(SC, 0, (1, P), p0=8, np_=8), c.rearrange("o (k p) -> (o k) p", p=P))
            load(view(SC, P, (1, P), np_=96), b_ada.rearrange("l (j p) -> (l j) p", p=P))
            load(view(SC, 2 * P, (1, P), np_=4), gla_gate_b.rearrange("l d k -> (l d) k"))
            load(prm("gup", (P, 4), (1, P), np_=RANK), gla_gate_up.rearrange("l d r k -> r (l d) k"))
            load(prm("sink", (1, 16)), attn_sink.rearrange("l h -> (l h)").partition_broadcast(P))
            load(prm("rb", (1, 8)), router_b[0].partition_broadcast(P))
            load(prm("rw", (8, 8), (1, 8)), router_w[0].rearrange("(k p) e -> p k e", p=P))
            for l in range(DEPTH):
                load(view(NW, l * 512, (1, 256)), mlstm_norm_w[l].partition_broadcast(P))
                load(view(NW, l * 512 + 256, (1, 256)), gla_norm_w[l].partition_broadcast(P))
            act.wait_ge(sm("cleared"), 1)
            with nc.allow_non_contiguous_dma(reason="gate biases, a few bytes"):
                for l in range(DEPTH):
                    for g in range(2):
                        for d in range(2):
                            load(prm("ib", (1, 1), off=2 * l + g, p0=32 * d, np_=4),
                                 mlstm_gate_b[l, d, g].rearrange("(h o) -> h o", o=1))

            def ln_rows(i):
                l, j = divmod(i, 2)
                if i:
                    act.wait_ge(sm("ln_used"), i)
                act.dma_start(view(LNR, 0, (1, D)), ln_w[l, j].partition_broadcast(P)).then_inc(sm("ln_rows"), 16)
                act.dma_start(view(LNR, D, (1, D)), ln_b[l, j].partition_broadcast(P)).then_inc(sm("ln_rows"), 16)

            ln_rows(0)
            act.wait_ge(sm("c_col"), 1)
            A(prm("ecol", (1, 16)), prm("ccol", (1, 16)), ACT.Exp, scale=-1.0).then_inc(sm("c_exp"), 1)
            for l in range(DEPTH):
                with act.Fori(0, N_ADA // 2) as it:
                    for j in range(2):
                        act.wait_ge(sm("ada_mm"), l * N_ADA + it * 2 + j + 1)
                        A(view(SC, ADAR + j * 512, (1, 512)), bank[j][:, :], ACT.Copy).then_inc(sm("ada_row"), 1)

            def gate_rows(i):
                for s in range(2):
                    for half in range(2):
                        k = i * 4 + s * 2 + half
                        act.wait_ge(sm("gate_mm"), k + 1)
                        A(view(GATE, s * D + half * 512, (1, 512)), bank[6 + half][:, :], ACT.Copy).then_inc(sm("gate_row"), 1)

            def h_context(u, l, six):
                for kt in range(KT):
                    act.wait_ge(sm("x_T"), u * KT + kt + 1)
                    A(view(HT, kt * 512, (1, 256)), bank[kt % 2][:, 0:256], ACT.Identity,
                      scale=mod(l, six + 1, kt, 0), bias=mod(l, six, kt, 0)).then_inc(sm("h_ctx"), 1)

            def slots_context(blk):
                for b in range(4):
                    act.wait_ge(sm("sw_T"), 4 * blk + b + 1)
                    A(view(SC, CWA + b * 512, (1, 512)), bank[b][:, :], ACT.Copy).then_inc(sm("sw_copy"), 1)
                with act.Fori(0, NE // 2) as it:
                    for j in range(2):
                        act.wait_ge(sm("gx_mm"), blk * NE + it * 2 + j + 1)
                        for q in range(4):
                            ins = A(BIG[:, bass.ds(it * 2048 + (XGA + j * 1024 + q * P), P)],
                                    bank[4 + 2 * j][:, q * P:(q + 1) * P], ACT.Identity,
                                    scale=mod(1, 4, q, 1), bias=mod(1, 3, q, 1))
                        ins.then_inc(sm("gx_a"), 1)

            def experts(blk):
                slots_context(blk)
                k0 = SF + blk * NE * N_EX
                over_experts(act, blk, lambda e, r: one_expert(act, k0, r, lambda k, kk: exp_gate(act, A, k, kk),
                                                               lambda k, kk: copy_hT(act, A, k, kk)))

            def rstd(name, src, dst, n, scale):
                step(A(dst, src, ACT.Ln, scale=scale, bias=view(ST, 500, (1, 1))))
                A(dst, dst, ACT.Exp, scale=-0.5).then_inc(sm(name), 1)

            for l in range(DEPTH):
                nto = N_TO[l]
                t0 = OUTS[l][0]
                gate_rows(2 * l)
                h_context(2 * l, l, 0)
                for g in range(0, N_IN * NT, 2):
                    cchunk, t = divmod(g, NT)
                    w = min(WC, NIN - cchunk * WC)
                    act.wait_ge(sm("p_mm"), l * N_IN * NT + g + 1)
                    A(big(t, cchunk * WC, w), bank[4 + g % 4][:, 0:w], ACT.Copy).then_inc(sm("p_act"), 1)
                for g in range(2):
                    act.wait_ge(sm("m_T"), l * 6 + g + 1)
                    A(view(SC, ROWI + g * 512, (1, 512), np_=64), bank[g][0:64, :], ACT.Identity,
                      bias=prm("ib", (1, 1), off=2 * l + g, np_=64)).then_inc(sm("gates"), 1)
                for g in range(2):
                    act.wait_ge(sm("m_T"), l * 6 + g + 3)
                    A(view(SC, MQT + g * 512, (1, 512)), bank[2 + g][:, :], ACT.Copy).then_inc(sm("mq_T"), 1)
                act.wait_ge(sm("f_abs"), l + 1)
                r = view(SC, ROWT, (1, 512), np_=64)
                step(A(r, r, ACT.Exp))
                A(r, r, ACT.Ln, bias=1.0).then_inc(sm("f_ln"), 1)
                act.wait_ge(sm("gate_rows_ready"), l + 1)
                A(r, r, ACT.Exp).then_inc(sm("floor_row"), 1)
                act.wait_ge(sm("gates_T"), l + 1)
                step(A(view(SC, ACOL, (1, 256)), bank[0][:, 0:256], ACT.Copy, scale=-1.0))
                A(view(SC, ACOL + 256, (1, 256)), bank[0][:, 256:512], ACT.Copy).then_inc(sm("gate_cols"), 1)
                for u in range(8):
                    h, d = divmod(u, 2)
                    act.wait_ge(sm("m_bc"), 8 * l + u + 1)
                    if 8 * l + u >= 2:
                        act.wait_ge(sm("m_pv"), 8 * l + u - 1)
                    for j in range(4):
                        a, n = (0, 512) if j < 2 else (256, 256)
                        step(A(view(SC, MD + d * 2048 + j * 512 + a, (1, n)), bank[4 + d][:, a:a + n], ACT.Relu,
                               bias=view(SC, ACOL + j * 64 + d * 32 + h, (1, 1))))
                    v = view(SC, MD + d * 2048, (1, 1024))
                    step(A(v, v, ACT.Exp, scale=-1.0))
                    v = view(SC, MD + d * 2048 + 1280, (512, 2), (1, 256))
                    A(v, v, ACT.Exp, scale=-1.0).then_inc(sm("m_decay"), 1)
                for j in range(6):
                    act.wait_ge(sm("a_T"), l * 6 + j + 1)
                    a = 256 if (j < 4 and l == DEPTH - 1) else 0
                    A(view(HT, AQT + j * 512 + a, (1, 512 - a)), bank[j][:, a:512], ACT.Copy,
                      scale=0.125 if j < 4 else 1.0).then_inc(sm("a_qk"), 1)
                off = sum(N_ATT[:l])
                for k in range(N_ATT[l] + 1):
                    if k < N_ATT[l]:
                        i, j, half = ATT[l][k]
                        n = 256 if i < 2 else 512
                        b = k % 2
                        act.wait_ge(sm("a_max"), off + k + 1)
                        if k >= 2:
                            act.wait_ge(sm("a_pT"), off + k - 1)
                            act.wait_ge(sm("a_out"), off + k - 1)
                        A(view(HT, AP_ + b * 512, (1, n)), bank[b][:, 0:n], ACT.Exp, bias=view(ST, 100 + b, (1, 1)),
                          accum_out=view(ST, 102 + b, (1, 1))).then_inc(sm("a_exp"), 1)
                        A(view(ST, 104 + b, (1, 1)), prm("sink", (1, 1), off=l * 8 + 2 * j + half), ACT.Exp,
                          bias=view(ST, 100 + b, (1, 1))).then_inc(sm("a_exp"), 1)
                    if k >= 1:
                        k1 = k - 1
                        n = 256 if ATT[l][k1][0] < 2 else 512
                        act.wait_ge(sm("a_pT"), off + k1 + 1)
                        if k1 >= 2:
                            act.wait_ge(sm("a_pv"), off + k1 - 1)
                        A(view(SC, APT + (k1 % 2) * 512, (1, n)), bank[2 + k1 % 2][:, 0:n], ACT.Copy).then_inc(sm("a_pTs"), 1)
                for g in range(2):
                    act.wait_ge(sm("g_T"), l * 4 + g + 1)
                    A(view(SC, GQT + g * 512, (1, 512)), bank[g][:, :], ACT.Copy,
                      scale=float(np.float32(DK ** -0.5)) if g == 0 else 1.0).then_inc(sm("g_qk"), 1)
                for d in range(2):
                    act.wait_ge(sm("g_z"), 2 * l + d + 1)
                    A(view(SC, GLG + d * 512, (1, 512)), bank[4 + d][:, :], ACT.Identity,
                      bias=prm("gb", (1, 1), off=2 * l + d)).then_inc(sm("g_zb"), 1)
                act.wait_ge(sm("g_abs"), l + 1)
                r = view(SC, GTMP, (1, 1024))
                step(A(r, r, ACT.Exp))
                A(r, r, ACT.Ln, bias=1.0).then_inc(sm("g_ln"), 1)
                act.wait_ge(sm("g_cum"), l + 1)
                A(view(SC, GEB, (1, 1024)), view(SC, GB_, (1, 1024)), ACT.Exp, scale=1 / 16).then_inc(sm("g_eb"), 1)
                A(view(SC, GNB, (1, 1024)), view(SC, GB_, (1, 1024)), ACT.Exp, scale=-1 / 16).then_inc(sm("g_eb"), 1)
                act.wait_ge(sm("g_rest"), l + 1)
                A(view(SC, GKD, (1, 1024)), view(SC, GKD, (1, 1024)), ACT.Exp, scale=1 / 16).then_inc(sm("g_eb"), 1)
                for d in range(2):
                    act.wait_ge(sm("g_kT"), 2 * l + d + 1)
                    A(view(SC, GKT + d * 512, (1, 512)), bank[6 + d][:, :], ACT.Copy).then_inc(sm("g_ktok"), 1)
                for d in range(2):
                    act.wait_ge(sm("g_a"), 2 * l + d + 1)
                    if d == 1:
                        act.wait_ge(sm("g_pv"), 2 * l + 1)
                    for h in range(4):
                        ins = A(view(SC, GAT + h * 512, (1, 512)), bank[4 + h][:, :], ACT.Copy)
                    ins.then_inc(sm("g_acopy"), 1)
                for g in range(2):
                    act.wait_ge(sm("n_gate_free"), 2 * l + g + 1)
                    A(view(SC, NG, (256, nto), (1, 256)), bigs(t0, nto, (C_MO, C_GG)[g], (1, 256)), ACT.Exp,
                      scale=-1.0).then_inc(sm("n_gate"), 1)
                    act.wait_ge(sm("n_var"), 2 * l + g + 1)
                    rstd("n_rstd", view(ST, 32, (1, 4 * nto)), view(ST, 48, (1, 4 * nto)), 16, 1 / HD)
                for kt in range(0, KT, 2):
                    act.wait_ge(sm("c_T"), l * KT + kt + 1)
                    A(view(HT, kt * 512 + t0 * P, (1, nto * P)), bank[kt % 4][:, t0 * P:512], ACT.Copy).then_inc(sm("c_act"), 1)
                act.wait_ge(sm("r_var"), 2 * l + 1)
                rstd("r_rstd", view(ST, 64 + 1, (2, nto)), view(ST, 80, (1, nto)), nto, 1.0)
                ln_rows(2 * l + 1)
                gate_rows(2 * l + 1)
                if l == 0:
                    h_context(1, 0, 3)
                    def exp(k, kk):
                        exp_gate(act, A, k, kk)

                    def hT(k, kk):
                        copy_hT(act, A, k, kk)

                    in_pairs(act, exp, hT)
                else:
                    act.wait_ge(sm("r_diff"), 1)
                    A(view(ST, 136, (1, 2)), view(ST, 136, (1, 2)), ACT.Exp).then_inc(sm("r_exp"), 1)
                    experts(0)
                    act.wait_ge(sm("overflow_known"), 1)
                    over = act.value_load(RI[0:1, 0:1], min_val=0, max_val=1)
                    with act.If(over > 0):
                        experts(1)
                act.wait_ge(sm("r_var"), 2 * l + 2)
                rstd("r_rstd", view(ST, 64 + 1, (2, nto)), view(ST, 80, (1, nto)), nto, 1.0)
                if l == 0:
                    ln_rows(2)

        @block.vector
        def _(dve):
            V = nc.vector
            step = Steps(dve, dve_step)

            def signal(ins, name, total):
                ins.then_inc(sm(name), 1)
                dve.wait_ge(sm(name), total)

            step(V.memset(view(ST, 500, (1, 1)), EPS))
            dve.wait_ge(sm("start_T"), 1)
            dve.wait_ge(sm("cleared"), 1)
            step(V.tensor_copy(prm("ccol", (1, 16)), bank[0][:, 0:16]))
            for s in range(2):
                step(V.tensor_copy(prm("bada", (2, 96), off=s), bank[0][:, 16:112]))
            V.tensor_copy(prm("gb", (1, 4)), bank[0][:, 112:116]).then_inc(sm("c_col"), 1)
            dve.wait_ge(sm("c_exp"), 1)
            e = prm("ecol", (1, 16))
            step(V.tensor_scalar(e, e, 1.0, None, ALU.add))
            step(V.reciprocal(e, e))
            V.tensor_tensor(view(SC, SCT, (1, 2), (32, KT)), prm("ccol", (8, 2), (1, 8)), prm("ecol", (8, 2), (1, 8)),
                            ALU.mult).then_inc(sm("sct"), 1)
            for l in range(DEPTH):
                with dve.Fori(0, N_ADA // 2) as it:
                    for j in range(2):
                        dve.wait_ge(sm("ada_col"), l * N_ADA + it * 2 + j + 1)
                        o = it * 16 + (l * 96 + j * 8)
                        V.tensor_tensor(MOD[:, bass.ds(o, 8)], bank[2 + j][:, 0:8],
                                        PRM[:, bass.ds(o + pos["bada"], 8)], ALU.add).then_inc(sm("mod"), 1)
                dve.wait_ge(sm("mod"), (l + 1) * N_ADA)
                v = view(MOD, l * 96 + 16, (48, 2), (1, 16))
                step(V.tensor_scalar(v, v, 1.0, None, ALU.add))
            V.memset(view(ST, 501, (1, 1)), 0.0).then_inc(sm("mods"), 1)

            def diagonals(i):
                l, j = divmod(i, 2)
                for s in range(2):
                    for half in range(2):
                        k = i * 4 + s * 2 + half
                        if k >= 2:
                            dve.wait_ge(sm("gate_mm"), k - 1)
                        for q in range(4):
                            ins = V.tensor_scalar(view(SC, DIAG + half * 512 + q * P, (1, P)), ident,
                                                  mod(l, 3 * j + 2, half * 4 + q, s), None, ALU.mult)
                        ins.then_inc(sm("diag"), 1)

            def h_latent(u, l, six):
                for kt in range(KT):
                    dve.wait_ge(sm("x_T"), u * KT + kt + 1)
                    V.tensor_scalar(view(HT, kt * 512 + 256, (1, 256)), bank[2 + kt % 2][:, 256:512],
                                    mod(l, six + 1, kt, 1), mod(l, six, kt, 1), ALU.mult, ALU.add).then_inc(sm("h_lat"), 1)

            def layer_norm(i, from_psum):
                l = i // 2
                outs = OUTS[l]
                dve.wait_ge(sm("gate_row"), 4 * (i + 1))
                dve.wait_ge(sm("ln_rows"), 32 * (i + 1))
                for n, t in enumerate(outs):
                    g = view(GATE, (t // 2) * D, (1, D))
                    if from_psum:
                        for cc in range(2):
                            dve.wait_ge(sm("o_mm"), sum(2 * m for m in N_TO[:l]) + cc * len(outs) + n + 1)
                            step(V.tensor_tensor(ysum(n, cc * 512, 512), bank[t * 2 + cc][:, :],
                                                 view(GATE, (t // 2) * D + cc * 512, (1, 512)), ALU.mult))
                    else:
                        step(V.tensor_tensor(ysum(n), ysum(n), g, ALU.mult))
                    step(V.scalar_tensor_tensor(ysum(n), xt(t), ALPHA, ysum(n), ALU.mult, ALU.add))
                    for cc in range(2):
                        step(V.bn_stats(view(ST, 240 + 6 * cc, (1, 6)), ysum(n, cc * 512, 512)))
                    step(V.bn_aggr(view(ST, 64 + 2 * n, (1, 2)), view(ST, 240, (1, 12))))
                V.memset(view(ST, 501, (1, 1)), 0.0).then_inc(sm("r_var"), 1)
                dve.wait_ge(sm("r_rstd"), i + 1)
                for n, t in enumerate(outs):
                    step(V.tensor_scalar(ysum(n), ysum(n), view(ST, 64 + 2 * n, (1, 1)), view(ST, 80 + n, (1, 1)),
                                         ALU.subtract, ALU.mult))
                    step(V.tensor_tensor(ysum(n), ysum(n), view(LNR, 0, (1, D)), ALU.mult))
                    ins = V.tensor_tensor(xt(t), ysum(n), view(LNR, D, (1, D)), ALU.add)
                    if i == 3:
                        signal(ins, "x_final", n + 1)
                    else:
                        signal(ins, "x_ready", X_READY[i] + n + 1)
                V.memset(view(ST, 501, (1, 1)), 0.0).then_inc(sm("ln_used"), 1)

            def scans(dst, off_src, op0, op1, cumulate):
                def go(p0, o, n, initial):
                    s = 1 if p0 == 0 else -1
                    src = view(SC, off_src + o, (s, n), p0=p0, np_=32)
                    first = view(CS, C_AT["ones"][0], (0, n), p0=p0, np_=32) if cumulate else src
                    step(V.tensor_tensor_scan(view(SC, dst + o, (s, n), p0=p0, np_=32), first, src, initial, op0, op1))
                go(0, 0, 512, 0.0)
                go(32, 255, 256, 0.0)
                go(32, 511, 256, view(SC, dst, (1, 1), p0=32, np_=32))

            def mask(name, k):
                o, w = C_AT[name]
                v = view(CS, o, (0, k), (1, P))
                return v.bitcast(U32)

            def zeros(k):
                return view(CS, C_AT["zeros"][0], (0, k), (0, P))

            for l in range(DEPTH):
                outs = OUTS[l]
                nto = len(outs)
                t0 = outs[0]
                last = l == DEPTH - 1
                diagonals(2 * l)
                h_latent(2 * l, l, 0)
                for g in range(1, N_IN * NT, 2):
                    cchunk, t = divmod(g, NT)
                    w = min(WC, NIN - cchunk * WC)
                    dve.wait_ge(sm("p_mm"), l * N_IN * NT + g + 1)
                    V.tensor_copy(big(t, cchunk * WC, w), bank[4 + g % 4][:, 0:w]).then_inc(sm("p_dve"), 1)
                dve.wait_ge(sm("gates"), 2 * l + 2)
                rf, rt = (view(SC, o, (1, 512), np_=64) for o in (ROWF, ROWT))
                V.scalar_tensor_tensor(rt, rf, -1.0, rf, ALU.mult, ALU.min).then_inc(sm("f_abs"), 1)
                for g in range(2):
                    dve.wait_ge(sm("m_T"), l * 6 + 5 + g)
                    V.tensor_scalar(view(SC, MKT + g * 512, (1, 512)), bank[4 + g][:, :], HD ** -0.5, None,
                                    ALU.mult).then_inc(sm("mk_T"), 1)
                dve.wait_ge(sm("p_act"), 12 * (l + 1))
                dve.wait_ge(sm("p_dve"), 12 * (l + 1))
                for t in (2, 3):
                    for jj in range(2):
                        step(V.tensor_tensor(view(SC, ROT + jj * 16, (64, 10), (32, 2), (1, 16)),
                                             view(BIG, t * NIN + C_AQ + (1 - jj) * 16, (64, 10), (32, 2), (1, 16)),
                                             view(CS, C_AT["sin"][0] + (t - 2) * 64 + jj * 16, (0, 10), (32, 2), (1, 16)),
                                             ALU.mult))
                    v = view(BIG, t * NIN + C_AQ, (64, 10), (1, 64))
                    step(V.tensor_tensor(v, v, view(CS, C_AT["cos"][0] + (t - 2) * 64, (0, 10), (1, 64)), ALU.mult))
                    v = view(BIG, t * NIN + C_AQ, (1, 640))
                    V.tensor_tensor(v, v, view(SC, ROT, (1, 640)), ALU.add).then_inc(sm("rope"), 1)
                    dve.wait_ge(sm("rope"), 2 * l + t - 1)
                dve.wait_ge(sm("f_ln"), l + 1)
                step(V.scalar_tensor_tensor(rf, rf, 0.0, rt, ALU.min, ALU.subtract))
                scans(ROWB, ROWF, ALU.mult, ALU.add, True)
                ra, rb_, rm, ri = (view(SC, o, (1, 512), np_=64) for o in (ROWA, ROWB, ROWM, ROWI))
                step(V.tensor_tensor(ra, ri, rb_, ALU.subtract))
                scans(ROWM, ROWA, ALU.max, ALU.max, False)
                V.scalar_tensor_tensor(rt, rb_, -1.0, rm, ALU.mult, ALU.subtract).then_inc(sm("gate_rows_ready"), 1)

                def weigh(u):
                    h, d = divmod(u, 2)
                    o = MD + d * 2048
                    dve.wait_ge(sm("m_decay"), 8 * l + u + 1)
                    step(V.copy_predicated(view(SC, o, (640, 4), (1, P)), mask(("not_fwd", "not_bwd")[d], 4), zeros(4)))
                    dve.wait_ge(sm("m_s"), 4 * l + h + 1)
                    for j in range(2):
                        v = view(SC, o + j * 512, (1, 512))
                        V.tensor_tensor(v, v, bank[1 + j][:, :], ALU.mult).then_inc(sm("m_w"), 1)
                    v = view(SC, o + 2 * 512 + 256, (512, 2), (1, 256))
                    V.tensor_tensor(v, v, bank[3][:, :].rearrange("p (a b) -> p a b", a=2), ALU.mult).then_inc(sm("m_w"), 1)

                def normalise(u):
                    h, d = divmod(u, 2)
                    dve.wait_ge(sm("m_pv"), 8 * l + u + 1)
                    pv = bank[6 + d][:, t0 * 65:260].rearrange("p (t c) -> p t c", c=65)
                    den = view(ST, 440, (1, nto))
                    dve.wait_ge(sm("gate_cols"), l + 1)
                    step(V.tensor_tensor(den, pv[:, :, 64], view(SC, ACOL + 256 + t0 * 64 + d * 32 + h, (64, nto)), ALU.max))
                    step(V.scalar_tensor_tensor(den, pv[:, :, 64], -1.0, den, ALU.mult, ALU.max))
                    step(V.reciprocal(den, den))
                    r = view(ST, 440, (1, nto), (0, 64))
                    dst = bigs(t0, nto, C_MQ + h * 64, (1, 64))
                    if d == 0:
                        signal(V.tensor_tensor(dst, pv[:, :, 0:64], r, ALU.mult), "m_hs", 8 * l + u + 1)
                    else:
                        tmp = view(SC, MT, (64, nto), (1, 64))
                        step(V.tensor_tensor(tmp, pv[:, :, 0:64], r, ALU.mult))
                        signal(V.tensor_tensor(dst, dst, tmp, ALU.add), "m_hs", 8 * l + u + 1)

                for u in range(9):
                    if u < 8:
                        weigh(u)
                    if u >= 1:
                        normalise(u - 1)
                off = sum(N_ATT[:l])
                for k in range(N_ATT[l] + 2):
                    if k < N_ATT[l]:
                        i, j, half = ATT[l][k]
                        b = k % 2
                        dve.wait_ge(sm("a_s"), off + k + 1)
                        step(V.tensor_reduce(view(ST, 106 + b, (1, 1)), bank[b][:, 0:256 if i < 2 else 512], AX, ALU.max))
                        V.tensor_scalar(view(ST, 100 + b, (1, 1)), view(ST, 106 + b, (1, 1)),
                                        prm("sink", (1, 1), off=l * 8 + 2 * j + half), -1.0, ALU.max,
                                        ALU.mult).then_inc(sm("a_max"), 1)
                    if k >= 2:
                        i, j, half = ATT[l][k - 2]
                        b = k % 2
                        dve.wait_ge(sm("a_pv"), off + k - 1)
                        den = view(ST, 108 + b, (1, 1))
                        V.tensor_scalar(big(i, C_AQ + (2 * j + half) * 64, 64), bank[4 + b][:, 0:64], den, None,
                                        ALU.mult).then_inc(sm("a_o"), 1)
                    if k >= 1 and k - 1 < N_ATT[l]:
                        b = (k - 1) % 2
                        dve.wait_ge(sm("a_exp"), 2 * (off + k))
                        den = view(ST, 108 + b, (1, 1))
                        step(V.tensor_tensor(den, view(ST, 102 + b, (1, 1)), view(ST, 104 + b, (1, 1)), ALU.add))
                        signal(V.reciprocal(den, den), "a_out", off + k)
                for d in range(2):
                    dve.wait_ge(sm("g_T"), 4 * l + 3 + d)
                    V.tensor_copy(view(SC, GRT + d * 512, (1, 512), np_=16), bank[2 + d][0:16, :]).then_inc(sm("g_r"), 1)
                dve.wait_ge(sm("g_zb"), 2 * l + 2)
                lg, tmp = view(SC, GLG, (1, 1024)), view(SC, GTMP, (1, 1024))
                V.scalar_tensor_tensor(tmp, lg, -1.0, lg, ALU.mult, ALU.min).then_inc(sm("g_abs"), 1)
                dve.wait_ge(sm("g_ln"), l + 1)
                step(V.scalar_tensor_tensor(lg, lg, 0.0, tmp, ALU.min, ALU.subtract))
                reset = cst("reset")
                step(V.tensor_tensor_scan(view(SC, GB_, (1, 512)), reset, view(SC, GLG, (1, 512)), 0.0, ALU.mult, ALU.add))
                signal(V.tensor_tensor_scan(view(SC, GB_ + 1023, (-1, 512)), reset, view(SC, GLG + 1023, (-1, 512)), 0.0,
                                            ALU.mult, ALU.add), "g_cum", l + 1)
                for d in range(2):
                    last_b = view(SC, GB_ + (63 if d == 0 else 512), (64, 8), (0, 64))
                    step(V.tensor_tensor(view(SC, GKD + d * 512, (64, 8), (1, 64)), last_b,
                                         view(SC, GB_ + d * 512, (64, 8), (1, 64)), ALU.subtract))
                V.memset(view(ST, 501, (1, 1)), 0.0).then_inc(sm("g_rest"), 1)
                dve.wait_ge(sm("g_eb"), 3 * (l + 1))
                for d in range(2):
                    step(V.tensor_copy(view(SC, GEL + d * 8, (1, 8)), view(SC, GEB + (63 if d == 0 else 512), (64, 8))))
                dve.wait_ge(sm("g_qk"), 2 * (l + 1))
                for dst, src in ((GKD, GKF), (GNB, GKF), (GEB, GQT)):
                    v = view(SC, dst, (512, 2), (1, 512))
                    V.tensor_tensor(v, v, view(SC, src, (0, 2), (1, 512)), ALU.mult).then_inc(sm("g_prod"), 1)
                for q in range(14):
                    k, d = divmod(q, 2)
                    n = 14 * l + q + 1
                    dve.wait_ge(sm("g_kv"), n)
                    new = view(SC, GS + (d * 7 + k + 1) * 256, (1, 256))
                    if k == 0:
                        signal(V.tensor_tensor(new, bank[q % 4][:, 0:256], cst("blocks"), ALU.mult), "g_st", n)
                        continue
                    kv = view(SC, GKV, (1, 256))
                    step(V.tensor_tensor(kv, bank[q % 4][:, 0:256], cst("blocks"), ALU.mult))
                    signal(V.scalar_tensor_tensor(new, view(SC, GS + (d * 7 + k) * 256, (1, 256)),
                                                  view(SC, GEL + d * 8 + chunk_of(d, k), (1, 1)), kv, ALU.mult, ALU.add),
                           "g_st", n)
                for d in range(2):
                    dve.wait_ge(sm("g_acopy"), 2 * l + d + 1)
                    V.copy_predicated(view(SC, GAT, (P, 16), (1, P)), mask(("gnot_fwd", "gnot_bwd")[d], 16),
                                      zeros(16)).then_inc(sm("g_aok"), 1)
                dve.wait_ge(sm("g_pv"), 2 * l + 2)
                for i in outs:
                    step(V.tensor_copy(big(i, C_GQ, 256), bank[i][:, 0:256]))

                for g in range(2):
                    col = (C_MQ, C_GQ)[g]
                    V.memset(view(ST, 501, (1, 1)), 0.0).then_inc(sm("n_gate_free"), 1)
                    src = bigs(t0, nto, col, (1, 256)).rearrange("p t (h c) -> p (t h) c", h=4) if False else None
                    mean, ssq = view(ST, 16, (1, 4 * nto)), view(ST, 32, (1, 4 * nto))
                    for n, t in enumerate(outs):
                        step(V.tensor_reduce(view(ST, 16 + 4 * n, (1, 4)), view(BIG, t * NIN + col, (64, 4), (1, 64)), AX, ALU.add))
                    step(V.tensor_scalar(mean, mean, 1.0 / HD, None, ALU.mult))
                    for n, t in enumerate(outs):
                        step(V.tensor_tensor(view(SC, NX + n * 256, (64, 4), (1, 64)), view(BIG, t * NIN + col, (64, 4), (1, 64)),
                                             view(ST, 16 + 4 * n, (1, 4), (0, 64)), ALU.subtract))
                    xc, sq = view(SC, NX, (1, 256 * nto)), view(SC, NSQ, (1, 256 * nto))
                    step(V.tensor_tensor(sq, xc, xc, ALU.mult))
                    V.tensor_reduce(ssq, view(SC, NSQ, (64, 4 * nto), (1, 64)), AX, ALU.add).then_inc(sm("n_var"), 1)
                    dve.wait_ge(sm("n_gate"), 2 * l + g + 1)
                    gate = view(SC, NG, (1, 256 * nto))
                    step(V.tensor_scalar(gate, gate, 1.0, None, ALU.add))
                    step(V.reciprocal(gate, gate))
                    gate2 = view(SC, NG, (256, nto), (1, 256))
                    if g == 1:
                        step(V.tensor_tensor(gate2, gate2, bigs(t0, nto, C_GG, (1, 256)), ALU.mult))
                    dve.wait_ge(sm("n_rstd"), 2 * l + g + 1)
                    x3 = view(SC, NX, (64, 4 * nto), (1, 64))
                    step(V.tensor_tensor(x3, x3, view(ST, 48, (1, 4 * nto), (0, 64)), ALU.mult))
                    x2 = view(SC, NX, (256, nto), (1, 256))
                    step(V.tensor_tensor(x2, x2, view(NW, l * 512 + g * 256, (0, nto), (1, 256)), ALU.mult))
                    signal(V.tensor_tensor(bigs(t0, nto, col, (1, 256)), x2, gate2, ALU.mult), "cat", 2 * l + g + 1)
                for kt in range(1, KT, 2):
                    dve.wait_ge(sm("c_T"), l * KT + kt + 1)
                    V.tensor_copy(view(HT, kt * 512 + t0 * P, (1, nto * P)), bank[kt % 4][:, t0 * P:512]).then_inc(sm("c_dve"), 1)
                layer_norm(2 * l, True)
                diagonals(2 * l + 1)
                h_latent(2 * l + 1, l, 3)

                def hidden(st, k, kk):
                    b = k % 2
                    e, tmp = view(SC, FE + b * FC, (1, FC)), view(SC, FT + b * FC, (1, FC))
                    dve.wait_ge(sm("f_exp"), kk + 1)
                    st(V.tensor_scalar(e, e, 1.0, None, ALU.add))
                    st(V.reciprocal(e, e))
                    st(V.tensor_tensor(tmp, bank[4 + b][:, 0:FC], e, ALU.mult))
                    if not (isinstance(kk, int) and kk < 2):
                        dve.wait_ge(sm("f_tr"), kk - 1)
                    V.tensor_tensor(view(SC, FH + b * FC, (1, FC)), tmp, bank[4 + b][:, FC:2 * FC], ALU.mult).then_inc(sm("f_h"), 1)

                def add_down(k, kk, y):
                    dve.wait_ge(sm("f_down"), kk + 1)
                    if not (isinstance(kk, int) and kk == 0):
                        dve.wait_ge(sm("f_y"), kk * 2)
                    for half in range(2):
                        v = y(half)
                        V.tensor_tensor(v, v, bank[half][:, :], ALU.add).then_inc(sm("f_y"), 1)

                if not last:
                    step(V.memset(view(BIG, 0, (1, NT * D)), 0.0))
                    def inner(it):
                        step.loop = it * (3 * 2 * NT) - 3 * 2 * NT

                    def first(k, kk):
                        hidden(step, k, kk)
                        if not isinstance(kk, int) and k == 2 * NT:
                            step.leave(3 * 2 * NT * (N_FF // 2 - 2))

                    in_pairs(dve, first, lambda k, kk: add_down(k, kk, lambda half: ysum(k % NT, half * 512, 512)), inner)
                    layer_norm(1, False)
                    continue

                dve.wait_ge(sm("r_mm"), 1)
                for i in range(2):
                    lo, top = view(ST, 200 + 8 * i, (1, 8)), view(ST, 216 + 8 * i, (1, 8))
                    step(V.tensor_tensor(lo, bank[4][:, 8 * i:8 * i + 8], prm("rb", (1, 8)), ALU.add))
                    step(V.max(top, lo))
                    step(V.max_index(IDX[:, 8 * i:8 * i + 8], top, lo))
                    step(V.tensor_tensor(view(ST, 136 + i, (1, 1)), view(ST, 217 + 8 * i, (1, 1)),
                                         view(ST, 216 + 8 * i, (1, 1)), ALU.subtract))
                V.tensor_copy(view(ST, 256, (1, 16)), IDX[:, :]).then_inc(sm("r_diff"), 1)
                dve.wait_ge(sm("r_diff"), 1)
                dve.wait_ge(sm("r_exp"), 1)
                step(V.tensor_scalar(view(ST, 138, (1, 2)), view(ST, 136, (1, 2)), 1.0, None, ALU.add))
                step(V.reciprocal(view(ST, 138, (1, 2)), view(ST, 138, (1, 2))))
                step(V.tensor_tensor(view(ST, 136, (1, 2)), view(ST, 136, (1, 2)), view(ST, 138, (1, 2)), ALU.mult))
                for i in range(2):
                    def one_hot(at, scale, which):
                        step(V.tensor_scalar(view(ST, at + 8 * i, (1, 8)), cst("eights"),
                                             view(ST, 256 + 8 * i + which, (1, 1)), scale, ALU.is_equal, ALU.mult))
                    one_hot(272, 1.0, 0)
                    one_hot(288, 1.0, 1)
                    one_hot(304, view(ST, 138 + i, (1, 1)), 0)
                    one_hot(320, view(ST, 136 + i, (1, 1)), 1)
                step(V.tensor_tensor(view(ST, 304, (1, 16)), view(ST, 304, (1, 16)), view(ST, 320, (1, 16)), ALU.add))
                signal(V.tensor_tensor(view(ST, 272, (1, 16)), view(ST, 272, (1, 16)), view(ST, 288, (1, 16)), ALU.add),
                       "r_chosen", 1)
                dve.wait_ge(sm("r_count"), 1)
                step(V.tensor_tensor(view(ST, 336, (1, 16)), bank[5][:, 0:16], view(ST, 272, (1, 16)), ALU.mult))
                step(V.tensor_scalar(view(ST, 336, (1, 16)), view(ST, 336, (1, 16)), -1.0, None, ALU.add))
                over_f, rank_f = view(ST, 353, (1, 8), np_=1), view(ST, 361, (1, 8), np_=1)
                step(V.tensor_scalar(over_f, bank[5][0:1, 16:24], float(P), None, ALU.is_gt))
                step(V.tensor_reduce(view(ST, 352, (1, 1), np_=1), over_f, AX, ALU.max))
                step(V.tensor_tensor_scan(rank_f, view(CS, C_AT["ones"][0], (0, 8), np_=1), over_f, 0.0, ALU.mult, ALU.add))
                step(V.tensor_tensor(rank_f, rank_f, over_f, ALU.subtract))
                V.tensor_copy(RI[0:1, 0:17], view(ST, 352, (1, 17), np_=1)).then_inc(sm("overflow_known"), 1)

                def experts(st, blk):
                    if blk:
                        st(V.tensor_scalar(view(ST, 336, (1, 16)), view(ST, 336, (1, 16)), -float(P), None, ALU.add))
                    for e in range(NE):
                        for i in range(2):
                            place = view(ST, 336 + 8 * i + e, (1, 1))
                            V.tensor_scalar(view(SC, SEL + e * 256 + i * P, (1, P)), cst("slots"), place, None,
                                            ALU.is_equal).then_inc(sm("sel"), 1)
                            V.tensor_scalar(view(SC, SELW + e * 256 + i * P, (1, P)), cst("slots"), place,
                                            view(ST, 304 + 8 * i + e, (1, 1)), ALU.is_equal, ALU.mult).then_inc(sm("sel"), 1)
                    with dve.Fori(0, NE // 2) as it:
                        for j in range(2):
                            dve.wait_ge(sm("gx_mm"), blk * NE + it * 2 + j + 1)
                            for q in range(4):
                                ins = V.tensor_scalar(BIG[:, bass.ds(it * 2048 + (XGA + j * 1024 + (4 + q) * P), P)],
                                                      bank[5 + 2 * j][:, q * P:(q + 1) * P], mod(1, 4, 4 + q, 1),
                                                      mod(1, 3, 4 + q, 1), ALU.mult, ALU.add)
                            ins.then_inc(sm("gx_d"), 1)
                    dve.wait_ge(sm("gx_a"), (blk + 1) * NE)
                    dve.wait_ge(sm("gx_d"), (blk + 1) * NE)
                    dve.wait_ge(sm("sw_copy"), 4 * (blk + 1))
                    k0 = SF + blk * NE * N_EX
                    n0 = st.n
                    per_unit = 3
                    per_expert = per_unit * N_EX
                    def body(e, r):
                        def inner(it):
                            st.loop = r * per_expert if it is None else r * per_expert + it * (2 * per_unit)
                            if it is None:
                                st.n += 2 * per_unit * (N_EX // 2 - 2)

                        st.loop = r * per_expert
                        for dst, src, n in ((view(SC, XGS, (1, D)), BIG[:, bass.ds(e * D + XGA, D)], 1),
                                            (view(SC, CWS, (1, 2 * P)), SC[:, bass.ds(e * 256 + CWA, 256)], 1)):
                            V.tensor_copy(dst, src).then_inc(sm("x_slots"), 1)
                        V.memset(view(SC, YE, (1, D)), 0.0).then_inc(sm("x_slots"), 1)
                        dve.wait_ge(sm("x_slots"), r * 3 + 3 * (blk * NE + 1))
                        one_expert(dve, k0, r, lambda k, kk: hidden(st, k, kk),
                                   lambda k, kk: add_down(k, kk, lambda half: view(SC, YE + half * 512, (1, 512))), inner)
                        dve.wait_ge(sm("s_mm"), r + blk * NE + 1)
                        for i in range(2):
                            for half in range(2):
                                v = ysum(i, half * 512, 512)
                                V.tensor_tensor(v, v, bank[2 * i + half][:, :], ALU.add).then_inc(sm("s_add"), 1)
                        dve.wait_ge(sm("s_add"), r * 4 + 4 * (blk * NE + 1))
                        V.memset(view(ST, 501, (1, 1)), 0.0)

                    over_experts(dve, blk, body)
                    assert st.n - n0 == per_expert, (st.n - n0, per_expert)
                    st.leave(per_expert * (NE - 1))

                step(V.memset(view(BIG, 0, (1, 2 * D)), 0.0))
                experts(step, 0)
                over = dve.value_load(RI[0:1, 0:1], min_val=0, max_val=1)
                with dve.If(over > 0):
                    experts(Steps(dve, dve_block_step), 1)
                layer_norm(3, False)

        @block.tensor
        def _(pe):
            T = nc.tensor
            mm = nc.tensor.matmul

            def ready(n, it=None):
                s = g_slot(n)
                for h in range(2):
                    v = 16 * (n // 2 + 1)
                    pe.wait_ge(g_loaded[2 * s + h], v if it is None else it * 16 + v)

            pe.wait_ge(params, 16 * 21)
            for a, n, o in ((0, 16, 0), (P, 96, 16), (2 * P, 4, 112)):
                ins = T.transpose(bank[0][:, o:o + n], view(SC, a, (1, P), np_=n), cst("ident", 0, n, n))
            ins.then_inc(sm("start_T"), 1)
            pe.wait_ge(sm("sct"), 1)
            def ada_pair(l, it):
                i = 0 if it is None else it
                for j in range(2):
                    n = base["ada", l] + j
                    ready(n, it)
                    for kt in range(KT):
                        g = kt % 4
                        ins = mm(bank[j][32 * g:32 * g + 32, :], view(SC, SCT + kt * 32, (1, 32)), gw(n, kt),
                                 start=kt < 4, stop=kt >= 4)
                    ins.then_inc(sm("ada_mm"), 1)
                for j in range(2):
                    pe.wait_ge(sm("ada_row"), i * 2 + (l * N_ADA + j + 1))
                    if it is not None:
                        pe.wait_ge(sm("mod"), i * 2 + l * N_ADA)
                    for q in range(4):
                        ins = mm(bank[2 + j][:, 2 * q:2 * q + 2], view(SC, ADAR + j * 512 + q * P, (1, P)), cst("pick"),
                                 start=True, stop=True)
                        if q == 0:
                            ins.then_inc(g_free[j], 1)
                    ins.then_inc(sm("ada_col"), 1)

            ada_pair(0, None)
            for l in range(DEPTH):
                with pe.Fori(1 - l, N_ADA // 2) as it:
                    ada_pair(l, it)
            pe.wait_ge(sm("mods"), 1)

            def gate_products(i):
                for s in range(2):
                    for half in range(2):
                        k = i * 4 + s * 2 + half
                        pe.wait_ge(sm("diag"), k + 1)
                        if k >= 2:
                            pe.wait_ge(sm("gate_row"), k - 1)
                        mm(bank[6 + half][:, :], cst("ones", n=P), view(SC, DIAG + half * 512, (1, 512)), start=True,
                           stop=True).then_inc(sm("gate_mm"), 1)

            def x_transposes(u, tiles):
                for kt in range(KT):
                    if kt >= 2:
                        pe.wait_ge(sm("h_lat"), u * KT + kt - 1)
                        if 0 in tiles:
                            pe.wait_ge(sm("h_ctx"), u * KT + kt - 1)
                    for t in tiles:
                        ins = T.transpose(bank[kt % 2 + 2 * (t // 2)][:, t * P:(t + 1) * P], xt(t, kt * P, P), ident)
                    ins.then_inc(sm("x_T"), 1)

            for l in range(DEPTH):
                outs = OUTS[l]
                t0 = outs[0]
                if l == 0:
                    pe.wait_ge(sm("x_loaded"), 16 * NT)
                else:
                    pe.wait_ge(sm("x_ready"), X_READY[2 * l])
                gate_products(2 * l)
                x_transposes(2 * l, range(NT))
                pe.wait_ge(sm("h_ctx"), KT * (2 * l + 1))
                pe.wait_ge(sm("h_lat"), KT * (2 * l + 1))
                for g in range(N_IN * NT):
                    cchunk, t = divmod(g, NT)
                    n = base["in", l] + cchunk
                    w = min(WC, NIN - cchunk * WC)
                    if t == 0:
                        ready(n)
                    if g >= 4:
                        pe.wait_ge(sm("p_dve" if g % 2 else "p_act"), 12 * l + (g - 4) // 2 + 1)
                    else:
                        pe.wait_ge(sm("gate_row"), 4 * (2 * l + 1))
                    for kt in range(KT):
                        ins = mm(bank[4 + g % 4][:, 0:w], view(HT, kt * 512 + t * P, (1, P)), gw(n, kt, 0, w),
                                 start=kt == 0, stop=kt == KT - 1)
                        if t == 0 and kt == 0 and cchunk:
                            ins.then_inc(g_free[g_slot(n - 1)], 1)
                    ins.then_inc(sm("p_mm"), 1)
                pe.wait_ge(sm("p_act"), 12 * (l + 1))
                pe.wait_ge(sm("p_dve"), 12 * (l + 1))
                for g in range(6):
                    for t in range(NT):
                        if g < 2:
                            for d in range(2):
                                ins = mm(bank[g][32 * d:32 * d + 32, t * P:(t + 1) * P], big(t, C_MG + 4 * g + 8 * d, 32),
                                         ident, start=True, stop=True)
                        else:
                            ins = T.transpose(bank[g][:, t * P:(t + 1) * P], big(t, (g - 2) * P, P), ident)
                        if g == 0 and t == 0:
                            ins.then_inc(g_free[g_slot(base["in", l] + N_IN - 1)], 1)
                    ins.then_inc(sm("m_T"), 1)
                pe.wait_ge(sm("mq_T"), 2 * (l + 1))
                pe.wait_ge(sm("mk_T"), 2 * (l + 1))
                pe.wait_ge(sm("v1"), 5 * (l + 1))

                def m_scores(h):
                    p0 = 64 * (h % 2)
                    if h:
                        pe.wait_ge(sm("m_w"), 3 * (8 * l + 2 * h))
                    for j in range(4):
                        dst = bank[1 + j][:, :] if j < 2 else bank[3][:, (j - 2) * 256:(j - 1) * 256]
                        a, n = (0, 512) if j < 2 else (256, 256)
                        ins = mm(dst, view(SC, MKT + (h // 2) * 512 + j * P, (1, P), p0=p0, np_=64),
                                 view(SC, MQT + (h // 2) * 512 + a, (1, n), p0=p0, np_=64), start=True, stop=True)
                    ins.then_inc(sm("m_s"), 1)

                def m_stabiliser(u):
                    h, d = divmod(u, 2)
                    if u >= 2:
                        pe.wait_ge(sm("m_decay"), 8 * l + u - 1)
                    row = d * 32 + h
                    o = C_AT["ident"][0]
                    mm(bank[4 + d][:, :], view(CS, o + row, (0, P), np_=64), view(SC, ROWM, (1, 512), np_=64), start=True,
                       stop=True).then_inc(sm("m_bc"), 1)

                def m_values(u):
                    h, d = divmod(u, 2)
                    pe.wait_ge(sm("m_w"), 3 * (8 * l + u + 1))
                    if u >= 2:
                        pe.wait_ge(sm("m_hs"), 8 * l + u - 1)
                    for i in outs:
                        if d == 0:
                            keys = list(range(i + 1))
                        else:
                            keys = [j for j in range(NT) if (j >= i if (i < 2) == (j < 2) else i >= 2)]
                        for q, j in enumerate(keys):
                            ins = mm(bank[6 + d][:, i * 65:(i + 1) * 65], view(SC, MD + d * 2048 + j * 512 + i * P, (1, P)),
                                     view(SC, V1 + j * 260 + h * 65, (1, 65)), start=q == 0, stop=q == len(keys) - 1)
                    ins.then_inc(sm("m_pv"), 1)

                m_scores(0)
                pe.wait_ge(sm("gate_rows_ready"), l + 1)
                m_stabiliser(0)
                m_stabiliser(1)
                pe.wait_ge(sm("floor_row"), l + 1)
                for k, src in enumerate((ROWA, ROWT)):
                    for j in range(NT):
                        ins = T.transpose(bank[0][:, k * 256 + j * 64:k * 256 + (j + 1) * 64],
                                          view(SC, src + j * P, (1, P), np_=64), cst("ident", 0, 64, 64))
                ins.then_inc(sm("gates_T"), 1)
                for u in range(8):
                    if u + 2 < 8:
                        m_stabiliser(u + 2)
                    m_values(u)
                    if u % 2 and u < 7:
                        m_scores(u // 2 + 1)
                pe.wait_ge(sm("rope"), 2 * (l + 1))
                pe.wait_ge(sm("gate_cols"), l + 1)
                pe.wait_ge(sm("m_decay"), 8 * (l + 1))
                for j in range(6):
                    for t in (range(NT) if j >= 4 else outs):
                        if j < 4:
                            ins = T.transpose(bank[j][:, t * P:(t + 1) * P], big(t, C_AQ + j * P, P), ident)
                            continue
                        for half in range(2):
                            ins = mm(bank[j][64 * half:64 * half + 64, t * P:(t + 1) * P],
                                     big(t, C_AK + (j - 4) * 64, 64), ident, start=True, stop=True)
                    ins.then_inc(sm("a_T"), 1)
                pe.wait_ge(sm("a_qk"), 6 * (l + 1))
                off = sum(N_ATT[:l])
                for k in range(N_ATT[l] + 2):
                    if k < N_ATT[l]:
                        i, j, half = ATT[l][k]
                        b, n, p0 = k % 2, 256 if i < 2 else 512, 64 * half
                        if k >= 2:
                            pe.wait_ge(sm("a_exp"), 2 * (off + k - 1))
                        ins = mm(bank[b][:, 0:n], view(HT, AQT + j * 512 + i * P, (1, P), p0=p0, np_=64),
                                 view(HT, AQT + (4 + j // 2) * 512, (1, n), p0=p0, np_=64), start=True, stop=i < 2)
                        if i >= 2:
                            o = (5 - i) * P
                            ins = mm(bank[b][:, o:o + P], ident, cst("bias_t2" if i == 2 else "bias_t3"), start=False,
                                     stop=True)
                        ins.then_inc(sm("a_s"), 1)
                    if 1 <= k <= N_ATT[l]:
                        i = ATT[l][k - 1][0]
                        b = (k - 1) % 2
                        pe.wait_ge(sm("a_exp"), 2 * (off + k))
                        if k >= 3:
                            pe.wait_ge(sm("a_pTs"), off + k - 2)
                        for q in range(2 if i < 2 else 4):
                            ins = T.transpose(bank[2 + b][:, q * P:(q + 1) * P], view(HT, AP_ + b * 512 + q * P, (1, P)), ident)
                        ins.then_inc(sm("a_pT"), 1)
                    if k >= 2:
                        i, j, half = ATT[l][k - 2]
                        b = k % 2
                        pe.wait_ge(sm("a_pTs"), off + k - 1)
                        if k >= 4:
                            pe.wait_ge(sm("a_o"), off + k - 3)
                        nk = 2 if i < 2 else 4
                        for q in range(nk):
                            ins = mm(bank[4 + b][:, 0:64], view(SC, APT + b * 512 + q * P, (1, P)),
                                     big(q, C_AV + (j // 2) * 64, 64), start=q == 0, stop=q == nk - 1)
                        ins.then_inc(sm("a_pv"), 1)
                pe.wait_ge(sm("a_o"), off + N_ATT[l])
                pe.wait_ge(sm("m_hs"), 8 * (l + 1))
                for g in range(4):
                    for t in range(NT):
                        rows = P if g < 2 else RANK
                        c0 = (C_GQ, C_GK, C_GR, C_GR + RANK)[g]
                        ins = T.transpose(bank[g][0:rows, t * P:(t + 1) * P], big(t, c0, rows), ident)
                    ins.then_inc(sm("g_T"), 1)
                for d in range(2):
                    pe.wait_ge(sm("g_r"), 2 * l + d + 1)
                    mm(bank[4 + d][:, :], prm("gup", (1, P), off=(2 * l + d) * P, np_=RANK),
                       view(SC, GRT + d * 512, (1, 512), np_=RANK), start=True, stop=True).then_inc(sm("g_z"), 1)
                pe.wait_ge(sm("g_prod"), 3 * l + 1)
                for d in range(2):
                    for t in range(NT):
                        ins = T.transpose(bank[6 + d][:, t * P:(t + 1) * P], view(SC, GKD + d * 512 + t * P, (1, P)), ident)
                    ins.then_inc(sm("g_kT"), 1)
                pe.wait_ge(sm("g_qk"), 2 * (l + 1))
                pe.wait_ge(sm("g_prod"), 3 * l + 3)
                pe.wait_ge(sm("g_ktok"), 2 * (l + 1))

                def g_scores(d):
                    if d == 1:
                        pe.wait_ge(sm("g_acopy"), 2 * l + 1)
                    for i in range(NT):
                        for h in range(4):
                            a = d * 512 + i * P
                            ins = mm(bank[4 + h][:, i * P:(i + 1) * P], view(SC, GNB + a, (1, P), p0=32 * h, np_=32),
                                     view(SC, GEB + a, (1, P), p0=32 * h, np_=32), start=True, stop=True)
                    ins.then_inc(sm("g_a"), 1)

                def g_values(d):
                    pe.wait_ge(sm("g_aok"), 2 * l + d + 1)
                    for i in outs:
                        for h in range(4):
                            ins = mm(bank[i][:, h * 64:(h + 1) * 64], view(SC, GAT + h * 512 + i * P, (1, P)),
                                     big(i, C_GV + h * 64, 64), start=d == 0 and h == 0, stop=False, skip_group_check=True)
                        for cc in range(2):
                            ch = 2 * i + cc
                            k = ch if d == 0 else (3 - ch if ch < 4 else 11 - ch)
                            if k:
                                ins = mm(bank[i][64 * cc:64 * cc + 64, 0:256], view(SC, GEB + d * 512 + ch * 64, (1, 64)),
                                         view(SC, GS + (d * 7 + k) * 256, (1, 256)), start=False, stop=d == 1,
                                         skip_group_check=True)
                    ins.then_inc(sm("g_pv"), 1)

                g_scores(0)
                for q in range(14):
                    k, d = divmod(q, 2)
                    ch = chunk_of(d, k)
                    p0 = 64 * (ch % 2)
                    if q >= 4:
                        pe.wait_ge(sm("g_st"), 14 * l + q - 3)
                    mm(bank[q % 4][:, 0:256], view(SC, GKT + d * 512 + (ch // 2) * P, (1, P), p0=p0, np_=64),
                       view(BIG, (ch // 2) * NIN + C_GV, (1, 256), p0=p0, np_=64), start=True, stop=True).then_inc(sm("g_kv"), 1)
                g_scores(1)
                pe.wait_ge(sm("g_st"), 14 * (l + 1))
                g_values(0)
                g_values(1)
                pe.wait_ge(sm("cat"), 2 * (l + 1))
                for kt in range(KT):
                    if kt >= 4:
                        pe.wait_ge(sm("c_dve" if kt % 2 else "c_act"), 4 * l + (kt - 4) // 2 + 1)
                    c0 = C_MQ + kt * P if kt < 2 else (C_AQ + (kt - 2) * P if kt < 6 else C_GQ + (kt - 6) * P)
                    for t in outs:
                        ins = T.transpose(bank[kt % 4][:, t * P:(t + 1) * P], big(t, c0, P), ident)
                    ins.then_inc(sm("c_T"), 1)
                pe.wait_ge(sm("c_act"), 4 * (l + 1))
                pe.wait_ge(sm("c_dve"), 4 * (l + 1))
                for cc in range(N_OUT):
                    n = base["out", l] + cc
                    ready(n)
                    for t in outs:
                        for kt in range(KT):
                            ins = mm(bank[t * 2 + cc][:, :], view(HT, kt * 512 + t * P, (1, P)), gw(n, kt), start=kt == 0,
                                     stop=kt == KT - 1)
                        ins.then_inc(sm("o_mm"), 1)
                    pe.drain().then_inc(g_free[g_slot(n)], 1)
                pe.wait_ge(sm("x_ready"), X_READY[2 * l] + N_TO[l])
                gate_products(2 * l + 1)
                x_transposes(2 * l + 1, outs)

                def up(k, kk, n, moved, lhsT, first, frees):
                    b = k % 2
                    if first:
                        ready(n, moved)
                    if not (isinstance(kk, int) and kk < 2):
                        pe.wait_ge(sm("f_h"), kk - 1)
                    for kt in range(KT):
                        ins = mm(bank[4 + b][:, :], lhsT(kt), gw(n, kt), start=kt == 0, stop=kt == KT - 1)
                        if kt == 0 and first and frees:
                            ins.then_inc(g_free[g_slot(n - 1)], 1)
                    ins.then_inc(sm("f_up"), 1)

                def down(k, kk, m, moved, first, ends, n):
                    b = k % 2
                    pe.wait_ge(sm("f_h"), kk + 1)
                    for q in range(2):
                        ins = T.transpose(bank[6 + b][:, q * P:(q + 1) * P], view(SC, FH + b * FC + q * P, (1, P)), ident)
                        if ends and q == 0:
                            ins.then_inc(g_free[g_slot(n)], 1)
                    ins.then_inc(sm("f_tr"), 1)
                    if first:
                        v = 16 * (m // 2 + 1)
                        pe.wait_ge(d_loaded[m % 2], v if moved is None else moved * 16 + v)
                    pe.wait_ge(sm("f_hT"), kk + 1)
                    if not (isinstance(kk, int) and kk == 0):
                        pe.wait_ge(sm("f_y"), kk * 2)
                    for half in range(2):
                        for q in range(2):
                            ins = mm(bank[half][:, :], view(SC, FHT + b * FC + q * P, (1, P)), dw(m, q, half), start=q == 0,
                                     stop=q == 1)
                    ins.then_inc(sm("f_down"), 1)

                if l == 0:
                    pe.wait_ge(sm("h_ctx"), KT * 2)
                    pe.wait_ge(sm("h_lat"), KT * 2)
                    n0 = base["ff", 0]

                    state = {"it": None}

                    def first(k, kk):
                        ch, t = divmod(k, NT)
                        moved = None if isinstance(kk, int) else state["it"]
                        up(k, kk, n0 + ch, moved, lambda kt: view(HT, kt * 512 + t * P, (1, P)), t == 0, k > 0)

                    def second(k, kk):
                        ch, t = divmod(k, NT)
                        moved = None if isinstance(kk, int) else state["it"]
                        down(k, kk, ch, moved, t == 0, False, n0 + ch)

                    in_pairs(pe, first, second, lambda it: state.update(it=it))
                    pe.drain().then_inc(g_free[g_slot(n0 + N_FF - 1)], 1)
                    continue

                pe.wait_ge(sm("h_lat"), KT * 4)
                for i in range(2):
                    for kt in range(KT):
                        ins = mm(bank[4][:, 8 * i:8 * i + 8], view(HT, kt * 512 + (2 + i) * P, (1, P)), prm("rw", (1, 8), off=8 * kt),
                                 start=kt == 0, stop=kt == KT - 1)
                ins.then_inc(sm("r_mm"), 1)
                pe.wait_ge(sm("r_chosen"), 1)
                chosen = [view(ST, 272 + 8 * i, (1, 8)) for i in range(2)]
                ones = cst("ones", n=P)
                mm(bank[5][:, 0:8], cst("fwd"), chosen[0], start=True, stop=True)
                mm(bank[5][:, 8:16], ones, chosen[0], start=True, stop=False)
                mm(bank[5][:, 8:16], cst("fwd"), chosen[1], start=False, stop=True)
                mm(bank[5][0:1, 16:24], cst("ones", n=1), chosen[0], start=True, stop=False)
                mm(bank[5][0:1, 16:24], cst("ones", n=1), chosen[1], start=False, stop=True).then_inc(sm("r_count"), 1)

                def experts(blk):
                    pe.wait_ge(sm("sel"), (blk + 1) * NE * 4)
                    for q in range(16):
                        ins = T.transpose(bank[q // 4][:, (q % 4) * P:(q % 4 + 1) * P], view(SC, SELW + q * P, (1, P)), ident)
                        if q % 4 == 3:
                            ins.then_inc(sm("sw_T"), 1)
                    def gather(it):
                        for j in range(2):
                            if not isinstance(it, int):
                                pe.wait_ge(sm("gx_a"), it * 2 + blk * NE)
                                pe.wait_ge(sm("gx_d"), it * 2 + blk * NE)
                            for kt in range(KT):
                                for i in range(2):
                                    ins = mm(bank[4 + 2 * j + kt // 4][:, (kt % 4) * P:(kt % 4 + 1) * P], xt(2 + i, kt * P, P),
                                             SC[:, bass.ds(it * 512 + (SEL + j * 256 + i * P), P)], start=i == 0, stop=i == 1)
                            ins.then_inc(sm("gx_mm"), 1)

                    gather(0)
                    with pe.Fori(1, NE // 2) as it:
                        gather(it)
                    pe.wait_ge(sm("gx_a"), blk * NE + NE)
                    pe.wait_ge(sm("gx_d"), blk * NE + NE)
                    pe.wait_ge(sm("sw_copy"), 4 * (blk + 1))
                    n0, m0, k0 = base["ff", 1] + blk * NE * N_EX, N_FF + blk * NE * N_EX, SF + blk * NE * N_EX
                    def body(e, r):
                        pe.wait_ge(sm("x_slots"), r * 3 + 3 * (blk * NE + 1))
                        st = {"moved": r * (N_EX // 2)}

                        def first(k, kk):
                            up(k, kk, n0 + k - k0, st["moved"], lambda kt: view(SC, XGS + kt * P, (1, P)), True, k > k0)

                        def second(k, kk):
                            down(k, kk, m0 + k - k0, st["moved"], True, k == k0 + N_EX - 1, n0 + k - k0)

                        def inner(it):
                            st["moved"] = r * (N_EX // 2) if it is None else r * (N_EX // 2) + it

                        one_expert(pe, k0, r, first, second, inner)
                        pe.wait_ge(sm("f_y"), (r * N_EX + (k0 + N_EX)) * 2)
                        for i in range(2):
                            for half in range(2):
                                ins = mm(bank[2 * i + half][:, :], view(SC, CWS + i * P, (1, P)), view(SC, YE + half * 512, (1, 512)),
                                         start=True, stop=True)
                        ins.then_inc(sm("s_mm"), 1)
                        pe.wait_ge(sm("s_add"), r * 4 + 4 * (blk * NE + 1))

                    over_experts(pe, blk, body)

                experts(0)
                over = pe.value_load(RI[0:1, 0:1], min_val=0, max_val=1)
                with pe.If(over > 0):
                    experts(1)


_INS = ["x", "c", "ctx", "c_ctx", "w_ada", "b_ada", "w_in", "mlstm_gate_b", "mlstm_norm_w", "attn_sink",
        "gla_gate_up", "gla_gate_b", "gla_norm_w", "w_out", "ln_w", "ln_b", "ffn_w_gu", "ffn_w_down",
        "router_w", "router_b", "moe_w_gu", "moe_w_down"]
_OUTS = [((1, 256, 1024), "float32")]


def kernel(**inputs):
    import numpy as _np
    import concourse.bacc as _bacc
    from concourse import mybir as _mybir
    from concourse.bass_utils import run_bass_kernel_spmd as _run

    nc = _bacc.Bacc("TRN2", target_bir_lowering=False, num_devices=1)
    arrays, args = {}, []
    for name in _INS + ["constants"]:
        a = _np.ascontiguousarray(inputs[name]) if name != "constants" else constants()
        arrays[f"in_{name}_dram"] = a
        args.append(nc.dram_tensor(f"in_{name}_dram", a.shape, _mybir.dt.from_np(a.dtype), kind="ExternalInput").ap())
    for i, (shape, dtype) in enumerate(_OUTS):
        dt = _mybir.dt.from_np(_np.dtype(dtype))
        args.append(nc.dram_tensor(f"out_{i}_dram", shape, dt, kind="ExternalOutput").ap())
    bass_hymba(nc, *args)
    r = _run(nc, [arrays], core_ids=[0])
    got = tuple(r.results[0][f"out_{i}_dram"] for i in range(len(_OUTS)))
    return got[0]
```

```python
from contextlib import ExitStack

import numpy as np

import concourse.bass as bass
from concourse import mybir
from concourse.alu_op_type import AluOpType as ALU

ACT = mybir.ActivationFunctionType
F32 = mybir.dt.float32
I32 = mybir.dt.int32
U32 = mybir.dt.uint32
F32R = mybir.dt.float32r
AX = mybir.AxisListType.X

P = 128
D = 1024
KT = D // P
NTOK = 512
NT = NTOK // P
DEPTH = 2
HEADS = 4
HD = 64
AH = 8
DK = 32
CH = 64
RANK = 16
NMOD = 6
C_MQ, C_MK, C_MV, C_MO, C_MG = 0, 256, 512, 768, 1024
C_AQ, C_AK, C_AV = 1040, 1552, 1680
C_GQ, C_GK, C_GV, C_GG, C_GR = 1808, 1936, 2064, 2320, 2576
NIN = 2608
WC = 512
N_IN = -(-NIN // WC)
N_ADA = NMOD * D // WC
N_OUT = D // WC
FC = 256
D_FF = 2816
N_FF = D_FF // FC
NE = 8
D_EX = 3584
N_EX = D_EX // FC
ALPHA = float((2 * DEPTH) ** 0.25)
EPS = 1e-5
NEG = -1.0e30

CONSTS = [("ident", 128), ("fwd", 128), ("bwd", 128), ("not_fwd", 128), ("not_bwd", 128),
          ("gnot_fwd", 128), ("gnot_bwd", 128), ("bias_t2", 128), ("bias_t3", 128),
          ("cos", 128), ("sin", 128), ("zeros", 1), ("reset", 512), ("ones", 128), ("blocks", 256),
          ("pick", 2), ("eights", 8), ("slots", 128)]
C_AT = {}
_n = 0
for _name, _w in CONSTS:
    C_AT[_name] = (_n, _w)
    _n += _w
NCONST = _n


def constants():
    c = np.zeros((P, NCONST), np.float32)

    def put(name, a):
        o, w = C_AT[name]
        c[:, o:o + w] = a

    i = np.arange(P)[:, None]
    j = np.arange(P)[None, :]
    put("ident", i == j)
    put("fwd", i <= j)
    put("bwd", i >= j)
    put("not_fwd", i > j)
    put("not_bwd", i < j)
    same = i // CH == j // CH
    put("gnot_fwd", ~(same & (i <= j)))
    put("gnot_bwd", ~(same & (i >= j)))
    put("bias_t2", np.where(j > i, NEG, 0.0))
    put("bias_t3", np.where(j < i, NEG, 0.0))
    inv = np.float32(10000.0) ** (-np.arange(16, dtype=np.float32) / np.float32(16))
    cos, sin = np.zeros((P, 2, 2, 2, 16)), np.zeros((P, 2, 2, 2, 16))
    for t in range(2):
        tok = t * P + np.arange(P)
        for half, pos in enumerate((tok // 64, tok % 64)):
            ang = (pos.astype(np.float32)[:, None] * inv).astype(np.float32)
            cos[:, t, half, :, :] = np.cos(ang)[:, None]
            sin[:, t, half, 0, :] = -np.sin(ang)
            sin[:, t, half, 1, :] = np.sin(ang)
    put("cos", cos.reshape(P, 128))
    put("sin", sin.reshape(P, 128))
    put("reset", np.broadcast_to((np.arange(512) % CH != 0).astype(np.float32), (P, 512)))
    put("ones", 1.0)
    put("blocks", i // DK == np.arange(256)[None, :] // HD)
    put("pick", i % 32 == np.arange(2)[None, :])
    put("eights", np.arange(8)[None, :])
    put("slots", np.arange(128)[None, :])
    return c


def bass_hymba(nc, x, c, ctx_in, c_ctx, w_ada, b_ada, w_in, mlstm_gate_b, mlstm_norm_w, attn_sink,
               gla_gate_up, gla_gate_b, gla_norm_w, w_out, ln_w, ln_b, ffn_w_gu, ffn_w_down,
               router_w, router_b, moe_w_gu, moe_w_down, consts, out):
    es = ExitStack()
    with es:
        PLACE = {}

        def sb(name, shape, dt=F32):
            t = es.enter_context(nc.sbuf_tensor(name, shape, dt))
            PLACE[t.name] = nc.sbuf_base - shape[1] * 4
            assert PLACE[t.name] % 32 == 0
            return t

        def sem(name):
            return es.enter_context(nc.semaphore(name))

        def view(t, off, *dims, p0=0, np_=P):
            row = t.shape[1]
            return bass.AP(tensor=t, offset=p0 * row + off, ap=[[row, np_]] + [list(d) for d in dims])

        X = sb("X", [P, NT * D])
        HT = sb("HT", [P, KT * NTOK])
        BIG = sb("BIG", [P, NT * NIN])
        GW = sb("GW", [P, 2 * KT * WC])
        DW = sb("DW", [P, 2 * 2 * D])
        GATE = sb("GATE", [P, 2 * D])
        LNR = sb("LNR", [P, 2 * D])
        CS = sb("CS", [P, NCONST])
        SC = sb("SC", [P, 13072])
        MOD = sb("MOD", [P, DEPTH * 48 * 2])
        PRM = sb("PRM", [P, 844])
        ST = sb("ST", [P, 512])
        RI = sb("RI", [P, 24], I32)
        IDX = sb("IDX", [P, 16], U32)
        bank = [es.enter_context(nc.psum_tensor(f"bank{i}", [P, 512], F32)) for i in range(8)]

        ROUNDED = {t.name: nc.alloc_sbuf_tensor_at(f"{t.name}_hi_lo", t.shape, F32R, offset=PLACE[t.name])
                   for t in (X, HT, BIG, GW, SC)}

        def rview(t, off, *dims, p0=0, np_=P):
            return view(ROUNDED[t.name], off, *dims, p0=p0, np_=np_)

        def cst(name, p0=0, np_=P, n=None):
            o, w = C_AT[name]
            return view(CS, o, (1, n or w), p0=p0, np_=np_)

        ident = cst("ident")
        at = 0
        pos = {}
        for name, w in (("sink", 16), ("rw", 64), ("rb", 8), ("gb", 4), ("ib", 4), 
                        ("bada", 192), ("gup", 512), ("ccol", 16), ("ecol", 16)):
            pos[name] = at
            at += w
        assert at <= 844
        NW = sb("NW", [P, 4 * 256])

        def prm(name, *dims, off=0, p0=0, np_=P):
            return view(PRM, pos[name] + off, *dims, p0=p0, np_=np_)

        def xt(t, a=0, n=D):
            return view(X, t * D + a, (1, n))

        def big(t, col, n):
            return view(BIG, t * NIN + col, (1, n))

        def bigs(t0, nt, col, *dims):
            return view(BIG, t0 * NIN + col, (NIN, nt), *dims)

        def ysum(t, a=0, n=D):
            return view(BIG, t * D + a, (1, n))

        def mod(layer, six, kt, s):
            return view(MOD, (layer * 48 + six * 8 + kt) * 2 + s, (1, 1))

        params = sem("params")
        g_loaded = [sem(f"g_loaded{s}{h}") for s in "01" for h in "ab"]
        g_free = [sem(f"g_free{s}") for s in "01"]
        d_loaded = [sem(f"d_loaded{s}") for s in "01"]
        dve_step = sem("dve_step")
        dve_block_step = sem("dve_block_step")
        act_step = sem("act_step")
        pool_step = sem("pool_step")
        S = {}

        def sm(name):
            if name not in S:
                S[name] = sem(name)
            return S[name]

        class Steps:

            def __init__(self, eng, s):
                self.eng, self.s, self.n, self.loop = eng, s, 0, None

            def __call__(self, ins):
                ins.then_inc(self.s, 1)
                self.n += 1
                self.eng.wait_ge(self.s, self.n if self.loop is None else self.n + self.loop)

            def enter(self, moved):
                self.loop = moved

            def leave(self, more):
                self.loop = None
                self.n += more

        base = {}
        n = 0
        base["ada", 0] = n
        n += N_ADA
        for l in range(DEPTH):
            base["in", l] = n
            n += N_IN
            if l == 0:
                base["ada", 1] = n
                n += N_ADA
            base["out", l] = n
            n += N_OUT
            base["ff", l] = n
            n += N_FF if l == 0 else 0

        def g_slot(n):
            return n % 2

        def gw(n, kt, a=0, w=WC):
            return view(GW, (g_slot(n) * KT + kt) * WC + a, (1, w))

        def dw(m, k, half):
            return view(DW, ((m % 2) * 2 + k) * D + half * WC, (1, WC))

        split_base = {("in", 0): 0, ("ff", 0): N_IN, ("in", 1): N_IN + N_FF, ("ex", 1): 2 * N_IN + N_FF}

        def hi_at(stage, s, kt):
            if stage == "in":
                return SC, (s * KT + kt) * WC
            if stage == "ff":
                return SC, 2048 + (s * KT + kt) * WC
            if s == 0:
                return HT, kt * WC
            return (X, kt * WC) if kt < 4 else (SC, SEL + (kt - 4) * WC)

        def hi(stage, n, kt, w=WC):
            t, o = hi_at(stage, g_slot(n), kt)
            return rview(t, o, (1, w))

        def lo(n, kt, w=WC):
            return rview(GW, (g_slot(n) * KT + kt) * WC, (1, w))

        def write_hi(act, stage, n, moved, half, w=WC):
            s = g_slot(n)
            act.wait_ge(g_loaded[2 * s + half], 32 * (n // 2 + 1) + (0 if moved is None else moved * 32))
            t, o = hi_at(stage, s, 4 * half)
            nc.scalar.activation(rview(t, o, (WC, 4), (1, w)),
                                 view(GW, (s * KT + 4 * half) * WC, (WC, 4), (1, w)), ACT.Copy).then_inc(sm("w_hi"), 1)

        def write_lo(dve, stage, n, i, moved, half, w=WC):
            s = g_slot(n)
            dve.wait_ge(sm("w_hi"), 2 * i + half + 1 + (0 if moved is None else moved * 4))
            t, o = hi_at(stage, s, 4 * half)
            at = (GW, (s * KT + 4 * half) * WC, (WC, 4), (1, w))
            nc.vector.tensor_tensor(rview(*at), view(*at), rview(t, o, (WC, 4), (1, w)).bitcast(F32), ALU.subtract).then_inc(sm("w_lo"), 1)

        def tokens_hi(u, kt, a=0, n=512):
            t, o = (BIG, NT * D) if u == 1 else (SC, 8192)
            return rview(t, o + kt * 512 + a, (1, n))

        def three_products(dst, lhs, rhs, w_lo_wait, pe, between=None):
            out = []
            for kt in range(KT):
                if kt == KT - 2 and between:
                    between()
                if w_lo_wait is not None and kt % 4 == 0:
                    pe.wait_ge(sm("w_lo"), w_lo_wait + kt // 4)
                (lh, ll), (rh, rl) = lhs(kt), rhs(kt)
                nc.tensor.matmul(dst, lh, rh, start=kt == 0, stop=False)
                nc.tensor.matmul(dst, lh, rl, start=False, stop=False)
                out.append(nc.tensor.matmul(dst, ll, rh, start=False, stop=kt == KT - 1))
            return out

        OUTS = [list(range(NT)), [2, 3]]

        ATT = [[(i, j, half) for i in OUTS[l] for j in range(4) for half in range(2)] for l in range(DEPTH)]
        N_ATT = [len(a) for a in ATT]
        N_TO = [len(o) for o in OUTS]
        X_READY = [0, 4, 8, 10]

        def chunk_of(d, k):
            return k if d == 0 else (3 - k if k < 4 else 11 - k)

        SF = NT * N_FF

        SCT = 12800
        ADAR = 1024
        ADAL = 8192

        def ada_after(k):
            c = (k - 4) // 2
            return c if k % 2 == 0 and 0 <= c < N_ADA else None

        DIAG = [(BIG, NT * NIN - 1024), (SC, 11264)]
        V1, ROWI, ROWF, ROWT, ROWB, ROWA, ROWM = 0, 1040, 1552, 2064, 2576, 3088, 3600
        MQT, MKT, ACOL, MD, MT, ROT = 4112, 5136, 6160, 6672, 10768, 11024
        AQT, AP_, APT = 0, 3072, 6672
        GQT, GKF, GRT, GLG, GTMP, GB_, GEB, GNB, GKD, GKT = 0, 512, 1024, 2048, 3072, 4096, 5120, 6144, 7168, 8192
        GKV, GS, GEL, GAT = 9216, 9216, 13056, 2048
        NG, NX, NSQ = 0, 1024, 2048
        FE, FH, FHT, FT = 0, 512, 1024, 1536
        SEL, CWA, YE, XGS, CWS, XGL, SELW = 2048, 4096, 6144, 7168, 8192, 8448, 10240
        XGA = 2 * D
        SELS = [(SC, SEL), (BIG, XGA + D)]

        def in_pairs(eng, first, second, inner=None, swap=False):
            def step(k, kk):
                if swap:
                    second(k, kk)
                first(k + 1, kk + 1)
                if not swap:
                    second(k, kk)

            first(0, 0)
            for k in range(2 * NT):
                step(k, k)
            with eng.Fori(1, N_FF // 2) as it:
                if inner:
                    inner(it)
                for j in range(2 * NT):
                    step(j, it * 2 * NT + j)
            k0 = (N_FF - 1) * NT
            for k in range(k0, k0 + NT - 1):
                step(k, k)
            second(k0 + NT - 1, k0 + NT - 1)

        def one_expert(eng, k0, e, first, step, last, inner=None):
            kk = e * N_EX + k0
            first(k0, kk)
            step(k0, kk)
            with eng.Fori(0, N_EX // 2 - 2) as it:
                if inner:
                    inner(it)
                for j in range(1, 3):
                    step(k0 + j, kk + it * 2 + j)
            if inner:
                inner(None)
            for i in (N_EX - 3, N_EX - 2):
                step(k0 + i, kk + i)
            last(k0 + N_EX - 1, kk + (N_EX - 1))

        def over_experts(eng, blk, body):
            if not blk:
                with eng.Fori(0, NE - 1) as e:
                    body(e, e, True)
                body(NE - 1, NE - 1, False)
                return
            with eng.Fori(0, NE) as e:
                has = eng.value_load(RI[0:1, bass.ds(e + 1, 1)], min_val=0, max_val=1)
                rank = eng.value_load(RI[0:1, bass.ds(e + 9, 1)], min_val=0, max_val=NE - 1)
                with eng.If(has > 0):
                    body(e, rank, False)

        def exp_gate(act, A, k, kk):
            b = k % 2
            act.wait_ge(sm("f_up"), kk + 1)
            if not (isinstance(kk, int) and kk < 2):
                act.wait_ge(sm("f_h"), kk - 1)
            A(view(SC, FE + b * FC, (1, FC)), bank[4 + b][:, 0:FC], ACT.Exp, scale=-1.0).then_inc(sm("f_exp"), 1)

        def copy_hT(act, A, k, kk):
            b = k % 2
            act.wait_ge(sm("f_tr"), kk + 1)
            A(view(SC, FHT + b * FC, (1, FC)), bank[6 + b][:, 0:FC], ACT.Copy).then_inc(sm("f_hT"), 1)

        block = es.enter_context(nc.Block())

        @block.sync
        def _(sp):
            def by_rows(n, it, w, col, width=WC):
                v = w.rearrange("(k p) n -> p k n", p=P)
                s = g_slot(n)
                if n >= 2 or it is not None:
                    sp.wait_ge(g_free[s], n // 2 + (0 if it is None else it))
                for q in range(4):
                    sp.dma_start(view(GW, (s * KT + 2 * q) * WC, (WC, 2), (1, width)),
                                 v[:, 2 * q:2 * q + 2, bass.ds(col, width)]).then_inc(g_loaded[2 * s + q // 2], 16)

            def gate_up(n, it, w, hidden, row, col):
                s = g_slot(n)
                if not (it is None and n < 2):
                    sp.wait_ge(g_free[s], n // 2 + (0 if it is None else it))
                for h in range(2):
                    v = w[bass.ds(row + 512 * h, 512), :].rearrange("(k p) n -> p k n", p=P)
                    for c in range(2):
                        sp.dma_start(view(GW, (s * KT + 4 * h) * WC + FC * c, (WC, 4), (1, FC)),
                                     v[:, :, bass.ds(col + c * hidden, FC)]).then_inc(g_loaded[2 * s + h], 16)

            def down(m, units, w, row):
                s = m % 2
                if units is not None:
                    sp.wait_ge(sm("f_down"), units)
                src = w[bass.ds(row, FC), :].rearrange("(k p) n -> p k n", p=P)
                sp.dma_start(view(DW, s * 2 * D, (D, 2), (1, D)), src).then_inc(d_loaded[s], 16)

            for j in range(2):
                by_rows(j, None, w_ada[0], j * WC)
            with sp.Fori(1, N_ADA // 2) as it:
                for j in range(2):
                    by_rows(j, it, w_ada[0], it * 2 * WC + j * WC)
            for l in range(DEPTH):
                for i in range(N_IN):
                    by_rows(base["in", l] + i, None, w_in[l], i * WC, min(WC, NIN - i * WC))
                if l == 0:
                    with sp.Fori(0, N_ADA // 2) as it:
                        for j in range(2):
                            by_rows(base["ada", 1] + j, it, w_ada[1], it * 2 * WC + j * WC)
                for i in range(N_OUT):
                    by_rows(base["out", l] + i, None, w_out[l], i * WC)
                if l == 0:
                    for j in range(2):
                        gate_up(base["ff", 0] + j, None, ffn_w_gu[0], D_FF, 0, j * FC)
                        down(j, None, ffn_w_down[0], j * FC)
                    with sp.Fori(1, N_FF // 2) as it:
                        for j in range(2):
                            gate_up(base["ff", 0] + j, it, ffn_w_gu[0], D_FF, 0, it * 2 * FC + j * FC)
                            down(j, it * 2 * NT + (j - 1) * NT, ffn_w_down[0], it * 2 * FC + j * FC)
                    i = N_FF - 1
                    gate_up(base["ff", 0] + i, None, ffn_w_gu[0], D_FF, 0, i * FC)
                    down(i, (i - 1) * NT, ffn_w_down[0], i * FC)

            def experts(blk):
                n0, m0 = base["ff", 1] + blk * NE * N_EX, N_FF + blk * NE * N_EX
                gu = moe_w_gu[0].rearrange("e d n -> (e d) n")
                dn = moe_w_down[0].rearrange("e f n -> (e f) n")
                def body(e, r, more):
                    k0 = SF + blk * NE * N_EX
                    def gate(i, it=None):
                        at = r * (N_EX // 2) if it is None else r * (N_EX // 2) + it
                        col = i * FC if it is None else it * 2 * FC + i * FC
                        if isinstance(i, int) and i == N_EX:
                            gate_up(n0 + i, at, gu, D_EX, e * D + D, 0)
                            return
                        gate_up(n0 + i, at, gu, D_EX, e * D, col)

                    def dwn(i, it=None):
                        at = r * N_EX if it is None else r * N_EX + it * 2
                        row = e * D_EX + i * FC if it is None else e * D_EX + it * 2 * FC + i * FC
                        down(m0 + i, at + (k0 + i - 1), dn, row)

                    if blk:
                        gate(0)
                    with sp.Fori(0, N_EX // 2 - 1) as it:
                        for i in range(2):
                            gate(i + 1, it)
                            dwn(i, it)
                    gate(N_EX - 1)
                    dwn(N_EX - 2)
                    if more:
                        gate(N_EX)
                    dwn(N_EX - 1)

                if not blk:
                    gate_up(n0, 0, gu, D_EX, 0, 0)
                over_experts(sp, blk, body)

            experts(0)
            sp.wait_ge(sm("overflow_known"), 1)
            over = sp.value_load(RI[0:1, 0:1], min_val=0, max_val=1)
            with sp.If(over > 0):
                experts(1)
            for t in range(2):
                sp.wait_ge(sm("x_final"), t + 1)
                sp.dma_start(out[0, t * P:(t + 1) * P, :], xt(2 + t)).then_inc(sm("stored"), 16)
            sp.wait_ge(sm("stored"), 32)

        @block.gpsimd
        def _(pool):
            step = Steps(pool, pool_step)
            for l in range(DEPTH):
                if l == 0:
                    step(nc.gpsimd.memset(view(SC, SCT, (1, KT * 32)), 0.0))
                    nc.gpsimd.memset(view(PRM, pos["ib"], (1, 4)), 0.0).then_inc(sm("cleared"), 1)
                pool.wait_ge(sm("p_act"), 12 * (l + 1))
                pool.wait_ge(sm("p_dve"), 12 * (l + 1))
                nc.gpsimd.memset(view(SC, V1 + 64, (65, 16), (1, 1)), 1.0).then_inc(sm("v1"), 1)
                for t in range(NT):
                    ins = nc.gpsimd.tensor_copy(view(SC, V1 + t * 260, (65, 4), (1, 64)),
                                                view(BIG, t * NIN + C_MV, (64, 4), (1, 64)))
                    ins.then_inc(sm("v1"), 1)

        @block.scalar
        def _(act):
            step = Steps(act, act_step)
            A = nc.scalar.activation

            def load(dst, src):
                act.dma_start(dst, src).then_inc(params, 16)

            for t in range(NT):
                src = (ctx_in if t < 2 else x)[0, (t % 2) * P:(t % 2 + 1) * P, :]
                act.dma_start(xt(t), src).then_inc(sm("x_loaded"), 16)
            load(CS[:, :], consts)
            load(view(SC, 0, (1, P), np_=8), c_ctx.rearrange("(k p) -> k p", p=P))
            load(view(SC, 0, (1, P), p0=8, np_=8), c.rearrange("o (k p) -> (o k) p", p=P))
            load(view(SC, P, (1, P), np_=96), b_ada.rearrange("l (j p) -> (l j) p", p=P))
            load(view(SC, 2 * P, (1, P), np_=4), gla_gate_b.rearrange("l d k -> (l d) k"))
            load(prm("gup", (P, 4), (1, P), np_=RANK), gla_gate_up.rearrange("l d r k -> r (l d) k"))
            load(prm("sink", (1, 16)), attn_sink.rearrange("l h -> (l h)").partition_broadcast(P))
            load(prm("rb", (1, 8)), router_b[0].partition_broadcast(P))
            load(prm("rw", (8, 8), (1, 8)), router_w[0].rearrange("(k p) e -> p k e", p=P))
            for l in range(DEPTH):
                load(view(NW, l * 512, (1, 256)), mlstm_norm_w[l].partition_broadcast(P))
                load(view(NW, l * 512 + 256, (1, 256)), gla_norm_w[l].partition_broadcast(P))
            act.wait_ge(sm("cleared"), 1)
            with nc.allow_non_contiguous_dma(reason="gate biases, a few bytes"):
                for l in range(DEPTH):
                    for g in range(2):
                        for d in range(2):
                            load(prm("ib", (1, 1), off=2 * l + g, p0=32 * d, np_=4),
                                 mlstm_gate_b[l, d, g].rearrange("(h o) -> h o", o=1))

            def ln_rows(i):
                l, j = divmod(i, 2)
                if i:
                    act.wait_ge(sm("ln_used"), i)
                act.dma_start(view(LNR, 0, (1, D)), ln_w[l, j].partition_broadcast(P)).then_inc(sm("ln_rows"), 16)
                act.dma_start(view(LNR, D, (1, D)), ln_b[l, j].partition_broadcast(P)).then_inc(sm("ln_rows"), 16)

            ln_rows(0)
            act.wait_ge(sm("c_col"), 1)
            A(prm("ecol", (1, 16)), prm("ccol", (1, 16)), ACT.Exp, scale=-1.0).then_inc(sm("c_exp"), 1)
            with act.Fori(0, N_ADA // 2) as it:
                    for j in range(2):
                        act.wait_ge(sm("ada_mm"), it * 2 + (j + 1))
                        A(view(SC, ADAR + j * 512, (1, 512)), bank[j][:, :], ACT.Copy).then_inc(sm("ada_row"), 1)

            def gate_rows(i):
                for s in range(2):
                    for half in range(2):
                        k = i * 4 + s * 2 + half
                        act.wait_ge(sm("gate_mm"), k + 1)
                        A(view(GATE, s * D + half * 512, (1, 512)), bank[6 + half][:, :], ACT.Copy).then_inc(sm("gate_row"), 1)

            def h_context(u, l, six):
                for kt in range(KT):
                    act.wait_ge(sm("x_T"), u * KT + kt + 1)
                    A(view(HT, kt * 512, (1, 256)), bank[kt % 2][:, 0:256], ACT.Identity,
                      scale=mod(l, six + 1, kt, 0), bias=mod(l, six, kt, 0)).then_inc(sm("h_ctx"), 1)
                    act.wait_ge(sm("h_ctx"), u * KT + kt + 1)
                    act.wait_ge(sm("h_lat"), u * KT + kt + 1)
                    A(tokens_hi(u, kt), view(HT, kt * 512, (1, 512)), ACT.Copy).then_inc(sm("h_hi"), 1)

            def slots_context(blk):
                for b in range(4):
                    act.wait_ge(sm("sw_T"), 4 * blk + b + 1)
                    A(view(SC, CWA + b * 512, (1, 512)), bank[b][:, :], ACT.Copy).then_inc(sm("sw_copy"), 1)
                if blk:
                    return
                with act.Fori(0, NE // 2) as it:
                    for j in range(2):
                        gathered(it * 2048, j, it * 2 + (j + 1))

            def gathered(moved, j, n):
                act.wait_ge(sm("gx_mm"), n)
                for q in range(4):
                    ins = A(BIG[:, bass.ds(moved + (XGA + j * 1024 + q * P), P)], bank[4 + 2 * j][:, q * P:(q + 1) * P],
                            ACT.Identity, scale=mod(1, 4, q, 1), bias=mod(1, 3, q, 1))
                ins.then_inc(sm("gx_a"), 1)

            def experts(blk):
                slots_context(blk)
                k0 = SF + blk * NE * N_EX
                n0 = base["ff", 1] + blk * NE * N_EX

                def tokens(e):
                    A(rview(SC, XGS, (1, D)), BIG[:, bass.ds(e * D + XGA, D)], ACT.Copy).then_inc(sm("x_hi"), 1)

                def two_chunks(moved):
                    for i in range(2):
                        for half in range(2):
                            write_hi(act, "ex", n0 + i, moved, half)

                def body(e, r, more):
                    st = {"moved": r * (N_EX // 2)}
                    if blk:
                        gathered(0, 0, r + (NE + 1))
                        act.wait_ge(sm("gx_a"), r + (NE + 1))
                        act.wait_ge(sm("gx_d"), r + (NE + 1))
                        tokens(0)
                        two_chunks(st["moved"])

                    def high(k, half):
                        if more or k - k0 + 2 < N_EX:
                            write_hi(act, "ex", n0 + k - k0 + 2, st["moved"], half)

                    def step(k, kk):
                        if k != k0:
                            high(k, 0)
                        copy_hT(act, A, k, kk)
                        exp_gate(act, A, k + 1, kk + 1)
                        if k == k0:
                            high(k, 0)
                        high(k, 1)

                    def last(k, kk):
                        if more:
                            tokens(e + 1)
                        copy_hT(act, A, k, kk)
                        act.wait_ge(sm("f_down"), r * N_EX + (k0 + N_EX))
                        for half in range(2):
                            A(view(SC, YE + half * 512, (1, 512)), bank[half][:, :], ACT.Copy).then_inc(sm("ye"), 1)
                        high(k, 0)
                        high(k, 1)

                    def inner(it):
                        st["moved"] = r * (N_EX // 2) if it is None else r * (N_EX // 2) + it

                    one_expert(act, k0, r, lambda k, kk: exp_gate(act, A, k, kk), step, last, inner)

                if not blk:
                    act.wait_ge(sm("gx_a"), NE)
                    act.wait_ge(sm("gx_d"), NE)
                    tokens(0)
                    two_chunks(0)
                over_experts(act, blk, body)

            def rstd(name, src, dst, n, scale):
                step(A(dst, src, ACT.Ln, scale=scale, bias=view(ST, 500, (1, 1))))
                A(dst, dst, ACT.Exp, scale=-0.5).then_inc(sm(name), 1)

            for l in range(DEPTH):
                nto = N_TO[l]
                t0 = OUTS[l][0]
                gate_rows(2 * l)
                h_context(2 * l, l, 0)
                for chunk in range(2):
                    for half in range(2):
                        write_hi(act, "in", base["in", l] + chunk, None, half)
                for g in range(0, N_IN * NT, 2):
                    cchunk, t = divmod(g, NT)
                    w = min(WC, NIN - cchunk * WC)
                    act.wait_ge(sm("p_mm"), l * N_IN * NT + g + 1)
                    A(big(t, cchunk * WC, w), bank[4 + g % 4][:, 0:w], ACT.Copy).then_inc(sm("p_act"), 1)
                    if t == 0 and 1 <= cchunk < N_IN - 1:
                        for half in range(2):
                            write_hi(act, "in", base["in", l] + cchunk + 1, None, half, min(WC, NIN - (cchunk + 1) * WC))
                for g in range(2):
                    act.wait_ge(sm("m_T"), l * 6 + g + 1)
                    A(view(SC, ROWI + g * 512, (1, 512), np_=64), bank[g][0:64, :], ACT.Identity,
                      bias=prm("ib", (1, 1), off=2 * l + g, np_=64)).then_inc(sm("gates"), 1)
                for g in range(2):
                    act.wait_ge(sm("m_T"), l * 6 + g + 3)
                    A(view(SC, MQT + g * 512, (1, 512)), bank[2 + g][:, :], ACT.Copy).then_inc(sm("mq_T"), 1)
                act.wait_ge(sm("f_abs"), l + 1)
                r = view(SC, ROWT, (1, 512), np_=64)
                step(A(r, r, ACT.Exp))
                A(r, r, ACT.Ln, bias=1.0).then_inc(sm("f_ln"), 1)
                act.wait_ge(sm("gate_rows_ready"), l + 1)
                A(r, r, ACT.Exp).then_inc(sm("floor_row"), 1)
                act.wait_ge(sm("gates_T"), l + 1)
                step(A(view(SC, ACOL, (1, 256)), bank[0][:, 0:256], ACT.Copy, scale=-1.0))
                A(view(SC, ACOL + 256, (1, 256)), bank[0][:, 256:512], ACT.Copy).then_inc(sm("gate_cols"), 1)
                for u in range(8):
                    h, d = divmod(u, 2)
                    act.wait_ge(sm("m_bc"), 8 * l + u + 1)
                    if 8 * l + u >= 2:
                        act.wait_ge(sm("m_pv"), 8 * l + u - 1)
                    for j in range(4):
                        a, n = (0, 512) if j < 2 else (256, 256)
                        step(A(view(SC, MD + d * 2048 + j * 512 + a, (1, n)), bank[4 + d][:, a:a + n], ACT.Relu,
                               bias=view(SC, ACOL + j * 64 + d * 32 + h, (1, 1))))
                    v = view(SC, MD + d * 2048, (1, 1024))
                    step(A(v, v, ACT.Exp, scale=-1.0))
                    v = view(SC, MD + d * 2048 + 1280, (512, 2), (1, 256))
                    A(v, v, ACT.Exp, scale=-1.0).then_inc(sm("m_decay"), 1)
                for j in range(6):
                    act.wait_ge(sm("a_T"), l * 6 + j + 1)
                    a = 256 if (j < 4 and l == DEPTH - 1) else 0
                    A(view(HT, AQT + j * 512 + a, (1, 512 - a)), bank[j][:, a:512], ACT.Copy,
                      scale=0.125 if j < 4 else 1.0).then_inc(sm("a_qk"), 1)
                off = sum(N_ATT[:l])
                for k in range(N_ATT[l] + 1):
                    if k < N_ATT[l]:
                        i, j, half = ATT[l][k]
                        n = 256 if i < 2 else 512
                        b = k % 2
                        act.wait_ge(sm("a_max"), off + k + 1)
                        if k >= 2:
                            act.wait_ge(sm("a_pT"), off + k - 1)
                            act.wait_ge(sm("a_out"), off + k - 1)
                        A(view(HT, AP_ + b * 512, (1, n)), bank[b][:, 0:n], ACT.Exp, bias=view(ST, 100 + b, (1, 1)),
                          accum_out=view(ST, 102 + b, (1, 1))).then_inc(sm("a_exp"), 1)
                        A(view(ST, 104 + b, (1, 1)), prm("sink", (1, 1), off=l * 8 + 2 * j + half), ACT.Exp,
                          bias=view(ST, 100 + b, (1, 1))).then_inc(sm("a_exp"), 1)
                    if k >= 1:
                        k1 = k - 1
                        n = 256 if ATT[l][k1][0] < 2 else 512
                        act.wait_ge(sm("a_pT"), off + k1 + 1)
                        if k1 >= 2:
                            act.wait_ge(sm("a_pv"), off + k1 - 1)
                        A(view(SC, APT + (k1 % 2) * 512, (1, n)), bank[2 + k1 % 2][:, 0:n], ACT.Copy).then_inc(sm("a_pTs"), 1)
                    if l == 0 and ada_after(k - 1) is not None:
                        act.wait_ge(sm("ada_mm"), N_ADA + ada_after(k - 1) + 1)
                        A(view(SC, ADAL, (1, 512)), bank[6][:, :], ACT.Copy).then_inc(sm("ada_row"), 1)
                for g in range(2):
                    act.wait_ge(sm("g_T"), l * 4 + g + 1)
                    A(view(SC, GQT + g * 512, (1, 512)), bank[g][:, :], ACT.Copy,
                      scale=float(np.float32(DK ** -0.5)) if g == 0 else 1.0).then_inc(sm("g_qk"), 1)
                for d in range(2):
                    act.wait_ge(sm("g_z"), 2 * l + d + 1)
                    A(view(SC, GLG + d * 512, (1, 512)), bank[4 + d][:, :], ACT.Identity,
                      bias=prm("gb", (1, 1), off=2 * l + d)).then_inc(sm("g_zb"), 1)
                act.wait_ge(sm("g_abs"), l + 1)
                r = view(SC, GTMP, (1, 1024))
                step(A(r, r, ACT.Exp))
                A(r, r, ACT.Ln, bias=1.0).then_inc(sm("g_ln"), 1)
                act.wait_ge(sm("g_cum"), l + 1)
                A(view(SC, GEB, (1, 1024)), view(SC, GB_, (1, 1024)), ACT.Exp, scale=1 / 16).then_inc(sm("g_eb"), 1)
                A(view(SC, GNB, (1, 1024)), view(SC, GB_, (1, 1024)), ACT.Exp, scale=-1 / 16).then_inc(sm("g_eb"), 1)
                act.wait_ge(sm("g_rest"), l + 1)
                A(view(SC, GKD, (1, 1024)), view(SC, GKD, (1, 1024)), ACT.Exp, scale=1 / 16).then_inc(sm("g_eb"), 1)
                for d in range(2):
                    act.wait_ge(sm("g_kT"), 2 * l + d + 1)
                    A(view(SC, GKT + d * 512, (1, 512)), bank[6 + d][:, :], ACT.Copy).then_inc(sm("g_ktok"), 1)
                for d in range(2):
                    act.wait_ge(sm("g_a"), 2 * l + d + 1)
                    if d == 1:
                        act.wait_ge(sm("g_pv"), 2 * l + 1)
                    for h in range(4):
                        ins = A(view(SC, GAT + h * 512, (1, 512)), bank[4 + h][:, :], ACT.Copy)
                    ins.then_inc(sm("g_acopy"), 1)
                for g in range(2):
                    act.wait_ge(sm("n_gate_free"), 2 * l + g + 1)
                    A(view(SC, NG, (256, nto), (1, 256)), bigs(t0, nto, (C_MO, C_GG)[g], (1, 256)), ACT.Exp,
                      scale=-1.0).then_inc(sm("n_gate"), 1)
                    act.wait_ge(sm("n_var"), 2 * l + g + 1)
                    rstd("n_rstd", view(ST, 32, (1, 4 * nto)), view(ST, 48, (1, 4 * nto)), 16, 1 / HD)
                for kt in range(0, KT, 2):
                    act.wait_ge(sm("c_T"), l * KT + kt + 1)
                    A(view(HT, kt * 512 + t0 * P, (1, nto * P)), bank[kt % 4][:, t0 * P:512], ACT.Copy).then_inc(sm("c_act"), 1)
                act.wait_ge(sm("r_var"), 2 * l + 1)
                rstd("r_rstd", view(ST, 64 + 1, (2, nto)), view(ST, 80, (1, nto)), nto, 1.0)
                ln_rows(2 * l + 1)
                gate_rows(2 * l + 1)
                if l == 0:
                    h_context(1, 0, 3)
                    state = {"it": None}
                    for half in range(2):
                        write_hi(act, "ff", base["ff", 0], None, half)

                    def exp(k, kk):
                        exp_gate(act, A, k, kk)
                        if k % NT == 2 and k < (N_FF - 1) * NT:
                            for half in range(2):
                                write_hi(act, "ff", base["ff", 0] + k // NT + 1, None if isinstance(kk, int) else state["it"], half)

                    def hT(k, kk):
                        copy_hT(act, A, k, kk)

                    in_pairs(act, exp, hT, lambda it: state.update(it=it), swap=True)
                else:
                    act.wait_ge(sm("r_diff"), 1)
                    A(view(ST, 136, (1, 2)), view(ST, 136, (1, 2)), ACT.Exp).then_inc(sm("r_exp"), 1)
                    experts(0)
                    act.wait_ge(sm("overflow_known"), 1)
                    over = act.value_load(RI[0:1, 0:1], min_val=0, max_val=1)
                    with act.If(over > 0):
                        experts(1)
                act.wait_ge(sm("r_var"), 2 * l + 2)
                rstd("r_rstd", view(ST, 64 + 1, (2, nto)), view(ST, 80, (1, nto)), nto, 1.0)
                if l == 0:
                    ln_rows(2)

        @block.vector
        def _(dve):
            V = nc.vector
            step = Steps(dve, dve_step)

            def signal(ins, name, total):
                ins.then_inc(sm(name), 1)
                dve.wait_ge(sm(name), total)

            step(V.memset(view(ST, 500, (1, 1)), EPS))
            dve.wait_ge(sm("start_T"), 1)
            dve.wait_ge(sm("cleared"), 1)
            step(V.tensor_copy(prm("ccol", (1, 16)), bank[0][:, 0:16]))
            for s in range(2):
                step(V.tensor_copy(prm("bada", (2, 96), off=s), bank[0][:, 16:112]))
            V.tensor_copy(prm("gb", (1, 4)), bank[0][:, 112:116]).then_inc(sm("c_col"), 1)
            dve.wait_ge(sm("c_exp"), 1)
            e = prm("ecol", (1, 16))
            step(V.tensor_scalar(e, e, 1.0, None, ALU.add))
            step(V.reciprocal(e, e))
            V.tensor_tensor(view(SC, SCT, (1, 2), (32, KT)), prm("ccol", (8, 2), (1, 8)), prm("ecol", (8, 2), (1, 8)),
                            ALU.mult).then_inc(sm("sct"), 1)
            with dve.Fori(0, N_ADA // 2) as it:
                for j in range(2):
                    dve.wait_ge(sm("ada_col"), it * 2 + (j + 1))
                    o = it * 16 + j * 8
                    V.tensor_tensor(MOD[:, bass.ds(o, 8)], bank[2 + j][:, 0:8],
                                    PRM[:, bass.ds(o + pos["bada"], 8)], ALU.add).then_inc(sm("mod"), 1)

            def scales(l):
                dve.wait_ge(sm("mod"), (l + 1) * N_ADA)
                v = view(MOD, l * 96 + 16, (48, 2), (1, 16))
                signal(V.tensor_scalar(v, v, 1.0, None, ALU.add), "mods", l + 1)

            scales(0)

            def diagonals(i):
                l, j = divmod(i, 2)
                for s in range(2):
                    for half in range(2):
                        k = i * 4 + s * 2 + half
                        if k >= 2:
                            dve.wait_ge(sm("gate_mm"), k - 1)
                        for q in range(4):
                            ins = V.tensor_scalar(view(DIAG[j][0], DIAG[j][1] + half * 512 + q * P, (1, P)), ident,
                                                  mod(l, 3 * j + 2, half * 4 + q, s), None, ALU.mult)
                        ins.then_inc(sm("diag"), 1)

            def h_latent(u, l, six, split):
                def low(kt):
                    dve.wait_ge(sm("h_hi"), u * KT + kt + 1)
                    at = (HT, kt * 512, (1, 512))
                    V.tensor_tensor(rview(*at), view(*at), tokens_hi(u, kt).bitcast(F32), ALU.subtract).then_inc(sm("h_lo"), 1)

                for kt in range(KT):
                    dve.wait_ge(sm("x_T"), u * KT + kt + 1)
                    V.tensor_scalar(view(HT, kt * 512 + 256, (1, 256)), bank[2 + kt % 2][:, 256:512],
                                    mod(l, six + 1, kt, 1), mod(l, six, kt, 1), ALU.mult, ALU.add).then_inc(sm("h_lat"), 1)
                    if split and kt:
                        low(kt - 1)
                if split:
                    low(KT - 1)

            def layer_norm(i, from_psum):
                l = i // 2
                outs = OUTS[l]
                dve.wait_ge(sm("gate_row"), 4 * (i + 1))
                dve.wait_ge(sm("ln_rows"), 32 * (i + 1))
                for n, t in enumerate(outs):
                    g = view(GATE, (t // 2) * D, (1, D))
                    if from_psum:
                        for cc in range(2):
                            dve.wait_ge(sm("o_mm"), sum(2 * m for m in N_TO[:l]) + cc * len(outs) + n + 1)
                            step(V.tensor_tensor(ysum(n, cc * 512, 512), bank[t * 2 + cc][:, :],
                                                 view(GATE, (t // 2) * D + cc * 512, (1, 512)), ALU.mult))
                    else:
                        step(V.tensor_tensor(ysum(n), ysum(n), g, ALU.mult))
                    step(V.scalar_tensor_tensor(ysum(n), xt(t), ALPHA, ysum(n), ALU.mult, ALU.add))
                    for cc in range(2):
                        step(V.bn_stats(view(ST, 240 + 6 * cc, (1, 6)), ysum(n, cc * 512, 512)))
                    step(V.bn_aggr(view(ST, 64 + 2 * n, (1, 2)), view(ST, 240, (1, 12))))
                V.memset(view(ST, 501, (1, 1)), 0.0).then_inc(sm("r_var"), 1)
                dve.wait_ge(sm("r_rstd"), i + 1)
                for n, t in enumerate(outs):
                    step(V.tensor_scalar(ysum(n), ysum(n), view(ST, 64 + 2 * n, (1, 1)), view(ST, 80 + n, (1, 1)),
                                         ALU.subtract, ALU.mult))
                    step(V.tensor_tensor(ysum(n), ysum(n), view(LNR, 0, (1, D)), ALU.mult))
                    ins = V.tensor_tensor(xt(t), ysum(n), view(LNR, D, (1, D)), ALU.add)
                    if i == 3:
                        signal(ins, "x_final", n + 1)
                    else:
                        signal(ins, "x_ready", X_READY[i] + n + 1)
                V.memset(view(ST, 501, (1, 1)), 0.0).then_inc(sm("ln_used"), 1)

            def scans(dst, off_src, op0, op1, cumulate):
                def go(p0, o, n, initial):
                    s = 1 if p0 == 0 else -1
                    src = view(SC, off_src + o, (s, n), p0=p0, np_=32)
                    first = view(CS, C_AT["ones"][0], (0, n), p0=p0, np_=32) if cumulate else src
                    step(V.tensor_tensor_scan(view(SC, dst + o, (s, n), p0=p0, np_=32), first, src, initial, op0, op1))
                go(0, 0, 512, 0.0)
                go(32, 255, 256, 0.0)
                go(32, 511, 256, view(SC, dst, (1, 1), p0=32, np_=32))

            def mask(name, k):
                o, w = C_AT[name]
                v = view(CS, o, (0, k), (1, P))
                return v.bitcast(U32)

            def zeros(k):
                return view(CS, C_AT["zeros"][0], (0, k), (0, P))

            for l in range(DEPTH):
                outs = OUTS[l]
                nto = len(outs)
                t0 = outs[0]
                last = l == DEPTH - 1
                diagonals(2 * l)
                h_latent(2 * l, l, 0, True)
                for c in range(2):
                    for half in range(2):
                        write_lo(dve, "in", base["in", l] + c, split_base["in", l] + c, None, half)
                for g in range(1, N_IN * NT, 2):
                    cchunk, t = divmod(g, NT)
                    w = min(WC, NIN - cchunk * WC)
                    dve.wait_ge(sm("p_mm"), l * N_IN * NT + g + 1)
                    V.tensor_copy(big(t, cchunk * WC, w), bank[4 + g % 4][:, 0:w]).then_inc(sm("p_dve"), 1)
                    if t == 1 and 1 <= cchunk < N_IN - 1:
                        c = cchunk + 1
                        for half in range(2):
                            write_lo(dve, "in", base["in", l] + c, split_base["in", l] + c, None, half, min(WC, NIN - c * WC))
                dve.wait_ge(sm("gates"), 2 * l + 2)
                rf, rt = (view(SC, o, (1, 512), np_=64) for o in (ROWF, ROWT))
                V.scalar_tensor_tensor(rt, rf, -1.0, rf, ALU.mult, ALU.min).then_inc(sm("f_abs"), 1)
                for g in range(2):
                    dve.wait_ge(sm("m_T"), l * 6 + 5 + g)
                    V.tensor_scalar(view(SC, MKT + g * 512, (1, 512)), bank[4 + g][:, :], HD ** -0.5, None,
                                    ALU.mult).then_inc(sm("mk_T"), 1)
                dve.wait_ge(sm("p_act"), 12 * (l + 1))
                dve.wait_ge(sm("p_dve"), 12 * (l + 1))
                for t in (2, 3):
                    for jj in range(2):
                        step(V.tensor_tensor(view(SC, ROT + jj * 16, (64, 10), (32, 2), (1, 16)),
                                             view(BIG, t * NIN + C_AQ + (1 - jj) * 16, (64, 10), (32, 2), (1, 16)),
                                             view(CS, C_AT["sin"][0] + (t - 2) * 64 + jj * 16, (0, 10), (32, 2), (1, 16)),
                                             ALU.mult))
                    v = view(BIG, t * NIN + C_AQ, (64, 10), (1, 64))
                    step(V.tensor_tensor(v, v, view(CS, C_AT["cos"][0] + (t - 2) * 64, (0, 10), (1, 64)), ALU.mult))
                    v = view(BIG, t * NIN + C_AQ, (1, 640))
                    V.tensor_tensor(v, v, view(SC, ROT, (1, 640)), ALU.add).then_inc(sm("rope"), 1)
                    dve.wait_ge(sm("rope"), 2 * l + t - 1)
                dve.wait_ge(sm("f_ln"), l + 1)
                step(V.scalar_tensor_tensor(rf, rf, 0.0, rt, ALU.min, ALU.subtract))
                scans(ROWB, ROWF, ALU.mult, ALU.add, True)
                ra, rb_, rm, ri = (view(SC, o, (1, 512), np_=64) for o in (ROWA, ROWB, ROWM, ROWI))
                step(V.tensor_tensor(ra, ri, rb_, ALU.subtract))
                scans(ROWM, ROWA, ALU.max, ALU.max, False)
                V.scalar_tensor_tensor(rt, rb_, -1.0, rm, ALU.mult, ALU.subtract).then_inc(sm("gate_rows_ready"), 1)

                def weigh(u):
                    h, d = divmod(u, 2)
                    o = MD + d * 2048
                    dve.wait_ge(sm("m_decay"), 8 * l + u + 1)
                    step(V.copy_predicated(view(SC, o, (640, 4), (1, P)), mask(("not_fwd", "not_bwd")[d], 4), zeros(4)))
                    dve.wait_ge(sm("m_s"), 4 * l + h + 1)
                    for j in range(2):
                        v = view(SC, o + j * 512, (1, 512))
                        V.tensor_tensor(v, v, bank[1 + j][:, :], ALU.mult).then_inc(sm("m_w"), 1)
                    v = view(SC, o + 2 * 512 + 256, (512, 2), (1, 256))
                    V.tensor_tensor(v, v, bank[3][:, :].rearrange("p (a b) -> p a b", a=2), ALU.mult).then_inc(sm("m_w"), 1)

                def normalise(u):
                    h, d = divmod(u, 2)
                    dve.wait_ge(sm("m_pv"), 8 * l + u + 1)
                    pv = bank[6 + d][:, t0 * 65:260].rearrange("p (t c) -> p t c", c=65)
                    den = view(ST, 440, (1, nto))
                    dve.wait_ge(sm("gate_cols"), l + 1)
                    step(V.tensor_tensor(den, pv[:, :, 64], view(SC, ACOL + 256 + t0 * 64 + d * 32 + h, (64, nto)), ALU.max))
                    step(V.scalar_tensor_tensor(den, pv[:, :, 64], -1.0, den, ALU.mult, ALU.max))
                    step(V.reciprocal(den, den))
                    r = view(ST, 440, (1, nto), (0, 64))
                    dst = bigs(t0, nto, C_MQ + h * 64, (1, 64))
                    if d == 0:
                        signal(V.tensor_tensor(dst, pv[:, :, 0:64], r, ALU.mult), "m_hs", 8 * l + u + 1)
                    else:
                        tmp = view(SC, MT, (64, nto), (1, 64))
                        step(V.tensor_tensor(tmp, pv[:, :, 0:64], r, ALU.mult))
                        signal(V.tensor_tensor(dst, dst, tmp, ALU.add), "m_hs", 8 * l + u + 1)

                for u in range(9):
                    if u < 8:
                        weigh(u)
                    if u >= 1:
                        normalise(u - 1)
                off = sum(N_ATT[:l])
                for k in range(N_ATT[l] + 2):
                    if k < N_ATT[l]:
                        i, j, half = ATT[l][k]
                        b = k % 2
                        dve.wait_ge(sm("a_s"), off + k + 1)
                        step(V.tensor_reduce(view(ST, 106 + b, (1, 1)), bank[b][:, 0:256 if i < 2 else 512], AX, ALU.max))
                        V.tensor_scalar(view(ST, 100 + b, (1, 1)), view(ST, 106 + b, (1, 1)),
                                        prm("sink", (1, 1), off=l * 8 + 2 * j + half), -1.0, ALU.max,
                                        ALU.mult).then_inc(sm("a_max"), 1)
                    if k >= 2:
                        i, j, half = ATT[l][k - 2]
                        b = k % 2
                        dve.wait_ge(sm("a_pv"), off + k - 1)
                        den = view(ST, 108 + b, (1, 1))
                        V.tensor_scalar(big(i, C_AQ + (2 * j + half) * 64, 64), bank[4 + b][:, 0:64], den, None,
                                        ALU.mult).then_inc(sm("a_o"), 1)
                    if k >= 1 and k - 1 < N_ATT[l]:
                        b = (k - 1) % 2
                        dve.wait_ge(sm("a_exp"), 2 * (off + k))
                        den = view(ST, 108 + b, (1, 1))
                        step(V.tensor_tensor(den, view(ST, 102 + b, (1, 1)), view(ST, 104 + b, (1, 1)), ALU.add))
                        signal(V.reciprocal(den, den), "a_out", off + k)
                    if l == 0 and ada_after(k - 3) is not None:
                        c1 = ada_after(k - 3)
                        dve.wait_ge(sm("ada_col"), N_ADA + c1 + 1)
                        V.tensor_tensor(view(MOD, 96 + c1 * 8, (1, 8)), bank[7][:, 0:8], prm("bada", (1, 8), off=96 + c1 * 8),
                                        ALU.add).then_inc(sm("mod"), 1)
                if l == 0:
                    scales(1)
                for d in range(2):
                    dve.wait_ge(sm("g_T"), 4 * l + 3 + d)
                    V.tensor_copy(view(SC, GRT + d * 512, (1, 512), np_=16), bank[2 + d][0:16, :]).then_inc(sm("g_r"), 1)
                dve.wait_ge(sm("g_zb"), 2 * l + 2)
                lg, tmp = view(SC, GLG, (1, 1024)), view(SC, GTMP, (1, 1024))
                V.scalar_tensor_tensor(tmp, lg, -1.0, lg, ALU.mult, ALU.min).then_inc(sm("g_abs"), 1)
                dve.wait_ge(sm("g_ln"), l + 1)
                step(V.scalar_tensor_tensor(lg, lg, 0.0, tmp, ALU.min, ALU.subtract))
                reset = cst("reset")
                step(V.tensor_tensor_scan(view(SC, GB_, (1, 512)), reset, view(SC, GLG, (1, 512)), 0.0, ALU.mult, ALU.add))
                signal(V.tensor_tensor_scan(view(SC, GB_ + 1023, (-1, 512)), reset, view(SC, GLG + 1023, (-1, 512)), 0.0,
                                            ALU.mult, ALU.add), "g_cum", l + 1)
                for d in range(2):
                    last_b = view(SC, GB_ + (63 if d == 0 else 512), (64, 8), (0, 64))
                    step(V.tensor_tensor(view(SC, GKD + d * 512, (64, 8), (1, 64)), last_b,
                                         view(SC, GB_ + d * 512, (64, 8), (1, 64)), ALU.subtract))
                V.memset(view(ST, 501, (1, 1)), 0.0).then_inc(sm("g_rest"), 1)
                dve.wait_ge(sm("g_eb"), 3 * (l + 1))
                for d in range(2):
                    step(V.tensor_copy(view(SC, GEL + d * 8, (1, 8)), view(SC, GEB + (63 if d == 0 else 512), (64, 8))))
                dve.wait_ge(sm("g_qk"), 2 * (l + 1))
                for dst, src in ((GKD, GKF), (GNB, GKF), (GEB, GQT)):
                    v = view(SC, dst, (512, 2), (1, 512))
                    V.tensor_tensor(v, v, view(SC, src, (0, 2), (1, 512)), ALU.mult).then_inc(sm("g_prod"), 1)
                for q in range(14):
                    k, d = divmod(q, 2)
                    n = 14 * l + q + 1
                    dve.wait_ge(sm("g_kv"), n)
                    new = view(SC, GS + (d * 7 + k + 1) * 256, (1, 256))
                    if k == 0:
                        signal(V.tensor_tensor(new, bank[q % 4][:, 0:256], cst("blocks"), ALU.mult), "g_st", n)
                        continue
                    kv = view(SC, GKV, (1, 256))
                    step(V.tensor_tensor(kv, bank[q % 4][:, 0:256], cst("blocks"), ALU.mult))
                    signal(V.scalar_tensor_tensor(new, view(SC, GS + (d * 7 + k) * 256, (1, 256)),
                                                  view(SC, GEL + d * 8 + chunk_of(d, k), (1, 1)), kv, ALU.mult, ALU.add),
                           "g_st", n)
                for d in range(2):
                    dve.wait_ge(sm("g_acopy"), 2 * l + d + 1)
                    V.copy_predicated(view(SC, GAT, (P, 16), (1, P)), mask(("gnot_fwd", "gnot_bwd")[d], 16),
                                      zeros(16)).then_inc(sm("g_aok"), 1)
                dve.wait_ge(sm("g_pv"), 2 * l + 2)
                for i in outs:
                    step(V.tensor_copy(big(i, C_GQ, 256), bank[i][:, 0:256]))

                for g in range(2):
                    col = (C_MQ, C_GQ)[g]
                    V.memset(view(ST, 501, (1, 1)), 0.0).then_inc(sm("n_gate_free"), 1)
                    src = bigs(t0, nto, col, (1, 256)).rearrange("p t (h c) -> p (t h) c", h=4) if False else None
                    mean, ssq = view(ST, 16, (1, 4 * nto)), view(ST, 32, (1, 4 * nto))
                    for n, t in enumerate(outs):
                        step(V.tensor_reduce(view(ST, 16 + 4 * n, (1, 4)), view(BIG, t * NIN + col, (64, 4), (1, 64)), AX, ALU.add))
                    step(V.tensor_scalar(mean, mean, 1.0 / HD, None, ALU.mult))
                    for n, t in enumerate(outs):
                        step(V.tensor_tensor(view(SC, NX + n * 256, (64, 4), (1, 64)), view(BIG, t * NIN + col, (64, 4), (1, 64)),
                                             view(ST, 16 + 4 * n, (1, 4), (0, 64)), ALU.subtract))
                    xc, sq = view(SC, NX, (1, 256 * nto)), view(SC, NSQ, (1, 256 * nto))
                    step(V.tensor_tensor(sq, xc, xc, ALU.mult))
                    V.tensor_reduce(ssq, view(SC, NSQ, (64, 4 * nto), (1, 64)), AX, ALU.add).then_inc(sm("n_var"), 1)
                    dve.wait_ge(sm("n_gate"), 2 * l + g + 1)
                    gate = view(SC, NG, (1, 256 * nto))
                    step(V.tensor_scalar(gate, gate, 1.0, None, ALU.add))
                    step(V.reciprocal(gate, gate))
                    gate2 = view(SC, NG, (256, nto), (1, 256))
                    if g == 1:
                        step(V.tensor_tensor(gate2, gate2, bigs(t0, nto, C_GG, (1, 256)), ALU.mult))
                    dve.wait_ge(sm("n_rstd"), 2 * l + g + 1)
                    x3 = view(SC, NX, (64, 4 * nto), (1, 64))
                    step(V.tensor_tensor(x3, x3, view(ST, 48, (1, 4 * nto), (0, 64)), ALU.mult))
                    x2 = view(SC, NX, (256, nto), (1, 256))
                    step(V.tensor_tensor(x2, x2, view(NW, l * 512 + g * 256, (0, nto), (1, 256)), ALU.mult))
                    signal(V.tensor_tensor(bigs(t0, nto, col, (1, 256)), x2, gate2, ALU.mult), "cat", 2 * l + g + 1)
                for kt in range(1, KT, 2):
                    dve.wait_ge(sm("c_T"), l * KT + kt + 1)
                    V.tensor_copy(view(HT, kt * 512 + t0 * P, (1, nto * P)), bank[kt % 4][:, t0 * P:512]).then_inc(sm("c_dve"), 1)
                layer_norm(2 * l, True)
                diagonals(2 * l + 1)
                h_latent(2 * l + 1, l, 3, not last)

                def hidden(st, k, kk):
                    b = k % 2
                    e, tmp = view(SC, FE + b * FC, (1, FC)), view(SC, FT + b * FC, (1, FC))
                    dve.wait_ge(sm("f_exp"), kk + 1)
                    st(V.tensor_scalar(e, e, 1.0, None, ALU.add))
                    st(V.reciprocal(e, e))
                    st(V.tensor_tensor(tmp, bank[4 + b][:, 0:FC], e, ALU.mult))
                    if not (isinstance(kk, int) and kk < 2):
                        dve.wait_ge(sm("f_tr"), kk - 1)
                    V.tensor_tensor(view(SC, FH + b * FC, (1, FC)), tmp, bank[4 + b][:, FC:2 * FC], ALU.mult).then_inc(sm("f_h"), 1)

                def add_down(k, kk, y):
                    dve.wait_ge(sm("f_down"), kk + 1)
                    if not (isinstance(kk, int) and kk == 0):
                        dve.wait_ge(sm("f_y"), kk * 2)
                    for half in range(2):
                        v = y(half)
                        V.tensor_tensor(v, v, bank[half][:, :], ALU.add).then_inc(sm("f_y"), 1)

                if not last:
                    step(V.memset(view(BIG, 0, (1, NT * D)), 0.0))
                    state = {"it": None}
                    for half in range(2):
                        write_lo(dve, "ff", base["ff", 0], split_base["ff", 0], None, half)

                    def inner(it):
                        state["it"] = it
                        step.loop = it * (3 * 2 * NT) - 3 * 2 * NT

                    def first(k, kk):
                        hidden(step, k, kk)
                        if k % NT == 2 and k < (N_FF - 1) * NT:
                            c = k // NT + 1
                            for half in range(2):
                                write_lo(dve, "ff", base["ff", 0] + c, split_base["ff", 0] + c,
                                         None if isinstance(kk, int) else state["it"], half)
                        if not isinstance(kk, int) and k == 2 * NT:
                            step.leave(3 * 2 * NT * (N_FF // 2 - 2))

                    in_pairs(dve, first, lambda k, kk: add_down(k, kk, lambda half: ysum(k % NT, half * 512, 512)), inner)
                    layer_norm(1, False)
                    continue

                dve.wait_ge(sm("r_mm"), 1)
                for i in range(2):
                    lo, top = view(ST, 200 + 8 * i, (1, 8)), view(ST, 216 + 8 * i, (1, 8))
                    step(V.tensor_tensor(lo, bank[4][:, 8 * i:8 * i + 8], prm("rb", (1, 8)), ALU.add))
                    step(V.max(top, lo))
                    step(V.max_index(IDX[:, 8 * i:8 * i + 8], top, lo))
                    step(V.tensor_tensor(view(ST, 136 + i, (1, 1)), view(ST, 217 + 8 * i, (1, 1)),
                                         view(ST, 216 + 8 * i, (1, 1)), ALU.subtract))
                V.tensor_copy(view(ST, 256, (1, 16)), IDX[:, :]).then_inc(sm("r_diff"), 1)
                dve.wait_ge(sm("r_diff"), 1)
                dve.wait_ge(sm("r_exp"), 1)
                step(V.tensor_scalar(view(ST, 138, (1, 2)), view(ST, 136, (1, 2)), 1.0, None, ALU.add))
                step(V.reciprocal(view(ST, 138, (1, 2)), view(ST, 138, (1, 2))))
                step(V.tensor_tensor(view(ST, 136, (1, 2)), view(ST, 136, (1, 2)), view(ST, 138, (1, 2)), ALU.mult))
                for i in range(2):
                    def one_hot(at, scale, which):
                        step(V.tensor_scalar(view(ST, at + 8 * i, (1, 8)), cst("eights"),
                                             view(ST, 256 + 8 * i + which, (1, 1)), scale, ALU.is_equal, ALU.mult))
                    one_hot(272, 1.0, 0)
                    one_hot(288, 1.0, 1)
                    one_hot(304, view(ST, 138 + i, (1, 1)), 0)
                    one_hot(320, view(ST, 136 + i, (1, 1)), 1)
                step(V.tensor_tensor(view(ST, 304, (1, 16)), view(ST, 304, (1, 16)), view(ST, 320, (1, 16)), ALU.add))
                signal(V.tensor_tensor(view(ST, 272, (1, 16)), view(ST, 272, (1, 16)), view(ST, 288, (1, 16)), ALU.add),
                       "r_chosen", 1)
                dve.wait_ge(sm("r_count"), 1)
                step(V.tensor_tensor(view(ST, 336, (1, 16)), bank[5][:, 0:16], view(ST, 272, (1, 16)), ALU.mult))
                step(V.tensor_scalar(view(ST, 336, (1, 16)), view(ST, 336, (1, 16)), -1.0, None, ALU.add))
                over_f, rank_f = view(ST, 353, (1, 8), np_=1), view(ST, 361, (1, 8), np_=1)
                step(V.tensor_scalar(over_f, bank[5][0:1, 16:24], float(P), None, ALU.is_gt))
                step(V.tensor_reduce(view(ST, 352, (1, 1), np_=1), over_f, AX, ALU.max))
                step(V.tensor_tensor_scan(rank_f, view(CS, C_AT["ones"][0], (0, 8), np_=1), over_f, 0.0, ALU.mult, ALU.add))
                step(V.tensor_tensor(rank_f, rank_f, over_f, ALU.subtract))
                V.tensor_copy(RI[0:1, 0:17], view(ST, 352, (1, 17), np_=1)).then_inc(sm("overflow_known"), 1)

                def experts(st, blk):
                    if blk:
                        st(V.tensor_scalar(view(ST, 336, (1, 16)), view(ST, 336, (1, 16)), -float(P), None, ALU.add))
                    sel_t, sel_o = SELS[blk]
                    for e in range(NE):
                        for i in range(2):
                            place = view(ST, 336 + 8 * i + e, (1, 1))
                            V.tensor_scalar(view(sel_t, sel_o + e * 256 + i * P, (1, P)), cst("slots"), place, None,
                                            ALU.is_equal).then_inc(sm("sel"), 1)
                            V.tensor_scalar(view(SC, SELW + e * 256 + i * P, (1, P)), cst("slots"), place,
                                            view(ST, 304 + 8 * i + e, (1, 1)), ALU.is_equal, ALU.mult).then_inc(sm("sel"), 1)

                    def gathered(moved, j, n):
                        dve.wait_ge(sm("gx_mm"), n)
                        for q in range(4):
                            ins = V.tensor_scalar(BIG[:, bass.ds(moved + (XGA + j * 1024 + (4 + q) * P), P)],
                                                  bank[5 + 2 * j][:, q * P:(q + 1) * P], mod(1, 4, 4 + q, 1),
                                                  mod(1, 3, 4 + q, 1), ALU.mult, ALU.add)
                        ins.then_inc(sm("gx_d"), 1)

                    if not blk:
                        with dve.Fori(0, NE // 2) as it:
                            for j in range(2):
                                gathered(it * 2048, j, it * 2 + (j + 1))
                    dve.wait_ge(sm("sw_copy"), 4 * (blk + 1))
                    k0 = SF + blk * NE * N_EX
                    n0, i0 = base["ff", 1] + blk * NE * N_EX, split_base["ex", 1] + blk * NE * N_EX
                    start = st.n
                    per_unit = 3
                    per_expert = per_unit * N_EX

                    def tokens(e, n):
                        dve.wait_ge(sm("x_hi"), n)
                        V.tensor_tensor(rview(SC, XGL, (1, D)), BIG[:, bass.ds(e * D + XGA, D)],
                                        rview(SC, XGS, (1, D)).bitcast(F32), ALU.subtract).then_inc(sm("x_lo"), 1)

                    def scatter(e):
                        V.tensor_copy(view(SC, CWS, (1, 2 * P)), SC[:, bass.ds(e * 256 + CWA, 256)]).then_inc(sm("cw"), 1)

                    def two_chunks(moved):
                        for c in range(2):
                            for half in range(2):
                                write_lo(dve, "ex", n0 + c, i0 + c, moved, half)

                    def body(e, r, more):
                        at = {"moved": r * (N_EX // 2)}
                        st.loop = r * per_expert
                        if blk:
                            gathered(0, 0, r + (NE + 1))
                            dve.wait_ge(sm("gx_d"), r + (NE + 1))
                            tokens(0, r + (NE + 1))
                            two_chunks(at["moved"])
                        scatter(e)

                        def low(k, half):
                            if more or k - k0 + 2 < N_EX:
                                c = k - k0 + 2
                                write_lo(dve, "ex", n0 + c, i0 + c, at["moved"], half)

                        def pair(k, kk):
                            low(k, 0)
                            hidden(st, k + 1, kk + 1)
                            low(k, 1)

                        def last(k, kk):
                            if more:
                                tokens(e + 1, r + (blk * NE + 2))
                            low(k, 0)
                            low(k, 1)

                        def inner(it):
                            if it is None:
                                st.loop = r * per_expert
                                st.n += 2 * per_unit * (N_EX // 2 - 3)
                                at["moved"] = r * (N_EX // 2)
                            else:
                                st.loop = r * per_expert + it * (2 * per_unit)
                                at["moved"] = r * (N_EX // 2) + it

                        one_expert(dve, k0, r, lambda k, kk: hidden(st, k, kk), pair, last, inner)
                        dve.wait_ge(sm("s_mm"), r + blk * NE + 1)
                        for i in range(2):
                            for half in range(2):
                                v = ysum(i, half * 512, 512)
                                V.tensor_tensor(v, v, bank[2 * i + half][:, :], ALU.add).then_inc(sm("s_add"), 1)
                        dve.wait_ge(sm("s_add"), r * 4 + (1 + 4 * (blk * NE + 1)))
                        V.memset(view(ST, 501, (1, 1)), 0.0)
                        assert st.n - start == per_expert
                        st.n = start

                    if not blk:
                        tokens(0, 1)
                        two_chunks(0)
                    over_experts(dve, blk, body)
                    st.leave(per_expert * NE)

                V.memset(view(BIG, 0, (1, 2 * D)), 0.0).then_inc(sm("s_add"), 1)
                dve.wait_ge(sm("s_add"), 1)
                experts(step, 0)
                over = dve.value_load(RI[0:1, 0:1], min_val=0, max_val=1)
                with dve.If(over > 0):
                    experts(Steps(dve, dve_block_step), 1)
                layer_norm(3, False)

        @block.tensor
        def _(pe):
            T = nc.tensor
            mm = nc.tensor.matmul

            def ready(n, it=None):
                s = g_slot(n)
                for h in range(2):
                    v = 32 * (n // 2 + 1)
                    pe.wait_ge(g_loaded[2 * s + h], v if it is None else it * 32 + v)

            pe.wait_ge(params, 16 * 21)
            for a, n, o in ((0, 16, 0), (P, 96, 16), (2 * P, 4, 112)):
                ins = T.transpose(bank[0][:, o:o + n], view(SC, a, (1, P), np_=n), cst("ident", 0, n, n))
            ins.then_inc(sm("start_T"), 1)
            pe.wait_ge(sm("sct"), 1)
            def ada_rows(dst, n, it, frees=None):
                ready(n, it)
                for kt in range(KT):
                    g = kt % 4
                    ins = mm(bank[dst][32 * g:32 * g + 32, :], view(SC, SCT + kt * 32, (1, 32)), gw(n, kt),
                             start=kt < 4, stop=kt >= 4)
                    if kt == 0 and frees is not None:
                        ins.then_inc(g_free[g_slot(frees)], 1)
                ins.then_inc(sm("ada_mm"), 1)

            def ada_columns(dst, rows, frees):
                for q in range(4):
                    ins = mm(bank[dst][:, 2 * q:2 * q + 2], view(SC, rows + q * P, (1, P)), cst("pick"), start=True, stop=True)
                    if q == 0 and frees is not None:
                        ins.then_inc(g_free[g_slot(frees)], 1)
                ins.then_inc(sm("ada_col"), 1)

            def ada_columns_0(j, it, frees):
                i = 0 if it is None else it
                pe.wait_ge(sm("ada_row"), i * 2 + (j + 1))
                if it is not None:
                    pe.wait_ge(sm("mod"), i * 2 + j)
                ada_columns(2 + j % 2, ADAR + (j % 2) * 512, frees)

            ada_rows(0, 0, None)
            ada_rows(1, 1, None, 0)
            ada_columns_0(0, None, 1)
            with pe.Fori(1, N_ADA // 2) as it:
                ada_rows(0, 0, it)
                ada_columns_0(-1, it, 0)
                ada_rows(1, 1, it)
                ada_columns_0(0, it, 1)
            ada_columns_0(-1, N_ADA // 2, None)
            pe.wait_ge(sm("mods"), 1)

            def gate_products(i):
                for s in range(2):
                    for half in range(2):
                        k = i * 4 + s * 2 + half
                        pe.wait_ge(sm("diag"), k + 1)
                        if k >= 2:
                            pe.wait_ge(sm("gate_row"), k - 1)
                        mm(bank[6 + half][:, :], cst("ones", n=P), view(DIAG[i % 2][0], DIAG[i % 2][1] + half * 512, (1, 512)), start=True,
                           stop=True).then_inc(sm("gate_mm"), 1)

            def x_transposes(u, tiles):
                for kt in range(KT):
                    if kt >= 2:
                        pe.wait_ge(sm("h_lat"), u * KT + kt - 1)
                        if 0 in tiles:
                            pe.wait_ge(sm("h_ctx"), u * KT + kt - 1)
                    for t in tiles:
                        ins = T.transpose(bank[kt % 2 + 2 * (t // 2)][:, t * P:(t + 1) * P], xt(t, kt * P, P), ident)
                    ins.then_inc(sm("x_T"), 1)

            for l in range(DEPTH):
                outs = OUTS[l]
                t0 = outs[0]
                if l == 0:
                    pe.wait_ge(sm("x_loaded"), 16 * NT)
                else:
                    pe.wait_ge(sm("x_ready"), X_READY[2 * l])
                gate_products(2 * l)
                x_transposes(2 * l, range(NT))
                pe.wait_ge(sm("h_lo"), KT * (2 * l + 1))
                for g in range(N_IN * NT):
                    cchunk, t = divmod(g, NT)
                    n = base["in", l] + cchunk
                    w = min(WC, NIN - cchunk * WC)
                    if g >= 4:
                        pe.wait_ge(sm("p_dve" if g % 2 else "p_act"), 12 * l + (g - 4) // 2 + 1)
                    else:
                        pe.wait_ge(sm("gate_row"), 4 * (2 * l + 1))
                    ins = three_products(bank[4 + g % 4][:, 0:w],
                                         lambda kt: (tokens_hi(2 * l, kt, t * P, P),
                                                     rview(HT, kt * 512 + t * P, (1, P))),
                                         lambda kt: (hi("in", n, kt, w), lo(n, kt, w)),
                                         2 * (split_base["in", l] + cchunk) + 1 if t == 0 else None, pe)
                    if t == 0 and cchunk:
                        ins[0].then_inc(g_free[g_slot(n - 1)], 1)
                    ins[-1].then_inc(sm("p_mm"), 1)
                pe.wait_ge(sm("p_act"), 12 * (l + 1))
                pe.wait_ge(sm("p_dve"), 12 * (l + 1))
                for g in range(6):
                    for t in range(NT):
                        if g < 2:
                            for d in range(2):
                                ins = mm(bank[g][32 * d:32 * d + 32, t * P:(t + 1) * P], big(t, C_MG + 4 * g + 8 * d, 32),
                                         ident, start=True, stop=True)
                        else:
                            ins = T.transpose(bank[g][:, t * P:(t + 1) * P], big(t, (g - 2) * P, P), ident)
                        if g == 0 and t == 0:
                            ins.then_inc(g_free[g_slot(base["in", l] + N_IN - 1)], 1)
                    ins.then_inc(sm("m_T"), 1)
                pe.wait_ge(sm("mq_T"), 2 * (l + 1))
                pe.wait_ge(sm("mk_T"), 2 * (l + 1))
                pe.wait_ge(sm("v1"), 5 * (l + 1))

                def m_scores(h):
                    p0 = 64 * (h % 2)
                    if h:
                        pe.wait_ge(sm("m_w"), 3 * (8 * l + 2 * h))
                    for j in range(4):
                        dst = bank[1 + j][:, :] if j < 2 else bank[3][:, (j - 2) * 256:(j - 1) * 256]
                        a, n = (0, 512) if j < 2 else (256, 256)
                        ins = mm(dst, view(SC, MKT + (h // 2) * 512 + j * P, (1, P), p0=p0, np_=64),
                                 view(SC, MQT + (h // 2) * 512 + a, (1, n), p0=p0, np_=64), start=True, stop=True)
                    ins.then_inc(sm("m_s"), 1)

                def m_stabiliser(u):
                    h, d = divmod(u, 2)
                    if u >= 2:
                        pe.wait_ge(sm("m_decay"), 8 * l + u - 1)
                    row = d * 32 + h
                    o = C_AT["ident"][0]
                    mm(bank[4 + d][:, :], view(CS, o + row, (0, P), np_=64), view(SC, ROWM, (1, 512), np_=64), start=True,
                       stop=True).then_inc(sm("m_bc"), 1)

                def m_values(u):
                    h, d = divmod(u, 2)
                    pe.wait_ge(sm("m_w"), 3 * (8 * l + u + 1))
                    if u >= 2:
                        pe.wait_ge(sm("m_hs"), 8 * l + u - 1)
                    for i in outs:
                        if d == 0:
                            keys = list(range(i + 1))
                        else:
                            keys = [j for j in range(NT) if (j >= i if (i < 2) == (j < 2) else i >= 2)]
                        for q, j in enumerate(keys):
                            ins = mm(bank[6 + d][:, i * 65:(i + 1) * 65], view(SC, MD + d * 2048 + j * 512 + i * P, (1, P)),
                                     view(SC, V1 + j * 260 + h * 65, (1, 65)), start=q == 0, stop=q == len(keys) - 1)
                    ins.then_inc(sm("m_pv"), 1)

                m_scores(0)
                pe.wait_ge(sm("gate_rows_ready"), l + 1)
                m_stabiliser(0)
                m_stabiliser(1)
                pe.wait_ge(sm("floor_row"), l + 1)
                for k, src in enumerate((ROWA, ROWT)):
                    for j in range(NT):
                        ins = T.transpose(bank[0][:, k * 256 + j * 64:k * 256 + (j + 1) * 64],
                                          view(SC, src + j * P, (1, P), np_=64), cst("ident", 0, 64, 64))
                ins.then_inc(sm("gates_T"), 1)
                for u in range(8):
                    if u + 2 < 8:
                        m_stabiliser(u + 2)
                    m_values(u)
                    if u % 2 and u < 7:
                        m_scores(u // 2 + 1)
                pe.wait_ge(sm("rope"), 2 * (l + 1))
                pe.wait_ge(sm("gate_cols"), l + 1)
                pe.wait_ge(sm("m_decay"), 8 * (l + 1))
                for j in range(6):
                    for t in (range(NT) if j >= 4 else outs):
                        if j < 4:
                            ins = T.transpose(bank[j][:, t * P:(t + 1) * P], big(t, C_AQ + j * P, P), ident)
                            continue
                        for half in range(2):
                            ins = mm(bank[j][64 * half:64 * half + 64, t * P:(t + 1) * P],
                                     big(t, C_AK + (j - 4) * 64, 64), ident, start=True, stop=True)
                    ins.then_inc(sm("a_T"), 1)
                pe.wait_ge(sm("a_qk"), 6 * (l + 1))
                off = sum(N_ATT[:l])
                for k in range(N_ATT[l] + 2):
                    if k < N_ATT[l]:
                        i, j, half = ATT[l][k]
                        b, n, p0 = k % 2, 256 if i < 2 else 512, 64 * half
                        if k >= 2:
                            pe.wait_ge(sm("a_exp"), 2 * (off + k - 1))
                        ins = mm(bank[b][:, 0:n], view(HT, AQT + j * 512 + i * P, (1, P), p0=p0, np_=64),
                                 view(HT, AQT + (4 + j // 2) * 512, (1, n), p0=p0, np_=64), start=True, stop=i < 2)
                        if i >= 2:
                            o = (5 - i) * P
                            ins = mm(bank[b][:, o:o + P], ident, cst("bias_t2" if i == 2 else "bias_t3"), start=False,
                                     stop=True)
                        ins.then_inc(sm("a_s"), 1)
                    if 1 <= k <= N_ATT[l]:
                        i = ATT[l][k - 1][0]
                        b = (k - 1) % 2
                        pe.wait_ge(sm("a_exp"), 2 * (off + k))
                        if k >= 3:
                            pe.wait_ge(sm("a_pTs"), off + k - 2)
                        for q in range(2 if i < 2 else 4):
                            ins = T.transpose(bank[2 + b][:, q * P:(q + 1) * P], view(HT, AP_ + b * 512 + q * P, (1, P)), ident)
                        ins.then_inc(sm("a_pT"), 1)
                    if k >= 2:
                        i, j, half = ATT[l][k - 2]
                        b = k % 2
                        pe.wait_ge(sm("a_pTs"), off + k - 1)
                        if k >= 4:
                            pe.wait_ge(sm("a_o"), off + k - 3)
                        nk = 2 if i < 2 else 4
                        for q in range(nk):
                            ins = mm(bank[4 + b][:, 0:64], view(SC, APT + b * 512 + q * P, (1, P)),
                                     big(q, C_AV + (j // 2) * 64, 64), start=q == 0, stop=q == nk - 1)
                        ins.then_inc(sm("a_pv"), 1)
                    if l == 0 and ada_after(k - 2) is not None:
                        c1 = ada_after(k - 2)
                        pe.wait_ge(sm("ada_row"), N_ADA + c1 + 1)
                        if c1:
                            pe.wait_ge(sm("mod"), N_ADA + c1)
                        ada_columns(7, ADAL, base["ada", 1] + c1)
                    if l == 0 and ada_after(k) is not None:
                        if ada_after(k) == 0:
                            pe.wait_ge(sm("m_hs"), 8)
                        ada_rows(6, base["ada", 1] + ada_after(k), None)
                if l == 0:
                    pe.wait_ge(sm("mods"), 2)
                pe.wait_ge(sm("a_o"), off + N_ATT[l])
                pe.wait_ge(sm("m_hs"), 8 * (l + 1))
                for g in range(4):
                    for t in range(NT):
                        rows = P if g < 2 else RANK
                        c0 = (C_GQ, C_GK, C_GR, C_GR + RANK)[g]
                        ins = T.transpose(bank[g][0:rows, t * P:(t + 1) * P], big(t, c0, rows), ident)
                    ins.then_inc(sm("g_T"), 1)
                for d in range(2):
                    pe.wait_ge(sm("g_r"), 2 * l + d + 1)
                    mm(bank[4 + d][:, :], prm("gup", (1, P), off=(2 * l + d) * P, np_=RANK),
                       view(SC, GRT + d * 512, (1, 512), np_=RANK), start=True, stop=True).then_inc(sm("g_z"), 1)
                pe.wait_ge(sm("g_prod"), 3 * l + 1)
                for d in range(2):
                    for t in range(NT):
                        ins = T.transpose(bank[6 + d][:, t * P:(t + 1) * P], view(SC, GKD + d * 512 + t * P, (1, P)), ident)
                    ins.then_inc(sm("g_kT"), 1)
                pe.wait_ge(sm("g_qk"), 2 * (l + 1))
                pe.wait_ge(sm("g_prod"), 3 * l + 3)
                pe.wait_ge(sm("g_ktok"), 2 * (l + 1))

                def g_scores(d):
                    if d == 1:
                        pe.wait_ge(sm("g_acopy"), 2 * l + 1)
                    for i in range(NT):
                        for h in range(4):
                            a = d * 512 + i * P
                            ins = mm(bank[4 + h][:, i * P:(i + 1) * P], view(SC, GNB + a, (1, P), p0=32 * h, np_=32),
                                     view(SC, GEB + a, (1, P), p0=32 * h, np_=32), start=True, stop=True)
                    ins.then_inc(sm("g_a"), 1)

                def g_values(d):
                    pe.wait_ge(sm("g_aok"), 2 * l + d + 1)
                    for i in outs:
                        for h in range(4):
                            ins = mm(bank[i][:, h * 64:(h + 1) * 64], view(SC, GAT + h * 512 + i * P, (1, P)),
                                     big(i, C_GV + h * 64, 64), start=d == 0 and h == 0, stop=False, skip_group_check=True)
                        for cc in range(2):
                            ch = 2 * i + cc
                            k = ch if d == 0 else (3 - ch if ch < 4 else 11 - ch)
                            if k:
                                ins = mm(bank[i][64 * cc:64 * cc + 64, 0:256], view(SC, GEB + d * 512 + ch * 64, (1, 64)),
                                         view(SC, GS + (d * 7 + k) * 256, (1, 256)), start=False, stop=d == 1,
                                         skip_group_check=True)
                    ins.then_inc(sm("g_pv"), 1)

                g_scores(0)
                for q in range(14):
                    k, d = divmod(q, 2)
                    ch = chunk_of(d, k)
                    p0 = 64 * (ch % 2)
                    if q >= 4:
                        pe.wait_ge(sm("g_st"), 14 * l + q - 3)
                    mm(bank[q % 4][:, 0:256], view(SC, GKT + d * 512 + (ch // 2) * P, (1, P), p0=p0, np_=64),
                       view(BIG, (ch // 2) * NIN + C_GV, (1, 256), p0=p0, np_=64), start=True, stop=True).then_inc(sm("g_kv"), 1)
                g_scores(1)
                pe.wait_ge(sm("g_st"), 14 * (l + 1))
                g_values(0)
                g_values(1)
                pe.wait_ge(sm("cat"), 2 * (l + 1))
                for kt in range(KT):
                    if kt >= 4:
                        pe.wait_ge(sm("c_dve" if kt % 2 else "c_act"), 4 * l + (kt - 4) // 2 + 1)
                    c0 = C_MQ + kt * P if kt < 2 else (C_AQ + (kt - 2) * P if kt < 6 else C_GQ + (kt - 6) * P)
                    for t in outs:
                        ins = T.transpose(bank[kt % 4][:, t * P:(t + 1) * P], big(t, c0, P), ident)
                    ins.then_inc(sm("c_T"), 1)
                pe.wait_ge(sm("c_act"), 4 * (l + 1))
                pe.wait_ge(sm("c_dve"), 4 * (l + 1))
                for cc in range(N_OUT):
                    n = base["out", l] + cc
                    ready(n)
                    for t in outs:
                        for kt in range(KT):
                            ins = mm(bank[t * 2 + cc][:, :], view(HT, kt * 512 + t * P, (1, P)), gw(n, kt), start=kt == 0,
                                     stop=kt == KT - 1)
                        ins.then_inc(sm("o_mm"), 1)
                    pe.drain().then_inc(g_free[g_slot(n)], 1)
                pe.wait_ge(sm("x_ready"), X_READY[2 * l] + N_TO[l])
                gate_products(2 * l + 1)
                x_transposes(2 * l + 1, outs)

                def up(k, kk, stage, n, i, moved, lhs, first, frees, between=None):
                    b = k % 2
                    if not (isinstance(kk, int) and kk < 2):
                        pe.wait_ge(sm("f_h"), kk - 1)
                    w = None
                    if first:
                        w = 2 * i + 1 if moved is None else moved * 4 + (2 * i + 1)
                    ins = three_products(bank[4 + b][:, :], lhs, lambda kt: (hi(stage, n, kt), lo(n, kt)), w, pe, between)
                    if frees:
                        ins[0].then_inc(g_free[g_slot(n - 1)], 1)
                    ins[-1].then_inc(sm("f_up"), 1)

                def turn(k, kk):
                    b = k % 2
                    pe.wait_ge(sm("f_h"), kk + 1)
                    for q in range(2):
                        ins = T.transpose(bank[6 + b][:, q * P:(q + 1) * P], view(SC, FH + b * FC + q * P, (1, P)), ident)
                    ins.then_inc(sm("f_tr"), 1)

                def down(k, kk, m, moved, first, frees, start, stop, before=None):
                    b = k % 2
                    if first:
                        v = 16 * (m // 2 + 1)
                        pe.wait_ge(d_loaded[m % 2], v if moved is None else moved * 16 + v)
                    pe.wait_ge(sm("f_hT"), kk + 1)
                    if before:
                        before()
                    for half in range(2):
                        for q in range(2):
                            ins = mm(bank[half][:, :], view(SC, FHT + b * FC + q * P, (1, P)), dw(m, q, half),
                                     start=start and q == 0, stop=stop and q == 1)
                            if frees is not None and half == 0 and q == 0:
                                ins.then_inc(g_free[g_slot(frees)], 1)
                    ins.then_inc(sm("f_down"), 1)

                if l == 0:
                    pe.wait_ge(sm("h_lo"), KT * 2)
                    n0, i0 = base["ff", 0], split_base["ff", 0]

                    state = {"it": None}

                    def first(k, kk):
                        ch, t = divmod(k, NT)
                        moved = None if isinstance(kk, int) else state["it"]
                        up(k, kk, "ff", n0 + ch, i0 + ch, moved,
                           lambda kt: (tokens_hi(1, kt, t * P, P), rview(HT, kt * 512 + t * P, (1, P))),
                           t == 0, False, (lambda: turn(k - 1, kk - 1)) if k else None)

                    def second(k, kk):
                        ch, t = divmod(k, NT)
                        moved = None if isinstance(kk, int) else state["it"]

                        def summed():
                            if not (isinstance(kk, int) and kk == 0):
                                pe.wait_ge(sm("f_y"), kk * 2)

                        if k == N_FF * NT - 1:
                            turn(k, kk)
                        down(k, kk, ch, moved, t == 0, n0 + ch if t == 2 else None, True, True, summed)

                    in_pairs(pe, first, second, lambda it: state.update(it=it))
                    continue

                pe.wait_ge(sm("h_lat"), KT * 4)
                for i in range(2):
                    for kt in range(KT):
                        ins = mm(bank[4][:, 8 * i:8 * i + 8], view(HT, kt * 512 + (2 + i) * P, (1, P)), prm("rw", (1, 8), off=8 * kt),
                                 start=kt == 0, stop=kt == KT - 1)
                ins.then_inc(sm("r_mm"), 1)
                pe.wait_ge(sm("r_chosen"), 1)
                chosen = [view(ST, 272 + 8 * i, (1, 8)) for i in range(2)]
                ones = cst("ones", n=P)
                mm(bank[5][:, 0:8], cst("fwd"), chosen[0], start=True, stop=True)
                mm(bank[5][:, 8:16], ones, chosen[0], start=True, stop=False)
                mm(bank[5][:, 8:16], cst("fwd"), chosen[1], start=False, stop=True)
                mm(bank[5][0:1, 16:24], cst("ones", n=1), chosen[0], start=True, stop=False)
                mm(bank[5][0:1, 16:24], cst("ones", n=1), chosen[1], start=False, stop=True).then_inc(sm("r_count"), 1)

                def experts(blk):
                    pe.wait_ge(sm("sel"), (blk + 1) * NE * 4)
                    for q in range(16):
                        ins = T.transpose(bank[q // 4][:, (q % 4) * P:(q % 4 + 1) * P], view(SC, SELW + q * P, (1, P)), ident)
                        if q % 4 == 3:
                            ins.then_inc(sm("sw_T"), 1)
                    sel_t, sel_o = SELS[blk]

                    def gather(moved, j):
                        for kt in range(KT):
                            for i in range(2):
                                ins = mm(bank[4 + 2 * j + kt // 4][:, (kt % 4) * P:(kt % 4 + 1) * P], xt(2 + i, kt * P, P),
                                         sel_t[:, bass.ds(moved + (sel_o + j * 256 + i * P), P)], start=i == 0, stop=i == 1)
                        ins.then_inc(sm("gx_mm"), 1)

                    if not blk:
                        for j in range(2):
                            gather(0, j)
                        with pe.Fori(1, NE // 2) as it:
                            for j in range(2):
                                pe.wait_ge(sm("gx_a"), it * 2)
                                pe.wait_ge(sm("gx_d"), it * 2)
                                gather(it * 512, j)
                        pe.wait_ge(sm("gx_a"), NE)
                        pe.wait_ge(sm("gx_d"), NE)
                    pe.wait_ge(sm("sw_copy"), 4 * (blk + 1))
                    n0, m0, k0 = base["ff", 1] + blk * NE * N_EX, N_FF + blk * NE * N_EX, SF + blk * NE * N_EX
                    i0 = split_base["ex", 1] + blk * NE * N_EX

                    def body(e, r, more, begin=False):
                        if blk:
                            gather(e * 256, 0)
                        st = {"moved": r * (N_EX // 2)}

                        def first(k, kk, frees=False, between=None):
                            up(k, kk, "ex", n0 + k - k0, i0 + k - k0, st["moved"],
                               lambda kt: (rview(SC, XGS + kt * P, (1, P)), rview(SC, XGL + kt * P, (1, P))),
                               True, frees, between)

                        def summed():
                            pe.wait_ge(sm("s_add"), r * 4 + (1 + 4 * blk * NE))

                        def step(k, kk):
                            first(k + 1, kk + 1, k == k0, lambda: turn(k, kk))
                            down(k, kk, m0 + k - k0, st["moved"], True, n0 + k - k0 + 1, k == k0, False,
                                 summed if k == k0 else None)

                        def last(k, kk):
                            turn(k, kk)
                            down(k, kk, m0 + k - k0, st["moved"], True, None, False, True)
                            if more:
                                pe.wait_ge(sm("x_lo"), r + 2)
                                first(k + 1, kk + 1)

                        def inner(it):
                            st["moved"] = r * (N_EX // 2) if it is None else r * (N_EX // 2) + it

                        if blk or begin:
                            pe.wait_ge(sm("x_lo"), r + (blk * NE + 1))
                            first(k0, r * N_EX + k0)
                        if begin:
                            return
                        one_expert(pe, k0, r, lambda k, kk: None, step, last, inner)
                        pe.wait_ge(sm("ye"), r * 2 + 2 * (blk * NE + 1))
                        pe.wait_ge(sm("cw"), r + (blk * NE + 1))
                        for i in range(2):
                            for half in range(2):
                                ins = mm(bank[2 * i + half][:, :], view(SC, CWS + i * P, (1, P)), view(SC, YE + half * 512, (1, 512)),
                                         start=True, stop=True)
                        ins.then_inc(sm("s_mm"), 1)

                    if not blk:
                        body(0, 0, True, begin=True)
                    over_experts(pe, blk, body)
                    if not blk:
                        pe.wait_ge(sm("s_add"), 1 + 4 * NE)

                experts(0)
                over = pe.value_load(RI[0:1, 0:1], min_val=0, max_val=1)
                with pe.If(over > 0):
                    experts(1)


_INS = ["x", "c", "ctx", "c_ctx", "w_ada", "b_ada", "w_in", "mlstm_gate_b", "mlstm_norm_w", "attn_sink",
        "gla_gate_up", "gla_gate_b", "gla_norm_w", "w_out", "ln_w", "ln_b", "ffn_w_gu", "ffn_w_down",
        "router_w", "router_b", "moe_w_gu", "moe_w_down"]
_OUTS = [((1, 256, 1024), "float32")]


def kernel(**inputs):
    import numpy as _np
    import concourse.bacc as _bacc
    from concourse import mybir as _mybir
    from concourse.bass_utils import run_bass_kernel_spmd as _run

    nc = _bacc.Bacc("TRN2", target_bir_lowering=False, num_devices=1)
    arrays, args = {}, []
    for name in _INS + ["constants"]:
        a = _np.ascontiguousarray(inputs[name]) if name != "constants" else constants()
        arrays[f"in_{name}_dram"] = a
        args.append(nc.dram_tensor(f"in_{name}_dram", a.shape, _mybir.dt.from_np(a.dtype), kind="ExternalInput").ap())
    for i, (shape, dtype) in enumerate(_OUTS):
        dt = _mybir.dt.from_np(_np.dtype(dtype))
        args.append(nc.dram_tensor(f"out_{i}_dram", shape, dt, kind="ExternalOutput").ap())
    bass_hymba(nc, *args)
    r = _run(nc, [arrays], core_ids=[0])
    got = tuple(r.results[0][f"out_{i}_dram"] for i in range(len(_OUTS)))
    return got[0]
```

```python
from contextlib import ExitStack

import numpy as np

import concourse.bass as bass
from concourse import mybir
from concourse.alu_op_type import AluOpType as ALU

ACT = mybir.ActivationFunctionType
F32 = mybir.dt.float32
I32 = mybir.dt.int32
U32 = mybir.dt.uint32
F32R = mybir.dt.float32r
AX = mybir.AxisListType.X

P = 128
D = 1024
KT = D // P
NTOK = 512
NT = NTOK // P
DEPTH = 2
HEADS = 4
HD = 64
AH = 8
DK = 32
CH = 64
RANK = 16
NMOD = 6
C_MQ, C_MK, C_MV, C_MO, C_MG = 0, 256, 512, 768, 1024
C_AQ, C_AK, C_AV = 1040, 1552, 1680
C_GQ, C_GK, C_GV, C_GG, C_GR = 1808, 1936, 2064, 2320, 2576
NIN = 2608
WC = 512
WI = 436
N_IN = -(-NIN // WI)
N_ADA = NMOD * D // WC
N_OUT = D // WC
FC = 256
D_FF = 2816
N_FF = D_FF // FC
NE = 8
D_EX = 3584
N_EX = D_EX // FC
ALPHA = float((2 * DEPTH) ** 0.25)
EPS = 1e-5
NEG = -1.0e30

CONSTS = [("ident", 128), ("fwd", 128), ("bwd", 128), ("not_fwd", 128), ("not_bwd", 128),
          ("gnot_fwd", 128), ("gnot_bwd", 128), ("bias_t2", 128), ("bias_t3", 128),
          ("cos", 128), ("sin", 128), ("zeros", 1), ("reset", 512), ("ones", 128), ("blocks", 256),
          ("pick", 2), ("eights", 8), ("slots", 128)]
C_AT = {}
_n = 0
for _name, _w in CONSTS:
    C_AT[_name] = (_n, _w)
    _n += _w
NCONST = _n


def constants():
    c = np.zeros((P, NCONST), np.float32)

    def put(name, a):
        o, w = C_AT[name]
        c[:, o:o + w] = a

    i = np.arange(P)[:, None]
    j = np.arange(P)[None, :]
    put("ident", i == j)
    put("fwd", i <= j)
    put("bwd", i >= j)
    put("not_fwd", i > j)
    put("not_bwd", i < j)
    same = i // CH == j // CH
    put("gnot_fwd", ~(same & (i <= j)))
    put("gnot_bwd", ~(same & (i >= j)))
    put("bias_t2", np.where(j > i, NEG, 0.0))
    put("bias_t3", np.where(j < i, NEG, 0.0))
    inv = np.float32(10000.0) ** (-np.arange(16, dtype=np.float32) / np.float32(16))
    cos, sin = np.zeros((P, 2, 2, 2, 16)), np.zeros((P, 2, 2, 2, 16))
    for t in range(2):
        tok = t * P + np.arange(P)
        for half, pos in enumerate((tok // 64, tok % 64)):
            ang = (pos.astype(np.float32)[:, None] * inv).astype(np.float32)
            cos[:, t, half, :, :] = np.cos(ang)[:, None]
            sin[:, t, half, 0, :] = -np.sin(ang)
            sin[:, t, half, 1, :] = np.sin(ang)
    put("cos", cos.reshape(P, 128))
    put("sin", sin.reshape(P, 128))
    put("reset", np.broadcast_to((np.arange(512) % CH != 0).astype(np.float32), (P, 512)))
    put("ones", 1.0)
    put("blocks", i // DK == np.arange(256)[None, :] // HD)
    put("pick", i % 32 == np.arange(2)[None, :])
    put("eights", np.arange(8)[None, :])
    put("slots", np.arange(128)[None, :])
    return c


def bass_hymba(nc, x, c, ctx_in, c_ctx, w_ada, b_ada, w_in, mlstm_gate_b, mlstm_norm_w, attn_sink,
               gla_gate_up, gla_gate_b, gla_norm_w, w_out, ln_w, ln_b, ffn_w_gu, ffn_w_down,
               router_w, router_b, moe_w_gu, moe_w_down, consts, out):
    es = ExitStack()
    with es:
        PLACE = {}

        def sb(name, shape, dt=F32):
            t = es.enter_context(nc.sbuf_tensor(name, shape, dt))
            PLACE[t.name] = nc.sbuf_base - shape[1] * 4
            assert PLACE[t.name] % 32 == 0
            return t

        def sem(name):
            return es.enter_context(nc.semaphore(name))

        def view(t, off, *dims, p0=0, np_=P):
            row = t.shape[1]
            return bass.AP(tensor=t, offset=p0 * row + off, ap=[[row, np_]] + [list(d) for d in dims])

        X = sb("X", [P, NT * D])
        HT = sb("HT", [P, KT * NTOK])
        BIG = sb("BIG", [P, NT * NIN])
        GW = sb("GW", [P, 2 * KT * WC])
        DW = sb("DW", [P, 2 * 2 * D])
        GATE = sb("GATE", [P, 2 * D])
        LNR = sb("LNR", [P, 2 * D])
        CS = sb("CS", [P, NCONST])
        SC = sb("SC", [P, 13072])
        MOD = sb("MOD", [P, DEPTH * 48 * 2])
        PRM = sb("PRM", [P, 844])
        ST = sb("ST", [P, 512])
        RI = sb("RI", [P, 24], I32)
        IDX = sb("IDX", [P, 16], U32)
        bank = [es.enter_context(nc.psum_tensor(f"bank{i}", [P, 512], F32)) for i in range(8)]

        ROUNDED = {t.name: nc.alloc_sbuf_tensor_at(f"{t.name}_hi_lo", t.shape, F32R, offset=PLACE[t.name])
                   for t in (X, HT, BIG, GW, DW, SC)}

        def rview(t, off, *dims, p0=0, np_=P):
            return view(ROUNDED[t.name], off, *dims, p0=p0, np_=np_)

        def cst(name, p0=0, np_=P, n=None):
            o, w = C_AT[name]
            return view(CS, o, (1, n or w), p0=p0, np_=np_)

        ident = cst("ident")
        at = 0
        pos = {}
        for name, w in (("sink", 16), ("rw", 64), ("rb", 8), ("gb", 4), ("ib", 4),
                        ("bada", 192), ("gup", 512), ("ccol", 16), ("ecol", 16)):
            pos[name] = at
            at += w
        assert at <= 844
        NW = sb("NW", [P, 4 * 256])

        def prm(name, *dims, off=0, p0=0, np_=P):
            return view(PRM, pos[name] + off, *dims, p0=p0, np_=np_)

        def xt(t, a=0, n=D):
            return view(X, t * D + a, (1, n))

        def big(t, col, n):
            return view(BIG, t * NIN + col, (1, n))

        def bigs(t0, nt, col, *dims):
            return view(BIG, t0 * NIN + col, (NIN, nt), *dims)

        def ysum(t, a=0, n=D):
            return view(BIG, t * D + a, (1, n))

        def mod(layer, six, kt, s):
            return view(MOD, (layer * 48 + six * 8 + kt) * 2 + s, (1, 1))

        params = sem("params")
        g_loaded = [sem(f"g_loaded{s}{h}") for s in "01" for h in "ab"]
        g_free = [sem(f"g_free{s}{h}") for s in "01" for h in "ab"]
        d_loaded = [sem(f"d_loaded{s}") for s in "01"]
        dve_step = sem("dve_step")
        dve_block_step = sem("dve_block_step")
        act_step = sem("act_step")
        pool_step = sem("pool_step")
        S = {}

        def sm(name):
            if name not in S:
                S[name] = sem(name)
            return S[name]

        class Steps:

            def __init__(self, eng, s):
                self.eng, self.s, self.n, self.loop = eng, s, 0, None

            def __call__(self, ins):
                ins.then_inc(self.s, 1)
                self.n += 1
                self.eng.wait_ge(self.s, self.n if self.loop is None else self.n + self.loop)

            def leave(self, more):
                self.loop = None
                self.n += more

        base = {}
        n = 0
        base["ada", 0] = n
        n += N_ADA
        for l in range(DEPTH):
            base["in", l] = n
            n += N_IN
            if l == 0:
                base["ada", 1] = n
                n += N_ADA
            base["out", l] = n
            n += N_OUT
            base["ff", l] = n
            n += N_FF if l == 0 else 0

        def g_slot(n):
            return n % 2

        def gw(n, kt, a=0, w=WC):
            return view(GW, (g_slot(n) * KT + kt) * WC + a, (1, w))

        def dw(m, k, half):
            return view(DW, ((m % 2) * 2 + k) * D + half * WC, (1, WC))

        split_base = {("in", 0): 0, ("ff", 0): N_IN, ("in", 1): N_IN + N_FF, ("ex", 1): 2 * N_IN + N_FF}

        def hi_at(stage, s, kt):
            if stage == "in":
                return SC, (s * KT + kt) * WC
            if stage == "ff":
                return SC, 2048 + (s * KT + kt) * WC
            if s == g_slot(base["ff", 1]):
                return HT, kt * WC
            return (X, kt * WC) if kt < 4 else (SC, SEL + (kt - 4) * WC)

        def hi(stage, n, kt, a=0, w=WC):
            t, o = hi_at(stage, g_slot(n), kt)
            return rview(t, o + a, (1, w))

        def lo(n, kt, a=0, w=WC):
            return rview(GW, (g_slot(n) * KT + kt) * WC + a, (1, w))

        def write_hi(act, stage, n, moved, half, w=WC):
            s = g_slot(n)
            act.wait_ge(g_loaded[2 * s + half], 32 * (n // 2 + 1) + (0 if moved is None else moved * 32))
            t, o = hi_at(stage, s, 4 * half)
            nc.scalar.activation(rview(t, o, (WC, 4), (1, w)),
                                 view(GW, (s * KT + 4 * half) * WC, (WC, 4), (1, w)), ACT.Copy).then_inc(sm("w_hi"), 1)

        def write_lo(dve, stage, n, i, moved, half, w=WC):
            s = g_slot(n)
            dve.wait_ge(sm("w_hi"), 2 * i + half + 1 + (0 if moved is None else moved * 4))
            t, o = hi_at(stage, s, 4 * half)
            at = (GW, (s * KT + 4 * half) * WC, (WC, 4), (1, w))
            nc.vector.tensor_tensor(rview(*at), view(*at), rview(t, o, (WC, 4), (1, w)).bitcast(F32), ALU.subtract).then_inc(sm("w_lo"), 1)

        def down_hi(m, k, a=0, n=D):
            t, o = ((BIG, 8192), (SC, 10240))[m % 2]
            return rview(t, o + k * D + a, (1, n))

        def down_lo(m, k, a=0, n=D):
            return rview(DW, ((m % 2) * 2 + k) * D + a, (1, n))

        def tokens_hi(u, kt, a=0, n=512):
            t, o = (BIG, NT * D) if u == 1 else (SC, 8192)
            return rview(t, o + kt * 512 + a, (1, n))

        def three_products(dst, lhs, rhs, w_lo_wait, pe, between=None, frees=None):
            out = []
            for kt in range(KT):
                if kt == KT - 2 and between:
                    between()
                if w_lo_wait is not None and kt % 4 == 0:
                    pe.wait_ge(sm("w_lo"), w_lo_wait + kt // 4)
                (lh, ll), (rh, rl) = lhs(kt), rhs(kt)
                ins = nc.tensor.matmul(dst, lh, rh, start=kt == 0, stop=False)
                if kt == 4 and frees is not None:
                    ins.then_inc(g_free[2 * g_slot(frees)], 1)
                nc.tensor.matmul(dst, lh, rl, start=False, stop=False)
                out.append(nc.tensor.matmul(dst, ll, rh, start=False, stop=kt == KT - 1))
            return out

        def columns(l, t, c):
            if l == DEPTH - 1 and t < 2:
                first, end = {0: (WI - 256, WI), 1: (0, C_MO - WI), 2: (C_MG - 2 * WI, C_MG - 2 * WI + 256),
                              3: (WI - 256, WI)}.get(c, (0, min(WI, NIN - c * WI)))
                return first, end - first
            return 0, min(WI, NIN - c * WI)

        OUTS = [list(range(NT)), [2, 3]]

        ATT = [[(i, j, half) for i in OUTS[l] for j in range(4) for half in range(2)] for l in range(DEPTH)]
        N_ATT = [len(a) for a in ATT]
        N_TO = [len(o) for o in OUTS]
        NORMED = [0, 4, 8, 10]
        X_READY = [0, 4, 6, 8]
        LNC = 20
        MC = [None, 444, 142, None]

        def column(u, six, kt, s):
            if MC[u] is None:
                return mod(u // 2, 3 * (u % 2) + six, kt, s)
            return view(ST, MC[u] + 16 * (1 - six) + 2 * kt + s, (1, 1))

        def chunk_of(d, k):
            return k if d == 0 else (3 - k if k < 4 else 11 - k)

        SF = NT * N_FF

        SCT = 12800
        ADAR = 1024
        ADAL = 8192

        def ada_after(k):
            c = (k - 4) // 2
            return c if k % 2 == 0 and 0 <= c < N_ADA else None

        DIAG = [(BIG, NT * NIN - 1024), (SC, 11264)]
        V1, ROWI, ROWF, ROWT, ROWB, ROWA, ROWM = 0, 1040, 1552, 2064, 2576, 3088, 3600
        MQT, MKT, ACOL, MD, MT, ROT = 4112, 5136, 6160, 6672, 10768, 11024
        AQT, AP_, APT = 0, 3072, 6672
        GQT, GKF, GRT, GLG, GTMP, GB_, GEB, GNB, GKD, GKT = 0, 512, 1024, 2048, 3072, 4096, 5120, 6144, 7168, 8192
        GKV, GS, GEL, GAT = 9216, 9216, 13056, 2048
        NG, NSQ = 8960, 2048
        NSQM = 8704
        SSQ, RST = 376, 408
        FE, FH, FHT, FT, FHL = 0, 512, 1024, 1536, 12288
        SEL, CWA, YE, XGS, CWS, XGL, SELW = 2048, 4096, 6144, 7168, 8192, 8448, 10240
        XSH, XSL = 6144, 8192
        XGA = 2 * D
        SELS = [(SC, SEL), (BIG, XGA + D)]

        def in_pairs(eng, first, second, inner=None, swap=False):
            def step(k, kk):
                if swap:
                    second(k, kk)
                first(k + 1, kk + 1)
                if not swap:
                    second(k, kk)

            first(0, 0)
            for k in range(2 * NT):
                step(k, k)
            with eng.Fori(1, N_FF // 2) as it:
                if inner:
                    inner(it)
                for j in range(2 * NT):
                    step(j, it * 2 * NT + j)
            k0 = (N_FF - 1) * NT
            for k in range(k0, k0 + NT - 1):
                step(k, k)
            second(k0 + NT - 1, k0 + NT - 1)

        def one_expert(eng, k0, e, first, step, last, inner=None):
            kk = e * N_EX + k0
            first(k0, kk)
            step(k0, kk)
            with eng.Fori(0, N_EX // 2 - 2) as it:
                if inner:
                    inner(it)
                for j in range(1, 3):
                    step(k0 + j, kk + it * 2 + j)
            if inner:
                inner(None)
            for i in (N_EX - 3, N_EX - 2):
                step(k0 + i, kk + i)
            last(k0 + N_EX - 1, kk + (N_EX - 1))

        def over_experts(eng, blk, body):
            if not blk:
                with eng.Fori(0, NE - 1) as e:
                    body(e, e, True)
                body(NE - 1, NE - 1, False)
                return
            with eng.Fori(0, NE) as e:
                has = eng.value_load(RI[0:1, bass.ds(e + 1, 1)], min_val=0, max_val=1)
                rank = eng.value_load(RI[0:1, bass.ds(e + 9, 1)], min_val=0, max_val=NE - 1)
                with eng.If(has > 0):
                    body(e, rank, False)

        def gathered_at(q):
            return view(BIG, XGA + q // KT * 4 * D + q % KT * P, (D, 4), (1, P))

        def four(b):
            return b[:, :].rearrange("p (e s) -> p e s", e=4)

        def exp_gate(act, A, k, kk):
            b = k % 2
            act.wait_ge(sm("f_up"), kk + 1)
            if not (isinstance(kk, int) and kk < 2):
                act.wait_ge(sm("f_h"), kk - 1)
            A(view(SC, FE + b * FC, (1, FC)), bank[4 + b][:, 0:FC], ACT.Exp, scale=-1.0).then_inc(sm("f_exp"), 1)

        def copy_hT(act, A, k, kk):
            b = k % 2
            act.wait_ge(sm("f_tr"), kk + 1)
            A(view(SC, FHT + b * FC, (1, FC)), bank[6 + b][:, 0:FC], ACT.Copy).then_inc(sm("f_hT"), 1)

        block = es.enter_context(nc.Block())

        @block.sync
        def _(sp):
            def by_rows(n, it, w, col, width=WC):
                v = w.rearrange("(k p) n -> p k n", p=P)
                s = g_slot(n)
                for q in range(4):
                    if q % 2 == 0 and (n >= 2 or it is not None):
                        sp.wait_ge(g_free[2 * s + q // 2], n // 2 + (0 if it is None else it))
                    sp.dma_start(view(GW, (s * KT + 2 * q) * WC, (WC, 2), (1, width)),
                                 v[:, 2 * q:2 * q + 2, bass.ds(col, width)]).then_inc(g_loaded[2 * s + q // 2], 16)

            def gate_up(n, it, w, hidden, row, col):
                s = g_slot(n)
                for h in range(2):
                    sp.wait_ge(g_free[2 * s + h], n // 2 + (0 if it is None else it))
                    v = w[bass.ds(row + 512 * h, 512), :].rearrange("(k p) n -> p k n", p=P)
                    for c in range(2):
                        sp.dma_start(view(GW, (s * KT + 4 * h) * WC + FC * c, (WC, 4), (1, FC)),
                                     v[:, :, bass.ds(col + c * hidden, FC)]).then_inc(g_loaded[2 * s + h], 16)

            def down(m, units, w, row):
                s = m % 2
                if units is not None:
                    sp.wait_ge(sm("f_down"), units)
                src = w[bass.ds(row, FC), :].rearrange("(k p) n -> p k n", p=P)
                sp.dma_start(view(DW, s * 2 * D, (D, 2), (1, D)), src).then_inc(d_loaded[s], 16)

            for j in range(2):
                by_rows(j, None, w_ada[0], j * WC)
            with sp.Fori(1, N_ADA // 2) as it:
                for j in range(2):
                    by_rows(j, it, w_ada[0], it * 2 * WC + j * WC)
            for l in range(DEPTH):
                for i in range(N_IN):
                    by_rows(base["in", l] + i, None, w_in[l], i * WI, min(WI, NIN - i * WI))
                if l == 0:
                    with sp.Fori(0, N_ADA // 2) as it:
                        for j in range(2):
                            by_rows(base["ada", 1] + j, it, w_ada[1], it * 2 * WC + j * WC)
                for i in range(N_OUT):
                    by_rows(base["out", l] + i, None, w_out[l], i * WC)
                if l == 0:
                    for j in range(2):
                        gate_up(base["ff", 0] + j, None, ffn_w_gu[0], D_FF, 0, j * FC)
                        down(j, None, ffn_w_down[0], j * FC)
                    with sp.Fori(1, N_FF // 2) as it:
                        for j in range(2):
                            gate_up(base["ff", 0] + j, it, ffn_w_gu[0], D_FF, 0, it * 2 * FC + j * FC)
                            down(j, it * 2 * NT + (j - 1) * NT, ffn_w_down[0], it * 2 * FC + j * FC)
                    i = N_FF - 1
                    gate_up(base["ff", 0] + i, None, ffn_w_gu[0], D_FF, 0, i * FC)
                    down(i, (i - 1) * NT, ffn_w_down[0], i * FC)

            def experts(blk):
                n0, m0 = base["ff", 1] + blk * NE * N_EX, N_FF + blk * NE * N_EX
                gu = moe_w_gu[0].rearrange("e d n -> (e d) n")
                dn = moe_w_down[0].rearrange("e f n -> (e f) n")
                def body(e, r, more):
                    k0 = SF + blk * NE * N_EX
                    def gate(i, it=None):
                        at = r * (N_EX // 2) if it is None else r * (N_EX // 2) + it
                        col = i * FC if it is None else it * 2 * FC + i * FC
                        if isinstance(i, int) and i == N_EX:
                            gate_up(n0 + i, at, gu, D_EX, e * D + D, 0)
                            return
                        gate_up(n0 + i, at, gu, D_EX, e * D, col)

                    def dwn(i, it=None):
                        at = r * N_EX if it is None else r * N_EX + it * 2
                        row = e * D_EX + i * FC if it is None else e * D_EX + it * 2 * FC + i * FC
                        down(m0 + i, at + (k0 + i - 1), dn, row)

                    if blk:
                        gate(0)
                    with sp.Fori(0, N_EX // 2 - 1) as it:
                        for i in range(2):
                            gate(i + 1, it)
                            dwn(i, it)
                    gate(N_EX - 1)
                    dwn(N_EX - 2)
                    if more:
                        gate(N_EX)
                    dwn(N_EX - 1)

                if not blk:
                    gate_up(n0, 0, gu, D_EX, 0, 0)
                over_experts(sp, blk, body)

            experts(0)
            sp.wait_ge(sm("overflow_known"), 1)
            over = sp.value_load(RI[0:1, 0:1], min_val=0, max_val=1)
            with sp.If(over > 0):
                experts(1)
            for t in range(2):
                sp.wait_ge(sm("x_final"), t + 1)
                sp.dma_start(out[0, t * P:(t + 1) * P, :], xt(2 + t)).then_inc(sm("stored"), 16)
            sp.wait_ge(sm("stored"), 32)

        @block.gpsimd
        def _(pool):
            step = Steps(pool, pool_step)
            for l in range(DEPTH):
                if l == 0:
                    step(nc.gpsimd.memset(view(SC, SCT, (1, KT * 32)), 0.0))
                    nc.gpsimd.memset(view(PRM, pos["ib"], (1, 4)), 0.0).then_inc(sm("cleared"), 1)
                pool.wait_ge(sm("p_act"), 12 * (l + 1))
                pool.wait_ge(sm("p_dve"), 12 * (l + 1))
                nc.gpsimd.memset(view(SC, V1 + 64, (65, 16), (1, 1)), 1.0).then_inc(sm("v1"), 1)
                for t in range(NT):
                    ins = nc.gpsimd.tensor_copy(view(SC, V1 + t * 260, (65, 4), (1, 64)),
                                                view(BIG, t * NIN + C_MV, (64, 4), (1, 64)))
                    ins.then_inc(sm("v1"), 1)

        @block.scalar
        def _(act):
            step = Steps(act, act_step)
            A = nc.scalar.activation

            def load(dst, src):
                act.dma_start(dst, src).then_inc(params, 16)

            load(CS[:, :], consts)
            load(view(SC, 0, (1, P), np_=8), c_ctx.rearrange("(k p) -> k p", p=P))
            load(view(SC, 0, (1, P), p0=8, np_=8), c.rearrange("o (k p) -> (o k) p", p=P))
            load(view(SC, P, (1, P), np_=96), b_ada.rearrange("l (j p) -> (l j) p", p=P))
            load(view(SC, 2 * P, (1, P), np_=4), gla_gate_b.rearrange("l d k -> (l d) k"))
            load(view(SC, 3 * P, (1, P), np_=16), ln_w[0].rearrange("j (k p) -> (j k) p", p=P))
            load(view(SC, 4 * P, (1, P), np_=16), ln_b[0].rearrange("j (k p) -> (j k) p", p=P))
            load(prm("gup", (P, 4), (1, P), np_=RANK), gla_gate_up.rearrange("l d r k -> r (l d) k"))
            load(prm("sink", (1, 16)), attn_sink.rearrange("l h -> (l h)").partition_broadcast(P))
            load(prm("rb", (1, 8)), router_b[0].partition_broadcast(P))
            load(prm("rw", (8, 8), (1, 8)), router_w[0].rearrange("(k p) e -> p k e", p=P))
            for l in range(DEPTH):
                load(view(NW, l * 512, (1, 256)), mlstm_norm_w[l].partition_broadcast(P))
                load(view(NW, l * 512 + 256, (1, 256)), gla_norm_w[l].partition_broadcast(P))
            act.wait_ge(sm("cleared"), 1)
            with nc.allow_non_contiguous_dma(reason="gate biases, a few bytes"):
                for l in range(DEPTH):
                    for g in range(2):
                        for d in range(2):
                            load(prm("ib", (1, 1), off=2 * l + g, p0=32 * d, np_=4),
                                 mlstm_gate_b[l, d, g].rearrange("(h o) -> h o", o=1))

            for t in range(NT):
                src = (ctx_in if t < 2 else x)[0, (t % 2) * P:(t % 2 + 1) * P, :]
                act.dma_start(xt(t), src).then_inc(sm("x_loaded"), 16)

            def ln_rows(i):
                l, j = divmod(i, 2)
                if i:
                    act.wait_ge(sm("ln_used"), i)
                act.dma_start(view(LNR, 0, (1, D)), ln_w[l, j].partition_broadcast(P)).then_inc(sm("ln_rows"), 16)
                act.dma_start(view(LNR, D, (1, D)), ln_b[l, j].partition_broadcast(P)).then_inc(sm("ln_rows"), 16)

            ln_rows(0)
            act.wait_ge(sm("c_col"), 1)
            A(prm("ecol", (1, 16)), prm("ccol", (1, 16)), ACT.Exp, scale=-1.0).then_inc(sm("c_exp"), 1)
            with act.Fori(0, N_ADA // 2) as it:
                    for j in range(2):
                        act.wait_ge(sm("ada_mm"), it * 2 + (j + 1))
                        A(view(SC, ADAR + j * 512, (1, 512)), bank[j][:, :], ACT.Copy).then_inc(sm("ada_row"), 1)

            def gate_rows(i):
                for s in range(2):
                    for half in range(2):
                        k = i * 4 + s * 2 + half
                        act.wait_ge(sm("gate_mm"), k + 1)
                        A(view(GATE, s * D + half * 512, (1, 512)), bank[6 + half][:, :], ACT.Copy).then_inc(sm("gate_row"), 1)

            def h_context(u):
                for kt in range(KT):
                    act.wait_ge(sm("x_T"), u * KT + kt + 1)
                    A(view(HT, kt * 512, (1, 256)), bank[kt % 2][:, 0:256], ACT.Identity,
                      scale=column(u, 1, kt, 0), bias=column(u, 0, kt, 0)).then_inc(sm("h_ctx"), 1)
                    act.wait_ge(sm("h_ctx"), u * KT + kt + 1)
                    act.wait_ge(sm("h_lat"), u * KT + kt + 1)
                    A(tokens_hi(u, kt), view(HT, kt * 512, (1, 512)), ACT.Copy).then_inc(sm("h_hi"), 1)

            def slots_context(blk):
                for b in range(4):
                    act.wait_ge(sm("sw_T"), 4 * blk + b + 1)
                    A(view(SC, CWA + b * 512, (1, 512)), bank[b][:, :], ACT.Copy).then_inc(sm("sw_copy"), 1)
            def gathered(n):
                act.wait_ge(sm("gx_mm"), n)
                for q in range(4):
                    ins = A(view(BIG, XGA + q * P, (1, P)), bank[4][:, q * P:(q + 1) * P], ACT.Identity,
                            scale=mod(1, 4, q, 1), bias=mod(1, 3, q, 1))
                ins.then_inc(sm("gx_a"), 1)

            def experts(blk):
                if blk:
                    slots_context(blk)
                k0 = SF + blk * NE * N_EX
                n0 = base["ff", 1] + blk * NE * N_EX

                def tokens(e):
                    A(rview(SC, XGS, (1, D)), BIG[:, bass.ds(e * D + XGA, D)], ACT.Copy).then_inc(sm("x_hi"), 1)

                def two_chunks(moved):
                    for i in range(2):
                        for half in range(2):
                            write_hi(act, "ex", n0 + i, moved, half)

                def body(e, r, more):
                    st = {"moved": r * (N_EX // 2)}
                    if blk:
                        two_chunks(st["moved"])
                        gathered(r + (2 * NE + 1))
                        act.wait_ge(sm("gx_a"), r + (NE + 1))
                        act.wait_ge(sm("gx_d"), r + (NE + 1))
                        tokens(0)

                    def high(k, half):
                        if more or k - k0 + 2 < N_EX:
                            write_hi(act, "ex", n0 + k - k0 + 2, st["moved"], half)

                    def step(k, kk):
                        if k != k0:
                            high(k, 0)
                        copy_hT(act, A, k, kk)
                        exp_gate(act, A, k + 1, kk + 1)
                        if k == k0:
                            high(k, 0)
                        high(k, 1)

                    def last(k, kk):
                        if more:
                            tokens(e + 1)
                        copy_hT(act, A, k, kk)
                        act.wait_ge(sm("f_down"), r * N_EX + (k0 + N_EX))
                        for half in range(2):
                            A(view(SC, YE + half * 512, (1, 512)), bank[half][:, :], ACT.Copy).then_inc(sm("ye"), 1)
                        high(k, 0)
                        high(k, 1)

                    def inner(it):
                        st["moved"] = r * (N_EX // 2) if it is None else r * (N_EX // 2) + it

                    one_expert(act, k0, r, lambda k, kk: exp_gate(act, A, k, kk), step, last, inner)

                if not blk:
                    for c, half in ((0, 0), (0, 1), (1, 0)):
                        write_hi(act, "ex", n0 + c, 0, half)
                    for q in range(0, 2 * NE, 2):
                        act.wait_ge(sm("gx_mm"), q + 1)
                        A(gathered_at(q), four(bank[4 + q % 4]), ACT.Identity, scale=mod(1, 4, q % KT, 1),
                          bias=mod(1, 3, q % KT, 1)).then_inc(sm("gx_a"), 1)
                    act.wait_ge(sm("gx_a"), NE)
                    act.wait_ge(sm("gx_d"), NE)
                    tokens(0)
                    write_hi(act, "ex", n0 + 1, 0, 1)
                    slots_context(0)
                over_experts(act, blk, body)

            def rstd(src, dst, scale):
                step(A(dst, src, ACT.Ln, scale=scale, bias=view(ST, 500, (1, 1))))
                return A(dst, dst, ACT.Exp, scale=-0.5)

            def normalise(i):
                nto = N_TO[i // 2]
                act.wait_ge(sm("r_var"), i + 1)
                step(rstd(view(ST, 65, (2, nto)), view(ST, 80, (1, nto)), 1.0))
                for n in range(nto):
                    step(A(view(ST, 84 + n, (1, 1)), view(ST, 84 + n, (1, 1)), ACT.Copy, scale=view(ST, 80 + n, (1, 1))))
                    A(xt(n) if i < 2 else ysum(n), ysum(n), ACT.Identity, scale=view(ST, 80 + n, (1, 1)),
                      bias=view(ST, 84 + n, (1, 1))).then_inc(sm("r_norm"), 1)

            for l in range(DEPTH):
                nto = N_TO[l]
                t0 = OUTS[l][0]
                gate_rows(2 * l)
                h_context(2 * l)
                for chunk in range(2):
                    for half in range(2):
                        write_hi(act, "in", base["in", l] + chunk, None, half, WI)
                for g in range(0, N_IN * NT, 2):
                    cchunk, t = divmod(g, NT)
                    a, w = columns(l, t, cchunk)
                    act.wait_ge(sm("p_mm"), l * N_IN * NT + g + 1)
                    A(big(t, cchunk * WI + a, w), bank[4 + g % 4][:, 0:w], ACT.Copy).then_inc(sm("p_act"), 1)
                    if t == 0 and 1 <= cchunk < N_IN - 1:
                        for half in range(2):
                            write_hi(act, "in", base["in", l] + cchunk + 1, None, half, min(WI, NIN - (cchunk + 1) * WI))
                for g in range(2):
                    act.wait_ge(sm("m_T"), l * 6 + g + 1)
                    A(view(SC, ROWI + g * 512, (1, 512), np_=64), bank[g][0:64, :], ACT.Identity,
                      bias=prm("ib", (1, 1), off=2 * l + g, np_=64)).then_inc(sm("gates"), 1)
                for g in range(2):
                    act.wait_ge(sm("m_T"), l * 6 + g + 3)
                    A(view(SC, MQT + g * 512 + t0 * P, (1, nto * P)), bank[2 + g][:, t0 * P:512], ACT.Copy).then_inc(sm("mq_T"), 1)
                act.wait_ge(sm("f_abs"), l + 1)
                r = view(SC, ROWT, (1, 512), np_=64)
                step(A(r, r, ACT.Exp))
                A(r, r, ACT.Ln, bias=1.0).then_inc(sm("f_ln"), 1)
                act.wait_ge(sm("gate_rows_ready"), l + 1)
                A(r, r, ACT.Exp).then_inc(sm("floor_row"), 1)
                act.wait_ge(sm("gates_T"), l + 1)
                step(A(view(SC, ACOL, (1, 256)), bank[0][:, 0:256], ACT.Copy, scale=-1.0))
                A(view(SC, ACOL + 256, (1, 256)), bank[0][:, 256:512], ACT.Copy).then_inc(sm("gate_cols"), 1)
                for u in range(8):
                    h, d = divmod(u, 2)
                    act.wait_ge(sm("m_bc"), 8 * l + u + 1)
                    if 8 * l + u >= 2:
                        act.wait_ge(sm("m_pv"), 8 * l + u - 1)
                    for j in range(4):
                        a, n = (t0 * P, nto * P) if j < 2 else (256, 256)
                        step(A(view(SC, MD + d * 2048 + j * 512 + a, (1, n)), bank[4 + d][:, a:a + n], ACT.Relu,
                               bias=view(SC, ACOL + j * 64 + d * 32 + h, (1, 1))))
                    v = view(SC, MD + d * 2048 + t0 * P, (512, 2), (1, nto * P))
                    step(A(v, v, ACT.Exp, scale=-1.0))
                    v = view(SC, MD + d * 2048 + 1280, (512, 2), (1, 256))
                    A(v, v, ACT.Exp, scale=-1.0).then_inc(sm("m_decay"), 1)
                for j in range(6):
                    act.wait_ge(sm("a_T"), l * 6 + j + 1)
                    a = 256 if (j < 4 and l == DEPTH - 1) else 0
                    A(view(HT, AQT + j * 512 + a, (1, 512 - a)), bank[j][:, a:512], ACT.Copy,
                      scale=0.125 if j < 4 else 1.0).then_inc(sm("a_qk"), 1)
                off = sum(N_ATT[:l])
                for k in range(N_ATT[l] + 1):
                    if k < N_ATT[l]:
                        i, j, half = ATT[l][k]
                        n = 256 if i < 2 else 512
                        b = k % 2
                        act.wait_ge(sm("a_max"), off + k + 1)
                        if k >= 2:
                            act.wait_ge(sm("a_pT"), off + k - 1)
                            act.wait_ge(sm("a_out"), off + k - 1)
                        A(view(HT, AP_ + b * 512, (1, n)), bank[b][:, 0:n], ACT.Exp, bias=view(ST, 100 + b, (1, 1)),
                          accum_out=view(ST, 102 + b, (1, 1))).then_inc(sm("a_exp"), 1)
                        A(view(ST, 104 + b, (1, 1)), prm("sink", (1, 1), off=l * 8 + 2 * j + half), ACT.Exp,
                          bias=view(ST, 100 + b, (1, 1))).then_inc(sm("a_exp"), 1)
                    if k >= 1:
                        k1 = k - 1
                        n = 256 if ATT[l][k1][0] < 2 else 512
                        act.wait_ge(sm("a_pT"), off + k1 + 1)
                        if k1 >= 2:
                            act.wait_ge(sm("a_pv"), off + k1 - 1)
                        A(view(SC, APT + (k1 % 2) * 512, (1, n)), bank[2 + k1 % 2][:, 0:n], ACT.Copy).then_inc(sm("a_pTs"), 1)
                    if k % 8 == 1 and k // 8 < nto:
                        t = OUTS[l][k // 8]
                        if l or k > 8:
                            act.wait_ge(sm("n_gate_free"), sum(N_TO[:l]) + k // 8)
                        A(big(t, C_MO, 256), big(t, C_MO, 256), ACT.Exp, scale=-1.0)
                        A(view(SC, NG, (1, 256)), big(t, C_GG, 256), ACT.Exp, scale=-1.0).then_inc(sm("n_gate"), 1)
                    if l == 0 and ada_after(k - 1) is not None:
                        act.wait_ge(sm("ada_mm"), N_ADA + ada_after(k - 1) + 1)
                        A(view(SC, ADAL, (1, 512)), bank[6][:, :], ACT.Copy).then_inc(sm("ada_row"), 1)
                for g in range(2):
                    act.wait_ge(sm("g_T"), l * 4 + g + 1)
                    A(view(SC, GQT + g * 512, (1, 512)), bank[g][:, :], ACT.Copy,
                      scale=float(np.float32(DK ** -0.5)) if g == 0 else 1.0).then_inc(sm("g_qk"), 1)
                for d in range(2):
                    act.wait_ge(sm("g_z"), 2 * l + d + 1)
                    A(view(SC, GLG + d * 512, (1, 512)), bank[4 + d][:, :], ACT.Identity,
                      bias=prm("gb", (1, 1), off=2 * l + d)).then_inc(sm("g_zb"), 1)
                act.wait_ge(sm("g_abs"), l + 1)
                r = view(SC, GTMP, (1, 1024))
                step(A(r, r, ACT.Exp))
                A(r, r, ACT.Ln, bias=1.0).then_inc(sm("g_ln"), 1)
                act.wait_ge(sm("g_cum"), l + 1)
                A(view(SC, GEB, (1, 1024)), view(SC, GB_, (1, 1024)), ACT.Exp, scale=1 / 16).then_inc(sm("g_eb"), 1)
                A(view(SC, GNB, (1, 1024)), view(SC, GB_, (1, 1024)), ACT.Exp, scale=-1 / 16).then_inc(sm("g_eb"), 1)
                act.wait_ge(sm("g_rest"), l + 1)
                A(view(SC, GKD, (1, 1024)), view(SC, GKD, (1, 1024)), ACT.Exp, scale=1 / 16).then_inc(sm("g_eb"), 1)
                for d in range(2):
                    act.wait_ge(sm("g_kT"), 2 * l + d + 1)
                    A(view(SC, GKT + d * 512, (1, 512)), bank[6 + d][:, :], ACT.Copy).then_inc(sm("g_ktok"), 1)
                for d in range(2):
                    act.wait_ge(sm("g_a"), 2 * l + d + 1)
                    if d == 1:
                        act.wait_ge(sm("g_pv"), 2 * l + 1)
                    for h in range(4):
                        ins = A(view(SC, GAT + h * 512, (1, 512)), bank[4 + h][:, :], ACT.Copy)
                    ins.then_inc(sm("g_acopy"), 1)
                if l:
                    ln_rows(2)
                act.wait_ge(sm("n_var"), l + 1)
                rstd(view(ST, SSQ, (1, 8 * nto)), view(ST, RST, (1, 8 * nto)), 1 / HD).then_inc(sm("n_rstd"), 1)
                for kt in range(0, KT, 2):
                    act.wait_ge(sm("c_T"), l * KT + kt + 1)
                    A(view(HT, kt * 512 + t0 * P, (1, nto * P)), bank[kt % 4][:, t0 * P:512], ACT.Copy).then_inc(sm("c_act"), 1)
                normalise(2 * l)
                if l:
                    ln_rows(3)
                gate_rows(2 * l + 1)
                if l == 0:
                    h_context(1)
                    state = {"it": None}

                    def write_down_hi(m, moved):
                        act.wait_ge(d_loaded[m % 2], 16 * (m // 2 + 1) + (0 if moved is None else moved * 16))
                        t, o = ((BIG, 8192), (SC, 10240))[m % 2]
                        A(rview(t, o, (1, 2 * D)), view(DW, (m % 2) * 2 * D, (1, 2 * D)), ACT.Copy).then_inc(sm("dw_hi"), 1)

                    for half in range(2):
                        write_hi(act, "ff", base["ff", 0], None, half)
                    write_down_hi(0, None)

                    def exp(k, kk):
                        exp_gate(act, A, k, kk)
                        if k % NT and k < (N_FF - 1) * NT:
                            m = k // NT + 1
                            moved = None if isinstance(kk, int) else state["it"]
                            if k % NT < 3:
                                write_hi(act, "ff", base["ff", 0] + m, moved, k % NT - 1)
                            else:
                                write_down_hi(m, moved)

                    def hT(k, kk):
                        act.wait_ge(sm("f_tr"), kk + 1)
                        A(rview(SC, FHT + (k % 2) * FC, (1, FC)), bank[6 + k % 2][:, 0:FC], ACT.Copy).then_inc(sm("f_hT"), 1)

                    in_pairs(act, exp, hT, lambda it: state.update(it=it), swap=True)
                    ln_rows(1)
                else:
                    act.wait_ge(sm("x_ready"), X_READY[2] + 2)
                    A(rview(SC, XSH, (1, 2 * D)), view(X, 2 * D, (1, 2 * D)), ACT.Copy).then_inc(sm("xs_hi"), 1)
                    act.wait_ge(sm("r_diff"), 1)
                    A(view(ST, 136, (1, 2)), view(ST, 136, (1, 2)), ACT.Exp).then_inc(sm("r_exp"), 1)
                    experts(0)
                    act.wait_ge(sm("overflow_known"), 1)
                    over = act.value_load(RI[0:1, 0:1], min_val=0, max_val=1)
                    with act.If(over > 0):
                        experts(1)
                normalise(2 * l + 1)

        @block.vector
        def _(dve):
            V = nc.vector
            step = Steps(dve, dve_step)

            def signal(ins, name, total):
                ins.then_inc(sm(name), 1)
                dve.wait_ge(sm(name), total)

            step(V.memset(view(ST, 500, (1, 1)), EPS))
            dve.wait_ge(sm("start_T"), 1)
            dve.wait_ge(sm("cleared"), 1)
            step(V.tensor_copy(prm("ccol", (1, 16)), bank[0][:, 0:16]))
            for s in range(2):
                step(V.tensor_copy(prm("bada", (2, 96), off=s), bank[0][:, 16:112]))
            step(V.tensor_copy(view(ST, LNC, (1, 32)), bank[0][:, 116:148]))
            V.tensor_copy(prm("gb", (1, 4)), bank[0][:, 112:116]).then_inc(sm("c_col"), 1)
            dve.wait_ge(sm("c_exp"), 1)
            e = prm("ecol", (1, 16))
            step(V.tensor_scalar(e, e, 1.0, None, ALU.add))
            step(V.reciprocal(e, e))
            V.tensor_tensor(view(SC, SCT, (1, 2), (32, KT)), prm("ccol", (8, 2), (1, 8)), prm("ecol", (8, 2), (1, 8)),
                            ALU.mult).then_inc(sm("sct"), 1)
            with dve.Fori(0, N_ADA // 2) as it:
                for j in range(2):
                    dve.wait_ge(sm("ada_col"), it * 2 + (j + 1))
                    o = it * 16 + j * 8
                    V.tensor_tensor(MOD[:, bass.ds(o, 8)], bank[2 + j][:, 0:8],
                                    PRM[:, bass.ds(o + pos["bada"], 8)], ALU.add).then_inc(sm("mod"), 1)

            def scales(l):
                dve.wait_ge(sm("mod"), (l + 1) * N_ADA)
                v = view(MOD, l * 96 + 16, (48, 2), (1, 16))
                step(V.tensor_scalar(v, v, 1.0, None, ALU.add))
                u, six = ((1, 3), (2, 0))[l]
                scale = view(MOD, (l * 48 + (six + 1) * 8) * 2, (2, 8), (1, 2))
                shift = view(MOD, (l * 48 + six * 8) * 2, (2, 8), (1, 2))
                w, b = (view(ST, LNC + 16 * q + 8 * l, (1, 8), (0, 2)) for q in range(2))
                both = [view(ST, MC[u] + 16 * q, (2, 8), (1, 2)) for q in range(2)]
                step(V.tensor_tensor(both[0], scale, w, ALU.mult))
                step(V.tensor_tensor(both[1], scale, b, ALU.mult))
                signal(V.tensor_tensor(both[1], both[1], shift, ALU.add), "mods", l + 1)

            scales(0)

            def diagonals(i):
                l, j = divmod(i, 2)
                for s in range(2):
                    for half in range(2):
                        k = i * 4 + s * 2 + half
                        if k >= 2:
                            dve.wait_ge(sm("gate_mm"), k - 1)
                        for q in range(4):
                            ins = V.tensor_scalar(view(DIAG[j][0], DIAG[j][1] + half * 512 + q * P, (1, P)), ident,
                                                  mod(l, 3 * j + 2, half * 4 + q, s), None, ALU.mult)
                        ins.then_inc(sm("diag"), 1)

            def h_latent(u, split):
                def low(kt):
                    dve.wait_ge(sm("h_hi"), u * KT + kt + 1)
                    at = (HT, kt * 512, (1, 512))
                    V.tensor_tensor(rview(*at), view(*at), tokens_hi(u, kt).bitcast(F32), ALU.subtract).then_inc(sm("h_lo"), 1)

                for kt in range(KT):
                    dve.wait_ge(sm("x_T"), u * KT + kt + 1)
                    V.tensor_scalar(view(HT, kt * 512 + 256, (1, 256)), bank[2 + kt % 2][:, 256:512],
                                    column(u, 1, kt, 1), column(u, 0, kt, 1), ALU.mult, ALU.add).then_inc(sm("h_lat"), 1)
                    if split and kt:
                        low(kt - 1)
                if split:
                    low(KT - 1)

            def affine(i, n, t, src):
                dve.wait_ge(sm("ln_rows"), 32 * (i + 1))
                dve.wait_ge(sm("r_norm"), NORMED[i] + OUTS[i // 2].index(t) + 1)
                step(V.tensor_tensor(src, src, view(LNR, 0, (1, D)), ALU.mult))
                ins = V.tensor_tensor(xt(t), src, view(LNR, D, (1, D)), ALU.add)
                if i == 3:
                    signal(ins, "x_final", n + 1)
                else:
                    signal(ins, "x_ready", X_READY[i] + n + 1)

            def ln_rows_used():
                V.memset(view(ST, 501, (1, 1)), 0.0).then_inc(sm("ln_used"), 1)

            def layer_norm(i, from_psum):
                l = i // 2
                outs = OUTS[l]

                dve.wait_ge(sm("gate_row"), 4 * (i + 1))
                for n, t in enumerate(outs):
                    g = view(GATE, (t // 2) * D, (1, D))
                    if from_psum:
                        for cc in range(2):
                            dve.wait_ge(sm("o_mm"), sum(2 * m for m in N_TO[:l]) + cc * len(outs) + n + 1)
                            step(V.tensor_tensor(ysum(n, cc * 512, 512), bank[t * 2 + cc][:, :],
                                                 view(GATE, (t // 2) * D + cc * 512, (1, 512)), ALU.mult))
                    else:
                        step(V.tensor_tensor(ysum(n), ysum(n), g, ALU.mult))
                    step(V.scalar_tensor_tensor(ysum(n), xt(t), ALPHA, ysum(n), ALU.mult, ALU.add))
                    for cc in range(2):
                        step(V.bn_stats(view(ST, 240 + 6 * cc, (1, 6)), ysum(n, cc * 512, 512)))
                    step(V.bn_aggr(view(ST, 64 + 2 * n, (1, 2)), view(ST, 240, (1, 12))))
                V.tensor_scalar(view(ST, 84, (1, len(outs))), view(ST, 64, (2, len(outs))), -1.0, None,
                                ALU.mult).then_inc(sm("r_var"), 1)
                if i >= 2:
                    for n, t in enumerate(outs):
                        affine(i, n, t, ysum(n))
                    ln_rows_used()

            def scans(dst, off_src, op0, op1, cumulate):
                def go(p0, o, n, initial):
                    s = 1 if p0 == 0 else -1
                    src = view(SC, off_src + o, (s, n), p0=p0, np_=32)
                    first = view(CS, C_AT["ones"][0], (0, n), p0=p0, np_=32) if cumulate else src
                    step(V.tensor_tensor_scan(view(SC, dst + o, (s, n), p0=p0, np_=32), first, src, initial, op0, op1))
                go(0, 0, 512, 0.0)
                go(32, 255, 256, 0.0)
                go(32, 511, 256, view(SC, dst, (1, 1), p0=32, np_=32))

            def mask(name, k):
                o, w = C_AT[name]
                v = view(CS, o, (0, k), (1, P))
                return v.bitcast(U32)

            def zeros(k):
                return view(CS, C_AT["zeros"][0], (0, k), (0, P))

            for l in range(DEPTH):
                outs = OUTS[l]
                nto = len(outs)
                t0 = outs[0]
                last = l == DEPTH - 1
                diagonals(2 * l)
                h_latent(2 * l, True)
                for c in range(2):
                    for half in range(2):
                        write_lo(dve, "in", base["in", l] + c, split_base["in", l] + c, None, half, WI)
                if l == 1:
                    for n, t in enumerate((2, 3)):
                        affine(1, n, t, xt(t))
                    ln_rows_used()
                for g in range(1, N_IN * NT, 2):
                    cchunk, t = divmod(g, NT)
                    a, w = columns(l, t, cchunk)
                    dve.wait_ge(sm("p_mm"), l * N_IN * NT + g + 1)
                    V.tensor_copy(big(t, cchunk * WI + a, w), bank[4 + g % 4][:, 0:w]).then_inc(sm("p_dve"), 1)
                    if t == 1 and 1 <= cchunk < N_IN - 1:
                        c = cchunk + 1
                        for half in range(2):
                            write_lo(dve, "in", base["in", l] + c, split_base["in", l] + c, None, half, min(WI, NIN - c * WI))
                dve.wait_ge(sm("gates"), 2 * l + 2)
                rf, rt = (view(SC, o, (1, 512), np_=64) for o in (ROWF, ROWT))
                V.scalar_tensor_tensor(rt, rf, -1.0, rf, ALU.mult, ALU.min).then_inc(sm("f_abs"), 1)
                for g in range(2):
                    dve.wait_ge(sm("m_T"), l * 6 + 5 + g)
                    V.tensor_scalar(view(SC, MKT + g * 512, (1, 512)), bank[4 + g][:, :], HD ** -0.5, None,
                                    ALU.mult).then_inc(sm("mk_T"), 1)
                dve.wait_ge(sm("p_act"), 12 * (l + 1))
                dve.wait_ge(sm("p_dve"), 12 * (l + 1))
                for t in (2, 3):
                    for jj in range(2):
                        step(V.tensor_tensor(view(SC, ROT + jj * 16, (64, 10), (32, 2), (1, 16)),
                                             view(BIG, t * NIN + C_AQ + (1 - jj) * 16, (64, 10), (32, 2), (1, 16)),
                                             view(CS, C_AT["sin"][0] + (t - 2) * 64 + jj * 16, (0, 10), (32, 2), (1, 16)),
                                             ALU.mult))
                    v = view(BIG, t * NIN + C_AQ, (64, 10), (1, 64))
                    step(V.tensor_tensor(v, v, view(CS, C_AT["cos"][0] + (t - 2) * 64, (0, 10), (1, 64)), ALU.mult))
                    v = view(BIG, t * NIN + C_AQ, (1, 640))
                    V.tensor_tensor(v, v, view(SC, ROT, (1, 640)), ALU.add).then_inc(sm("rope"), 1)
                    dve.wait_ge(sm("rope"), 2 * l + t - 1)
                dve.wait_ge(sm("f_ln"), l + 1)
                step(V.scalar_tensor_tensor(rf, rf, 0.0, rt, ALU.min, ALU.subtract))
                scans(ROWB, ROWF, ALU.mult, ALU.add, True)
                ra, rb_, rm, ri = (view(SC, o, (1, 512), np_=64) for o in (ROWA, ROWB, ROWM, ROWI))
                step(V.tensor_tensor(ra, ri, rb_, ALU.subtract))
                scans(ROWM, ROWA, ALU.max, ALU.max, False)
                V.scalar_tensor_tensor(rt, rb_, -1.0, rm, ALU.mult, ALU.subtract).then_inc(sm("gate_rows_ready"), 1)

                def weigh(u):
                    h, d = divmod(u, 2)
                    o = MD + d * 2048
                    dve.wait_ge(sm("m_decay"), 8 * l + u + 1)
                    step(V.copy_predicated(view(SC, o + t0 * 640, (640, nto), (1, P)), mask(("not_fwd", "not_bwd")[d], nto),
                                           zeros(nto)))
                    dve.wait_ge(sm("m_s"), 4 * l + h + 1)
                    for j in range(2):
                        v = view(SC, o + j * 512 + t0 * P, (1, nto * P))
                        V.tensor_tensor(v, v, bank[1 + j][:, t0 * P:512], ALU.mult).then_inc(sm("m_w"), 1)
                    v = view(SC, o + 2 * 512 + 256, (512, 2), (1, 256))
                    V.tensor_tensor(v, v, bank[3][:, :].rearrange("p (a b) -> p a b", a=2), ALU.mult).then_inc(sm("m_w"), 1)

                def normalise(u):
                    h, d = divmod(u, 2)
                    dve.wait_ge(sm("m_pv"), 8 * l + u + 1)
                    pv = bank[6 + d][:, t0 * 65:260].rearrange("p (t c) -> p t c", c=65)
                    den = view(ST, 440, (1, nto))
                    dve.wait_ge(sm("gate_cols"), l + 1)
                    step(V.tensor_tensor(den, pv[:, :, 64], view(SC, ACOL + 256 + t0 * 64 + d * 32 + h, (64, nto)), ALU.max))
                    step(V.scalar_tensor_tensor(den, pv[:, :, 64], -1.0, den, ALU.mult, ALU.max))
                    step(V.reciprocal(den, den))
                    r = view(ST, 440, (1, nto), (0, 64))
                    dst = bigs(t0, nto, C_MQ + h * 64, (1, 64))
                    if d == 0:
                        signal(V.tensor_tensor(dst, pv[:, :, 0:64], r, ALU.mult), "m_hs", 8 * l + u + 1)
                    else:
                        tmp = view(SC, MT, (64, nto), (1, 64))
                        step(V.tensor_tensor(tmp, pv[:, :, 0:64], r, ALU.mult))
                        signal(V.tensor_tensor(dst, dst, tmp, ALU.add), "m_hs", 8 * l + u + 1)

                for u in range(9):
                    if u < 8:
                        weigh(u)
                    if u >= 1:
                        normalise(u - 1)
                def centre(x, dst, sq, q):
                    mean = view(ST, 16, (1, 4))
                    step(V.tensor_reduce(mean, x, AX, ALU.add))
                    step(V.tensor_scalar(mean, mean, 1.0 / HD, None, ALU.mult))
                    step(V.tensor_tensor(dst, x, view(ST, 16, (1, 4), (0, 64)), ALU.subtract))
                    step(V.tensor_tensor(sq, dst, dst, ALU.mult))
                    step(V.tensor_reduce(view(ST, SSQ + 4 * q, (1, 4)), sq, AX, ALU.add))

                off = sum(N_ATT[:l])
                for k in range(N_ATT[l] + 2):
                    if k < N_ATT[l]:
                        i, j, half = ATT[l][k]
                        b = k % 2
                        dve.wait_ge(sm("a_s"), off + k + 1)
                        step(V.tensor_reduce(view(ST, 106 + b, (1, 1)), bank[b][:, 0:256 if i < 2 else 512], AX, ALU.max))
                        V.tensor_scalar(view(ST, 100 + b, (1, 1)), view(ST, 106 + b, (1, 1)),
                                        prm("sink", (1, 1), off=l * 8 + 2 * j + half), -1.0, ALU.max,
                                        ALU.mult).then_inc(sm("a_max"), 1)
                    if k >= 2:
                        i, j, half = ATT[l][k - 2]
                        b = k % 2
                        dve.wait_ge(sm("a_pv"), off + k - 1)
                        den = view(ST, 108 + b, (1, 1))
                        V.tensor_scalar(big(i, C_AQ + (2 * j + half) * 64, 64), bank[4 + b][:, 0:64], den, None,
                                        ALU.mult).then_inc(sm("a_o"), 1)
                    if k >= 1 and k - 1 < N_ATT[l]:
                        b = (k - 1) % 2
                        dve.wait_ge(sm("a_exp"), 2 * (off + k))
                        den = view(ST, 108 + b, (1, 1))
                        step(V.tensor_tensor(den, view(ST, 102 + b, (1, 1)), view(ST, 104 + b, (1, 1)), ALU.add))
                        signal(V.reciprocal(den, den), "a_out", off + k)
                    n, part = divmod(k, 8)
                    if n < nto:
                        t = outs[n]
                        xm = view(BIG, t * NIN + C_MQ, (64, 4), (1, 64))
                        flat, gm, gg = big(t, C_MQ, 256), big(t, C_MO, 256), view(SC, NG, (1, 256))
                        if part == 0:
                            centre(xm, xm, view(SC, NSQM, (64, 4), (1, 64)), n)
                        if part == 3:
                            dve.wait_ge(sm("n_gate"), sum(N_TO[:l]) + n + 1)
                            step(V.tensor_scalar(gm, gm, 1.0, None, ALU.add))
                            step(V.reciprocal(gm, gm))
                        if part == 5:
                            step(V.tensor_scalar(gg, gg, 1.0, None, ALU.add))
                            step(V.reciprocal(gg, gg))
                            V.tensor_tensor(big(t, C_GG, 256), gg, big(t, C_GG, 256), ALU.mult).then_inc(sm("n_gate_free"), 1)
                        if part == 7:
                            step(V.tensor_tensor(flat, flat, view(NW, l * 512, (1, 256)), ALU.mult))
                            step(V.tensor_tensor(flat, flat, gm, ALU.mult))
                    if l == 0 and ada_after(k - 3) is not None:
                        c1 = ada_after(k - 3)
                        dve.wait_ge(sm("ada_col"), N_ADA + c1 + 1)
                        V.tensor_tensor(view(MOD, 96 + c1 * 8, (1, 8)), bank[7][:, 0:8], prm("bada", (1, 8), off=96 + c1 * 8),
                                        ALU.add).then_inc(sm("mod"), 1)
                if l == 0:
                    scales(1)
                for d in range(2):
                    dve.wait_ge(sm("g_T"), 4 * l + 3 + d)
                    V.tensor_copy(view(SC, GRT + d * 512, (1, 512), np_=16), bank[2 + d][0:16, :]).then_inc(sm("g_r"), 1)
                dve.wait_ge(sm("g_zb"), 2 * l + 2)
                lg, tmp = view(SC, GLG, (1, 1024)), view(SC, GTMP, (1, 1024))
                V.scalar_tensor_tensor(tmp, lg, -1.0, lg, ALU.mult, ALU.min).then_inc(sm("g_abs"), 1)
                dve.wait_ge(sm("g_ln"), l + 1)
                step(V.scalar_tensor_tensor(lg, lg, 0.0, tmp, ALU.min, ALU.subtract))
                reset = cst("reset")
                step(V.tensor_tensor_scan(view(SC, GB_, (1, 512)), reset, view(SC, GLG, (1, 512)), 0.0, ALU.mult, ALU.add))
                signal(V.tensor_tensor_scan(view(SC, GB_ + 1023, (-1, 512)), reset, view(SC, GLG + 1023, (-1, 512)), 0.0,
                                            ALU.mult, ALU.add), "g_cum", l + 1)
                for d in range(2):
                    last_b = view(SC, GB_ + (63 if d == 0 else 512), (64, 8), (0, 64))
                    step(V.tensor_tensor(view(SC, GKD + d * 512, (64, 8), (1, 64)), last_b,
                                         view(SC, GB_ + d * 512, (64, 8), (1, 64)), ALU.subtract))
                V.memset(view(ST, 501, (1, 1)), 0.0).then_inc(sm("g_rest"), 1)
                dve.wait_ge(sm("g_eb"), 3 * (l + 1))
                for d in range(2):
                    step(V.tensor_copy(view(SC, GEL + d * 8, (1, 8)), view(SC, GEB + (63 if d == 0 else 512), (64, 8))))
                dve.wait_ge(sm("g_qk"), 2 * (l + 1))
                for dst, src in ((GKD, GKF), (GNB, GKF), (GEB, GQT)):
                    v = view(SC, dst, (512, 2), (1, 512))
                    V.tensor_tensor(v, v, view(SC, src, (0, 2), (1, 512)), ALU.mult).then_inc(sm("g_prod"), 1)
                for q in range(14):
                    k, d = divmod(q, 2)
                    n = 14 * l + q + 1
                    dve.wait_ge(sm("g_kv"), n)
                    new = view(SC, GS + (d * 7 + k + 1) * 256, (1, 256))
                    if k == 0:
                        signal(V.tensor_tensor(new, bank[q % 4][:, 0:256], cst("blocks"), ALU.mult), "g_st", n)
                        continue
                    kv = view(SC, GKV, (1, 256))
                    step(V.tensor_tensor(kv, bank[q % 4][:, 0:256], cst("blocks"), ALU.mult))
                    signal(V.scalar_tensor_tensor(new, view(SC, GS + (d * 7 + k) * 256, (1, 256)),
                                                  view(SC, GEL + d * 8 + chunk_of(d, k), (1, 1)), kv, ALU.mult, ALU.add),
                           "g_st", n)
                for d in range(2):
                    dve.wait_ge(sm("g_acopy"), 2 * l + d + 1)
                    V.copy_predicated(view(SC, GAT, (P, 16), (1, P)), mask(("gnot_fwd", "gnot_bwd")[d], 16),
                                      zeros(16)).then_inc(sm("g_aok"), 1)
                dve.wait_ge(sm("g_pv"), 2 * l + 2)
                for i in outs:
                    step(V.tensor_copy(big(i, C_GQ, 256), bank[i][:, 0:256]))

                for n, t in enumerate(outs):
                    x = view(BIG, t * NIN + C_GQ, (64, 4), (1, 64))
                    centre(x, x, view(SC, NSQ, (64, 4), (1, 64)), nto + n)
                V.memset(view(ST, 501, (1, 1)), 0.0).then_inc(sm("n_var"), 1)
                x2 = bigs(t0, nto, C_GQ, (1, 256))
                step(V.tensor_tensor(x2, x2, view(NW, l * 512 + 256, (0, nto), (1, 256)), ALU.mult))
                step(V.tensor_tensor(x2, x2, bigs(t0, nto, C_GG, (1, 256)), ALU.mult))
                dve.wait_ge(sm("n_rstd"), l + 1)
                for g in range(2):
                    for n, t in enumerate(outs):
                        x = view(BIG, t * NIN + (C_MQ, C_GQ)[g], (64, 4), (1, 64))
                        ins = V.tensor_tensor(x, x, view(ST, RST + 4 * (g * nto + n), (1, 4), (0, 64)), ALU.mult)
                        ins.then_inc(sm("cat"), 1)
                for kt in range(1, KT, 2):
                    dve.wait_ge(sm("c_T"), l * KT + kt + 1)
                    V.tensor_copy(view(HT, kt * 512 + t0 * P, (1, nto * P)), bank[kt % 4][:, t0 * P:512]).then_inc(sm("c_dve"), 1)
                layer_norm(2 * l, True)
                diagonals(2 * l + 1)
                h_latent(2 * l + 1, not last)

                def hidden(st, k, kk):
                    b = k % 2
                    e, tmp = view(SC, FE + b * FC, (1, FC)), view(SC, FT + b * FC, (1, FC))
                    dve.wait_ge(sm("f_exp"), kk + 1)
                    st(V.tensor_scalar(e, e, 1.0, None, ALU.add))
                    st(V.reciprocal(e, e))
                    st(V.tensor_tensor(tmp, bank[4 + b][:, 0:FC], e, ALU.mult))
                    if not (isinstance(kk, int) and kk < 2):
                        dve.wait_ge(sm("f_tr"), kk - 1)
                    V.tensor_tensor(view(SC, FH + b * FC, (1, FC)), tmp, bank[4 + b][:, FC:2 * FC], ALU.mult).then_inc(sm("f_h"), 1)

                def add_down(k, kk, y):
                    dve.wait_ge(sm("f_down"), kk + 1)
                    if not (isinstance(kk, int) and kk == 0):
                        dve.wait_ge(sm("f_y"), kk * 2)
                    for half in range(2):
                        v = y(half)
                        V.tensor_tensor(v, v, bank[half][:, :], ALU.add).then_inc(sm("f_y"), 1)

                if not last:
                    step(V.memset(view(BIG, 0, (1, NT * D)), 0.0))
                    state = {"it": None}
                    def write_down_lo(m, moved):
                        dve.wait_ge(sm("dw_hi"), m + 1 if moved is None else moved * 2 + (m + 1))
                        t, o = ((BIG, 8192), (SC, 10240))[m % 2]
                        at = (DW, (m % 2) * 2 * D, (1, 2 * D))
                        V.tensor_tensor(rview(*at), view(*at), rview(t, o, (1, 2 * D)).bitcast(F32), ALU.subtract).then_inc(sm("dw_lo"), 1)

                    def hidden_lo(k, kk):
                        b = k % 2
                        dve.wait_ge(sm("f_hT"), kk + 1)
                        V.tensor_tensor(rview(SC, FHL + b * FC, (1, FC)), bank[6 + b][:, 0:FC],
                                        rview(SC, FHT + b * FC, (1, FC)).bitcast(F32), ALU.subtract).then_inc(sm("f_hTl"), 1)

                    for half in range(2):
                        write_lo(dve, "ff", base["ff", 0], split_base["ff", 0], None, half)
                    write_down_lo(0, None)

                    def inner(it):
                        state["it"] = it
                        step.loop = it * (3 * 2 * NT) - 3 * 2 * NT

                    def first(k, kk):
                        if k:
                            hidden_lo(k - 1, kk - 1)
                        hidden(step, k, kk)
                        if isinstance(kk, int) and k < NT:
                            affine(0, k, k, xt(k))
                            if k == NT - 1:
                                ln_rows_used()
                        if k % NT and k < (N_FF - 1) * NT:
                            m = k // NT + 1
                            moved = None if isinstance(kk, int) else state["it"]
                            if k % NT < 3:
                                write_lo(dve, "ff", base["ff", 0] + m, split_base["ff", 0] + m, moved, k % NT - 1)
                            else:
                                write_down_lo(m, moved)
                        if not isinstance(kk, int) and k == 2 * NT:
                            step.leave(3 * 2 * NT * (N_FF // 2 - 2))

                    def second(k, kk):
                        if k == N_FF * NT - 1:
                            hidden_lo(k, kk)
                        add_down(k, kk, lambda half: ysum(k % NT, half * 512, 512))

                    in_pairs(dve, first, second, inner)
                    layer_norm(1, False)
                    continue

                dve.wait_ge(sm("xs_hi"), 1)
                V.tensor_tensor(rview(SC, XSL, (1, 2 * D)), view(X, 2 * D, (1, 2 * D)),
                                rview(SC, XSH, (1, 2 * D)).bitcast(F32), ALU.subtract).then_inc(sm("xs_lo"), 1)
                dve.wait_ge(sm("r_mm"), 1)
                for i in range(2):
                    lo, top = view(ST, 200 + 8 * i, (1, 8)), view(ST, 216 + 8 * i, (1, 8))
                    step(V.tensor_tensor(lo, bank[4][:, 8 * i:8 * i + 8], prm("rb", (1, 8)), ALU.add))
                    step(V.max(top, lo))
                    step(V.max_index(IDX[:, 8 * i:8 * i + 8], top, lo))
                    step(V.tensor_tensor(view(ST, 136 + i, (1, 1)), view(ST, 217 + 8 * i, (1, 1)),
                                         view(ST, 216 + 8 * i, (1, 1)), ALU.subtract))
                V.tensor_copy(view(ST, 256, (1, 16)), IDX[:, :]).then_inc(sm("r_diff"), 1)
                dve.wait_ge(sm("r_diff"), 1)
                dve.wait_ge(sm("r_exp"), 1)
                step(V.tensor_scalar(view(ST, 138, (1, 2)), view(ST, 136, (1, 2)), 1.0, None, ALU.add))
                step(V.reciprocal(view(ST, 138, (1, 2)), view(ST, 138, (1, 2))))
                step(V.tensor_tensor(view(ST, 136, (1, 2)), view(ST, 136, (1, 2)), view(ST, 138, (1, 2)), ALU.mult))
                for i in range(2):
                    def one_hot(at, scale, which):
                        step(V.tensor_scalar(view(ST, at + 8 * i, (1, 8)), cst("eights"),
                                             view(ST, 256 + 8 * i + which, (1, 1)), scale, ALU.is_equal, ALU.mult))
                    one_hot(272, 1.0, 0)
                    one_hot(288, 1.0, 1)
                    one_hot(304, view(ST, 138 + i, (1, 1)), 0)
                    one_hot(320, view(ST, 136 + i, (1, 1)), 1)
                step(V.tensor_tensor(view(ST, 304, (1, 16)), view(ST, 304, (1, 16)), view(ST, 320, (1, 16)), ALU.add))
                signal(V.tensor_tensor(view(ST, 272, (1, 16)), view(ST, 272, (1, 16)), view(ST, 288, (1, 16)), ALU.add),
                       "r_chosen", 1)
                dve.wait_ge(sm("r_count"), 1)
                step(V.tensor_tensor(view(ST, 336, (1, 16)), bank[5][:, 0:16], view(ST, 272, (1, 16)), ALU.mult))
                step(V.tensor_scalar(view(ST, 336, (1, 16)), view(ST, 336, (1, 16)), -1.0, None, ALU.add))
                over_f, rank_f = view(ST, 353, (1, 8), np_=1), view(ST, 361, (1, 8), np_=1)
                step(V.tensor_scalar(over_f, bank[5][0:1, 16:24], float(P), None, ALU.is_gt))
                step(V.tensor_reduce(view(ST, 352, (1, 1), np_=1), over_f, AX, ALU.max))
                step(V.tensor_tensor_scan(rank_f, view(CS, C_AT["ones"][0], (0, 8), np_=1), over_f, 0.0, ALU.mult, ALU.add))
                step(V.tensor_tensor(rank_f, rank_f, over_f, ALU.subtract))
                V.tensor_copy(RI[0:1, 0:17], view(ST, 352, (1, 17), np_=1)).then_inc(sm("overflow_known"), 1)

                def experts(st, blk):
                    if blk:
                        st(V.tensor_scalar(view(ST, 336, (1, 16)), view(ST, 336, (1, 16)), -float(P), None, ALU.add))
                    sel_t, sel_o = SELS[blk]
                    for e in range(NE):
                        for i in range(2):
                            place = view(ST, 336 + 8 * i + e, (1, 1))
                            sel_view = view if blk else rview
                            V.tensor_scalar(sel_view(sel_t, sel_o + e * 256 + i * P, (1, P)), cst("slots"), place, None,
                                            ALU.is_equal).then_inc(sm("sel"), 1)
                            V.tensor_scalar(view(SC, SELW + e * 256 + i * P, (1, P)), cst("slots"), place,
                                            view(ST, 304 + 8 * i + e, (1, 1)), ALU.is_equal, ALU.mult).then_inc(sm("sel"), 1)

                    def gathered(n):
                        dve.wait_ge(sm("gx_mm"), n)
                        for q in range(4):
                            ins = V.tensor_scalar(view(BIG, XGA + (4 + q) * P, (1, P)), bank[5][:, q * P:(q + 1) * P],
                                                  mod(1, 4, 4 + q, 1), mod(1, 3, 4 + q, 1), ALU.mult, ALU.add)
                        ins.then_inc(sm("gx_d"), 1)

                    k0 = SF + blk * NE * N_EX
                    n0, i0 = base["ff", 1] + blk * NE * N_EX, split_base["ex", 1] + blk * NE * N_EX
                    start = st.n
                    per_unit = 3
                    per_expert = per_unit * N_EX

                    def tokens(e, n):
                        dve.wait_ge(sm("x_hi"), n)
                        V.tensor_tensor(rview(SC, XGL, (1, D)), BIG[:, bass.ds(e * D + XGA, D)],
                                        rview(SC, XGS, (1, D)).bitcast(F32), ALU.subtract).then_inc(sm("x_lo"), 1)

                    def scatter(e):
                        V.tensor_copy(view(SC, CWS, (1, 2 * P)), SC[:, bass.ds(e * 256 + CWA, 256)]).then_inc(sm("cw"), 1)

                    def two_chunks(moved):
                        for c in range(2):
                            for half in range(2):
                                write_lo(dve, "ex", n0 + c, i0 + c, moved, half)

                    def body(e, r, more):
                        at = {"moved": r * (N_EX // 2)}
                        st.loop = r * per_expert
                        if blk:
                            two_chunks(at["moved"])
                            gathered(r + (2 * NE + 1))
                            dve.wait_ge(sm("gx_d"), r + (NE + 1))
                            tokens(0, r + (NE + 1))
                        scatter(e)

                        def low(k, half):
                            if more or k - k0 + 2 < N_EX:
                                c = k - k0 + 2
                                write_lo(dve, "ex", n0 + c, i0 + c, at["moved"], half)

                        def pair(k, kk):
                            low(k, 0)
                            hidden(st, k + 1, kk + 1)
                            low(k, 1)

                        def last(k, kk):
                            if more:
                                tokens(e + 1, r + (blk * NE + 2))
                            low(k, 0)
                            low(k, 1)
                            if more:
                                hidden(st, k + 1, kk + 1)

                        def inner(it):
                            if it is None:
                                st.loop = r * per_expert
                                st.n += 2 * per_unit * (N_EX // 2 - 3)
                                at["moved"] = r * (N_EX // 2)
                            else:
                                st.loop = r * per_expert + it * (2 * per_unit)
                                at["moved"] = r * (N_EX // 2) + it

                        if blk:
                            hidden(st, k0, r * N_EX + k0)
                        one_expert(dve, k0, r, lambda k, kk: None, pair, last, inner)
                        dve.wait_ge(sm("s_mm"), r + blk * NE + 1)
                        for i in range(2):
                            for half in range(2):
                                v = ysum(i, half * 512, 512)
                                V.tensor_tensor(v, v, bank[2 * i + half][:, :], ALU.add).then_inc(sm("s_add"), 1)
                        dve.wait_ge(sm("s_add"), r * 4 + (1 + 4 * (blk * NE + 1)))
                        V.memset(view(ST, 501, (1, 1)), 0.0)
                        st.n = start if blk or not more else start + per_unit

                    if not blk:
                        for c, half in ((0, 0), (0, 1), (1, 0)):
                            write_lo(dve, "ex", n0 + c, i0 + c, 0, half)
                        for q in range(1, 2 * NE, 2):
                            dve.wait_ge(sm("gx_mm"), q + 1)
                            V.tensor_scalar(gathered_at(q), four(bank[4 + q % 4]), mod(1, 4, q % KT, 1),
                                            mod(1, 3, q % KT, 1), ALU.mult, ALU.add).then_inc(sm("gx_d"), 1)
                        tokens(0, 1)
                        write_lo(dve, "ex", n0 + 1, i0 + 1, 0, 1)
                        hidden(st, k0, k0)
                    dve.wait_ge(sm("sw_copy"), 4 * (blk + 1))
                    over_experts(dve, blk, body)
                    st.leave(per_expert * NE)

                V.memset(view(BIG, 0, (1, 2 * D)), 0.0).then_inc(sm("s_add"), 1)
                dve.wait_ge(sm("s_add"), 1)
                experts(step, 0)
                over = dve.value_load(RI[0:1, 0:1], min_val=0, max_val=1)
                with dve.If(over > 0):
                    experts(Steps(dve, dve_block_step), 1)
                layer_norm(3, False)

        @block.tensor
        def _(pe):
            T = nc.tensor
            mm = nc.tensor.matmul

            def ready(n, it=None):
                s = g_slot(n)
                for h in range(2):
                    v = 32 * (n // 2 + 1)
                    pe.wait_ge(g_loaded[2 * s + h], v if it is None else it * 32 + v)

            pe.wait_ge(params, 16 * 23)
            for a, n, o in ((0, 16, 0), (P, 96, 16), (2 * P, 4, 112), (3 * P, 16, 116), (4 * P, 16, 132)):
                ins = T.transpose(bank[0][:, o:o + n], view(SC, a, (1, P), np_=n), cst("ident", 0, n, n))
            ins.then_inc(sm("start_T"), 1)
            pe.wait_ge(sm("sct"), 1)
            def ada_rows(dst, n, it, frees=None):
                ready(n, it)
                for kt in range(KT):
                    g = kt % 4
                    ins = mm(bank[dst][32 * g:32 * g + 32, :], view(SC, SCT + kt * 32, (1, 32)), gw(n, kt),
                             start=kt < 4, stop=kt >= 4)
                    if kt < 2 and frees is not None:
                        ins.then_inc(g_free[2 * g_slot(frees) + kt], 1)
                ins.then_inc(sm("ada_mm"), 1)

            def ada_columns(dst, rows, frees):
                for q in range(4):
                    ins = mm(bank[dst][:, 2 * q:2 * q + 2], view(SC, rows + q * P, (1, P)), cst("pick"), start=True, stop=True)
                    if q < 2 and frees is not None:
                        ins.then_inc(g_free[2 * g_slot(frees) + q], 1)
                ins.then_inc(sm("ada_col"), 1)

            def ada_columns_0(j, it, frees):
                i = 0 if it is None else it
                pe.wait_ge(sm("ada_row"), i * 2 + (j + 1))
                if it is not None:
                    pe.wait_ge(sm("mod"), i * 2 + j)
                ada_columns(2 + j % 2, ADAR + (j % 2) * 512, frees)

            ada_rows(0, 0, None)
            ada_rows(1, 1, None, 0)
            ada_columns_0(0, None, 1)
            with pe.Fori(1, N_ADA // 2) as it:
                ada_rows(0, 0, it)
                ada_columns_0(-1, it, 0)
                ada_rows(1, 1, it)
                ada_columns_0(0, it, 1)
            ada_columns_0(-1, N_ADA // 2, None)
            pe.wait_ge(sm("mods"), 1)

            def gate_products(i):
                for s in range(2):
                    for half in range(2):
                        k = i * 4 + s * 2 + half
                        pe.wait_ge(sm("diag"), k + 1)
                        if k >= 2:
                            pe.wait_ge(sm("gate_row"), k - 1)
                        mm(bank[6 + half][:, :], cst("ones", n=P), view(DIAG[i % 2][0], DIAG[i % 2][1] + half * 512, (1, 512)), start=True,
                           stop=True).then_inc(sm("gate_mm"), 1)

            def x_transposes(u, tiles):
                for kt in range(KT):
                    if kt >= 2:
                        pe.wait_ge(sm("h_lat"), u * KT + kt - 1)
                        if 0 in tiles:
                            pe.wait_ge(sm("h_ctx"), u * KT + kt - 1)
                    for t in tiles:
                        ins = T.transpose(bank[kt % 2 + 2 * (t // 2)][:, t * P:(t + 1) * P], xt(t, kt * P, P), ident)
                    ins.then_inc(sm("x_T"), 1)

            for l in range(DEPTH):
                outs = OUTS[l]
                t0, nto = outs[0], len(outs)
                if l == 0:
                    pe.wait_ge(sm("x_loaded"), 16 * NT)
                else:
                    pe.wait_ge(sm("r_norm"), NORMED[2])
                gate_products(2 * l)
                x_transposes(2 * l, range(NT))
                pe.wait_ge(sm("h_lo"), KT * (2 * l + 1))
                for g in range(N_IN * NT):
                    cchunk, t = divmod(g, NT)
                    n = base["in", l] + cchunk
                    a, w = columns(l, t, cchunk)
                    if g >= 4:
                        pe.wait_ge(sm("p_dve" if g % 2 else "p_act"), 12 * l + (g - 4) // 2 + 1)
                    else:
                        pe.wait_ge(sm("gate_row"), 4 * (2 * l + 1))
                    ins = three_products(bank[4 + g % 4][:, 0:w],
                                         lambda kt: (tokens_hi(2 * l, kt, t * P, P),
                                                     rview(HT, kt * 512 + t * P, (1, P))),
                                         lambda kt: (hi("in", n, kt, a, w), lo(n, kt, a, w)),
                                         2 * (split_base["in", l] + cchunk) + 1 if t == 0 else None, pe,
                                         frees=n if t == NT - 1 else None)
                    if t == 0 and cchunk:
                        ins[0].then_inc(g_free[2 * g_slot(n - 1) + 1], 1)
                    ins[-1].then_inc(sm("p_mm"), 1)
                pe.wait_ge(sm("p_act"), 12 * (l + 1))
                pe.wait_ge(sm("p_dve"), 12 * (l + 1))
                for g in range(6):
                    for t in (outs if g in (2, 3) else range(NT)):
                        if g < 2:
                            for d in range(2):
                                ins = mm(bank[g][32 * d:32 * d + 32, t * P:(t + 1) * P], big(t, C_MG + 4 * g + 8 * d, 32),
                                         ident, start=True, stop=True)
                        else:
                            ins = T.transpose(bank[g][:, t * P:(t + 1) * P], big(t, (g - 2) * P, P), ident)
                        if g == 0 and t == 0:
                            ins.then_inc(g_free[2 * g_slot(base["in", l] + N_IN - 1) + 1], 1)
                    ins.then_inc(sm("m_T"), 1)
                pe.wait_ge(sm("mq_T"), 2 * (l + 1))
                pe.wait_ge(sm("mk_T"), 2 * (l + 1))
                pe.wait_ge(sm("v1"), 5 * (l + 1))

                def m_scores(h):
                    p0 = 64 * (h % 2)
                    if h:
                        pe.wait_ge(sm("m_w"), 3 * (8 * l + 2 * h))
                    for j in range(4):
                        dst = bank[1 + j][:, t0 * P:512] if j < 2 else bank[3][:, (j - 2) * 256:(j - 1) * 256]
                        a, n = (t0 * P, nto * P) if j < 2 else (256, 256)
                        ins = mm(dst, view(SC, MKT + (h // 2) * 512 + j * P, (1, P), p0=p0, np_=64),
                                 view(SC, MQT + (h // 2) * 512 + a, (1, n), p0=p0, np_=64), start=True, stop=True)
                    ins.then_inc(sm("m_s"), 1)

                def m_stabiliser(u):
                    h, d = divmod(u, 2)
                    if u >= 2:
                        pe.wait_ge(sm("m_decay"), 8 * l + u - 1)
                    row = d * 32 + h
                    o = C_AT["ident"][0]
                    mm(bank[4 + d][:, :], view(CS, o + row, (0, P), np_=64), view(SC, ROWM, (1, 512), np_=64), start=True,
                       stop=True).then_inc(sm("m_bc"), 1)

                def m_values(u):
                    h, d = divmod(u, 2)
                    pe.wait_ge(sm("m_w"), 3 * (8 * l + u + 1))
                    if u >= 2:
                        pe.wait_ge(sm("m_hs"), 8 * l + u - 1)
                    for i in outs:
                        if d == 0:
                            keys = list(range(i + 1))
                        else:
                            keys = [j for j in range(NT) if (j >= i if (i < 2) == (j < 2) else i >= 2)]
                        for q, j in enumerate(keys):
                            ins = mm(bank[6 + d][:, i * 65:(i + 1) * 65], view(SC, MD + d * 2048 + j * 512 + i * P, (1, P)),
                                     view(SC, V1 + j * 260 + h * 65, (1, 65)), start=q == 0, stop=q == len(keys) - 1)
                    ins.then_inc(sm("m_pv"), 1)

                m_scores(0)
                pe.wait_ge(sm("gate_rows_ready"), l + 1)
                m_stabiliser(0)
                m_stabiliser(1)
                pe.wait_ge(sm("floor_row"), l + 1)
                for k, src in enumerate((ROWA, ROWT)):
                    for j in range(NT):
                        ins = T.transpose(bank[0][:, k * 256 + j * 64:k * 256 + (j + 1) * 64],
                                          view(SC, src + j * P, (1, P), np_=64), cst("ident", 0, 64, 64))
                ins.then_inc(sm("gates_T"), 1)
                for u in range(8):
                    if u + 2 < 8:
                        m_stabiliser(u + 2)
                    m_values(u)
                    if u % 2 and u < 7:
                        m_scores(u // 2 + 1)
                pe.wait_ge(sm("rope"), 2 * (l + 1))
                pe.wait_ge(sm("gate_cols"), l + 1)
                pe.wait_ge(sm("m_decay"), 8 * (l + 1))
                for j in range(6):
                    for t in (range(NT) if j >= 4 else outs):
                        if j < 4:
                            ins = T.transpose(bank[j][:, t * P:(t + 1) * P], big(t, C_AQ + j * P, P), ident)
                            continue
                        for half in range(2):
                            ins = mm(bank[j][64 * half:64 * half + 64, t * P:(t + 1) * P],
                                     big(t, C_AK + (j - 4) * 64, 64), ident, start=True, stop=True)
                    ins.then_inc(sm("a_T"), 1)
                pe.wait_ge(sm("a_qk"), 6 * (l + 1))
                off = sum(N_ATT[:l])
                for k in range(N_ATT[l] + 2):
                    if k < N_ATT[l]:
                        i, j, half = ATT[l][k]
                        b, n, p0 = k % 2, 256 if i < 2 else 512, 64 * half
                        if k >= 2:
                            pe.wait_ge(sm("a_exp"), 2 * (off + k - 1))
                        ins = mm(bank[b][:, 0:n], view(HT, AQT + j * 512 + i * P, (1, P), p0=p0, np_=64),
                                 view(HT, AQT + (4 + j // 2) * 512, (1, n), p0=p0, np_=64), start=True, stop=i < 2)
                        if i >= 2:
                            o = (5 - i) * P
                            ins = mm(bank[b][:, o:o + P], ident, cst("bias_t2" if i == 2 else "bias_t3"), start=False,
                                     stop=True)
                        ins.then_inc(sm("a_s"), 1)
                    if 1 <= k <= N_ATT[l]:
                        i = ATT[l][k - 1][0]
                        b = (k - 1) % 2
                        pe.wait_ge(sm("a_exp"), 2 * (off + k))
                        if k >= 3:
                            pe.wait_ge(sm("a_pTs"), off + k - 2)
                        for q in range(2 if i < 2 else 4):
                            ins = T.transpose(bank[2 + b][:, q * P:(q + 1) * P], view(HT, AP_ + b * 512 + q * P, (1, P)), ident)
                        ins.then_inc(sm("a_pT"), 1)
                    if k >= 2:
                        i, j, half = ATT[l][k - 2]
                        b = k % 2
                        pe.wait_ge(sm("a_pTs"), off + k - 1)
                        if k >= 4:
                            pe.wait_ge(sm("a_o"), off + k - 3)
                        nk = 2 if i < 2 else 4
                        for q in range(nk):
                            ins = mm(bank[4 + b][:, 0:64], view(SC, APT + b * 512 + q * P, (1, P)),
                                     big(q, C_AV + (j // 2) * 64, 64), start=q == 0, stop=q == nk - 1)
                        ins.then_inc(sm("a_pv"), 1)
                    if l == 0 and ada_after(k - 2) is not None:
                        c1 = ada_after(k - 2)
                        pe.wait_ge(sm("ada_row"), N_ADA + c1 + 1)
                        if c1:
                            pe.wait_ge(sm("mod"), N_ADA + c1)
                        ada_columns(7, ADAL, base["ada", 1] + c1)
                    if l == 0 and ada_after(k) is not None:
                        if ada_after(k) == 0:
                            pe.wait_ge(sm("m_hs"), 8)
                        ada_rows(6, base["ada", 1] + ada_after(k), None)
                if l == 0:
                    pe.wait_ge(sm("mods"), 2)
                pe.wait_ge(sm("a_o"), off + N_ATT[l])
                pe.wait_ge(sm("m_hs"), 8 * (l + 1))
                for g in range(4):
                    for t in range(NT):
                        rows = P if g < 2 else RANK
                        c0 = (C_GQ, C_GK, C_GR, C_GR + RANK)[g]
                        ins = T.transpose(bank[g][0:rows, t * P:(t + 1) * P], big(t, c0, rows), ident)
                    ins.then_inc(sm("g_T"), 1)
                for d in range(2):
                    pe.wait_ge(sm("g_r"), 2 * l + d + 1)
                    mm(bank[4 + d][:, :], prm("gup", (1, P), off=(2 * l + d) * P, np_=RANK),
                       view(SC, GRT + d * 512, (1, 512), np_=RANK), start=True, stop=True).then_inc(sm("g_z"), 1)
                pe.wait_ge(sm("g_prod"), 3 * l + 1)
                for d in range(2):
                    for t in range(NT):
                        ins = T.transpose(bank[6 + d][:, t * P:(t + 1) * P], view(SC, GKD + d * 512 + t * P, (1, P)), ident)
                    ins.then_inc(sm("g_kT"), 1)
                pe.wait_ge(sm("g_qk"), 2 * (l + 1))
                pe.wait_ge(sm("g_prod"), 3 * l + 3)
                pe.wait_ge(sm("g_ktok"), 2 * (l + 1))

                def g_scores(d):
                    if d == 1:
                        pe.wait_ge(sm("g_acopy"), 2 * l + 1)
                    for i in range(NT):
                        for h in range(4):
                            a = d * 512 + i * P
                            ins = mm(bank[4 + h][:, i * P:(i + 1) * P], view(SC, GNB + a, (1, P), p0=32 * h, np_=32),
                                     view(SC, GEB + a, (1, P), p0=32 * h, np_=32), start=True, stop=True)
                    ins.then_inc(sm("g_a"), 1)

                def g_values(d):
                    pe.wait_ge(sm("g_aok"), 2 * l + d + 1)
                    for i in outs:
                        for h in range(4):
                            ins = mm(bank[i][:, h * 64:(h + 1) * 64], view(SC, GAT + h * 512 + i * P, (1, P)),
                                     big(i, C_GV + h * 64, 64), start=d == 0 and h == 0, stop=False, skip_group_check=True)
                        for cc in range(2):
                            ch = 2 * i + cc
                            k = ch if d == 0 else (3 - ch if ch < 4 else 11 - ch)
                            if k:
                                ins = mm(bank[i][64 * cc:64 * cc + 64, 0:256], view(SC, GEB + d * 512 + ch * 64, (1, 64)),
                                         view(SC, GS + (d * 7 + k) * 256, (1, 256)), start=False, stop=d == 1,
                                         skip_group_check=True)
                    ins.then_inc(sm("g_pv"), 1)

                g_scores(0)
                for q in range(14):
                    k, d = divmod(q, 2)
                    ch = chunk_of(d, k)
                    p0 = 64 * (ch % 2)
                    if q >= 4:
                        pe.wait_ge(sm("g_st"), 14 * l + q - 3)
                    mm(bank[q % 4][:, 0:256], view(SC, GKT + d * 512 + (ch // 2) * P, (1, P), p0=p0, np_=64),
                       view(BIG, (ch // 2) * NIN + C_GV, (1, 256), p0=p0, np_=64), start=True, stop=True).then_inc(sm("g_kv"), 1)
                g_scores(1)
                pe.wait_ge(sm("g_st"), 14 * (l + 1))
                g_values(0)
                g_values(1)
                pe.wait_ge(sm("cat"), 2 * sum(N_TO[:l + 1]))
                for kt in range(KT):
                    if kt >= 4:
                        pe.wait_ge(sm("c_dve" if kt % 2 else "c_act"), 4 * l + (kt - 4) // 2 + 1)
                    c0 = C_MQ + kt * P if kt < 2 else (C_AQ + (kt - 2) * P if kt < 6 else C_GQ + (kt - 6) * P)
                    for t in outs:
                        ins = T.transpose(bank[kt % 4][:, t * P:(t + 1) * P], big(t, c0, P), ident)
                    ins.then_inc(sm("c_T"), 1)
                pe.wait_ge(sm("c_act"), 4 * (l + 1))
                pe.wait_ge(sm("c_dve"), 4 * (l + 1))
                for cc in range(N_OUT):
                    n = base["out", l] + cc
                    ready(n)
                    for t in outs:
                        for kt in range(KT):
                            ins = mm(bank[t * 2 + cc][:, :], view(HT, kt * 512 + t * P, (1, P)), gw(n, kt), start=kt == 0,
                                     stop=kt == KT - 1)
                        ins.then_inc(sm("o_mm"), 1)
                    for h in range(2):
                        pe.drain().then_inc(g_free[2 * g_slot(n) + h], 1)
                if l == 0:
                    pe.wait_ge(sm("r_norm"), NORMED[0] + NT)
                else:
                    pe.wait_ge(sm("x_ready"), X_READY[2] + 2)
                gate_products(2 * l + 1)
                x_transposes(2 * l + 1, outs)

                def up(k, kk, stage, n, i, moved, lhs, first, whole, frees, between=None):
                    b = k % 2
                    if not (isinstance(kk, int) and kk < 2):
                        pe.wait_ge(sm("f_h"), kk - 1)
                    w = None
                    if first:
                        w = 2 * i + 1 if moved is None else moved * 4 + (2 * i + 1)
                    ins = three_products(bank[4 + b][:, :], lhs, lambda kt: (hi(stage, n, kt), lo(n, kt)), w, pe, between,
                                         n if whole else None)
                    if frees:
                        ins[0].then_inc(g_free[2 * g_slot(n - 1) + 1], 1)
                    ins[-1].then_inc(sm("f_up"), 1)

                def turn(k, kk):
                    b = k % 2
                    pe.wait_ge(sm("f_h"), kk + 1)
                    for q in range(2):
                        ins = T.transpose(bank[6 + b][:, q * P:(q + 1) * P], view(SC, FH + b * FC + q * P, (1, P)), ident)
                    ins.then_inc(sm("f_tr"), 1)

                def down(k, kk, m, moved, frees, start, stop, before=None):
                    b = k % 2
                    pe.wait_ge(d_loaded[m % 2], moved * 16 + 16 * (m // 2 + 1))
                    pe.wait_ge(sm("f_hT"), kk + 1)
                    if before:
                        before()
                    for half in range(2):
                        for q in range(2):
                            ins = mm(bank[half][:, :], view(SC, FHT + b * FC + q * P, (1, P)), dw(m, q, half),
                                     start=start and q == 0, stop=stop and q == 1)
                            if frees is not None and half == 0 and q == 0:
                                ins.then_inc(g_free[2 * g_slot(frees) + 1], 1)
                    ins.then_inc(sm("f_down"), 1)

                if l == 0:
                    pe.wait_ge(sm("h_lo"), KT * 2)
                    n0, i0 = base["ff", 0], split_base["ff", 0]

                    state = {"it": None}

                    def first(k, kk):
                        ch, t = divmod(k, NT)
                        moved = None if isinstance(kk, int) else state["it"]
                        up(k, kk, "ff", n0 + ch, i0 + ch, moved,
                           lambda kt: (tokens_hi(1, kt, t * P, P), rview(HT, kt * 512 + t * P, (1, P))),
                           t == 0, t == NT - 1, False, (lambda: turn(k - 1, kk - 1)) if k else None)

                    def second(k, kk):
                        ch, t = divmod(k, NT)
                        moved = None if isinstance(kk, int) else state["it"]

                        def summed():
                            if not (isinstance(kk, int) and kk == 0):
                                pe.wait_ge(sm("f_y"), kk * 2)

                        if k == N_FF * NT - 1:
                            turn(k, kk)
                        if t == 0:
                            pe.wait_ge(sm("dw_lo"), ch + 1 if moved is None else moved * 2 + (ch + 1))
                        pe.wait_ge(sm("f_hTl"), kk + 1)
                        summed()
                        b = k % 2
                        for half in range(2):
                            for q in range(2):
                                hid = [rview(SC, at + b * FC + q * P, (1, P)) for at in (FHT, FHL)]
                                wts = [w(ch, q, half * 512, 512) for w in (down_hi, down_lo)]
                                ins = mm(bank[half][:, :], hid[0], wts[0], start=q == 0, stop=False)
                                if half == 0 and q == 0 and t == 2:
                                    ins.then_inc(g_free[2 * g_slot(n0 + ch) + 1], 1)
                                mm(bank[half][:, :], hid[0], wts[1], start=False, stop=False)
                                ins = mm(bank[half][:, :], hid[1], wts[0], start=False, stop=q == 1)
                        ins.then_inc(sm("f_down"), 1)

                    in_pairs(pe, first, second, lambda it: state.update(it=it))
                    continue

                pe.wait_ge(sm("h_lat"), KT * 4)
                for i in range(2):
                    for kt in range(KT):
                        ins = mm(bank[4][:, 8 * i:8 * i + 8], view(HT, kt * 512 + (2 + i) * P, (1, P)), prm("rw", (1, 8), off=8 * kt),
                                 start=kt == 0, stop=kt == KT - 1)
                ins.then_inc(sm("r_mm"), 1)
                pe.wait_ge(sm("r_chosen"), 1)
                chosen = [view(ST, 272 + 8 * i, (1, 8)) for i in range(2)]
                ones = cst("ones", n=P)
                mm(bank[5][:, 0:8], cst("fwd"), chosen[0], start=True, stop=True)
                mm(bank[5][:, 8:16], ones, chosen[0], start=True, stop=False)
                mm(bank[5][:, 8:16], cst("fwd"), chosen[1], start=False, stop=True)
                mm(bank[5][0:1, 16:24], cst("ones", n=1), chosen[0], start=True, stop=False)
                mm(bank[5][0:1, 16:24], cst("ones", n=1), chosen[1], start=False, stop=True).then_inc(sm("r_count"), 1)

                def experts(blk):
                    def scatters():
                        pe.wait_ge(sm("sel"), (blk + 1) * NE * 4)
                        for q in range(16):
                            ins = T.transpose(bank[q // 4][:, (q % 4) * P:(q % 4 + 1) * P], view(SC, SELW + q * P, (1, P)), ident)
                            if q % 4 == 3:
                                ins.then_inc(sm("sw_T"), 1)

                    sel_t, sel_o = SELS[blk]

                    def gather(moved):
                        for kt in range(KT):
                            for i in range(2):
                                ins = mm(bank[4 + kt // 4][:, (kt % 4) * P:(kt % 4 + 1) * P], xt(2 + i, kt * P, P),
                                         sel_t[:, bass.ds(moved + (sel_o + i * P), P)], start=i == 0, stop=i == 1)
                        ins.then_inc(sm("gx_mm"), 1)

                    if not blk:
                        pe.wait_ge(sm("xs_lo"), 1)
                        for q in range(2 * NE):
                            g, kt = divmod(q, KT)
                            pe.wait_ge(sm("sel"), 16 * (g + 1))
                            if q >= 4:
                                pe.wait_ge(sm("gx_d" if q % 2 else "gx_a"), (q - 4) // 2 + 1)
                            for i in range(2):
                                sel = rview(SC, SEL + g * 4 * 2 * P + i * P, (2 * P, 4), (1, P))
                                for at in (XSH, XSL):
                                    ins = mm(four(bank[4 + q % 4]), rview(SC, at + i * D + kt * P, (1, P)), sel,
                                             start=i == 0 and at == XSH, stop=i == 1 and at == XSL)
                            ins.then_inc(sm("gx_mm"), 1)
                    scatters()
                    if not blk:
                        pe.wait_ge(sm("gx_a"), NE)
                        pe.wait_ge(sm("gx_d"), NE)
                    n0, m0, k0 = base["ff", 1] + blk * NE * N_EX, N_FF + blk * NE * N_EX, SF + blk * NE * N_EX
                    i0 = split_base["ex", 1] + blk * NE * N_EX

                    def body(e, r, more, begin=False):
                        if blk:
                            gather(e * 256)
                        st = {"moved": r * (N_EX // 2)}

                        def first(k, kk, frees=False, between=None):
                            up(k, kk, "ex", n0 + k - k0, i0 + k - k0, st["moved"],
                               lambda kt: (rview(SC, XGS + kt * P, (1, P)), rview(SC, XGL + kt * P, (1, P))),
                               True, True, frees, between)

                        def summed():
                            pe.wait_ge(sm("s_add"), r * 4 + (1 + 4 * blk * NE))

                        def step(k, kk):
                            first(k + 1, kk + 1, k == k0, lambda: turn(k, kk))
                            down(k, kk, m0 + k - k0, st["moved"], n0 + k - k0 + 1, k == k0, False,
                                 summed if k == k0 else None)

                        def last(k, kk):
                            turn(k, kk)
                            down(k, kk, m0 + k - k0, st["moved"], None, False, True)
                            if more:
                                pe.wait_ge(sm("x_lo"), r + 2)
                                first(k + 1, kk + 1)

                        def inner(it):
                            st["moved"] = r * (N_EX // 2) if it is None else r * (N_EX // 2) + it

                        if blk or begin:
                            pe.wait_ge(sm("x_lo"), r + (blk * NE + 1))
                            first(k0, r * N_EX + k0)
                        if begin:
                            return
                        one_expert(pe, k0, r, lambda k, kk: None, step, last, inner)
                        pe.wait_ge(sm("ye"), r * 2 + 2 * (blk * NE + 1))
                        pe.wait_ge(sm("cw"), r + (blk * NE + 1))
                        for i in range(2):
                            for half in range(2):
                                ins = mm(bank[2 * i + half][:, :], view(SC, CWS + i * P, (1, P)), view(SC, YE + half * 512, (1, 512)),
                                         start=True, stop=True)
                        ins.then_inc(sm("s_mm"), 1)

                    if not blk:
                        body(0, 0, True, begin=True)
                    pe.wait_ge(sm("sw_copy"), 4 * (blk + 1))
                    over_experts(pe, blk, body)
                    if not blk:
                        pe.wait_ge(sm("s_add"), 1 + 4 * NE)

                experts(0)
                over = pe.value_load(RI[0:1, 0:1], min_val=0, max_val=1)
                with pe.If(over > 0):
                    experts(1)


_INS = ["x", "c", "ctx", "c_ctx", "w_ada", "b_ada", "w_in", "mlstm_gate_b", "mlstm_norm_w", "attn_sink",
        "gla_gate_up", "gla_gate_b", "gla_norm_w", "w_out", "ln_w", "ln_b", "ffn_w_gu", "ffn_w_down",
        "router_w", "router_b", "moe_w_gu", "moe_w_down"]
_OUTS = [((1, 256, 1024), "float32")]


def kernel(**inputs):
    import numpy as _np
    import concourse.bacc as _bacc
    from concourse import mybir as _mybir
    from concourse.bass_utils import run_bass_kernel_spmd as _run

    nc = _bacc.Bacc("TRN2", target_bir_lowering=False, num_devices=1)
    arrays, args = {}, []
    for name in _INS + ["constants"]:
        a = _np.ascontiguousarray(inputs[name]) if name != "constants" else constants()
        arrays[f"in_{name}_dram"] = a
        args.append(nc.dram_tensor(f"in_{name}_dram", a.shape, _mybir.dt.from_np(a.dtype), kind="ExternalInput").ap())
    for i, (shape, dtype) in enumerate(_OUTS):
        dt = _mybir.dt.from_np(_np.dtype(dtype))
        args.append(nc.dram_tensor(f"out_{i}_dram", shape, dt, kind="ExternalOutput").ap())
    bass_hymba(nc, *args)
    r = _run(nc, [arrays], core_ids=[0])
    got = tuple(r.results[0][f"out_{i}_dram"] for i in range(len(_OUTS)))
    return got[0]
```
